# Optimizing a Trainium2 kernel written in Bass

```python
import jax, jax.numpy as jnp
from jax import lax
import numpy as np
import math

D_MODEL = 1024
BATCH = 1
SEQ = 256
DEPTH = 1

HEAD_DIM = 64
D_MIX = D_MODEL
GDN_HEADS = (D_MIX // 2) // HEAD_DIM
GDN_WIDTH = GDN_HEADS * HEAD_DIM
SWA_Q_HEADS = (D_MIX - GDN_WIDTH) // HEAD_DIM
SWA_KV_HEADS = 2
SWA_GROUP = SWA_Q_HEADS // SWA_KV_HEADS
SWA_WIDTH = SWA_Q_HEADS * HEAD_DIM
SWA_KV_WIDTH = SWA_KV_HEADS * HEAD_DIM
WINDOW = 128
CONV_WIDTH = 4
CHUNK = 64
D_FF = ((8 * D_MODEL // 3 + 255) // 256) * 256
PROJ_WIDTH = 4 * GDN_WIDTH + 2 * GDN_HEADS + SWA_WIDTH + 2 * SWA_KV_WIDTH
EPS = 1e-6


def rms_norm(x, w):
    xf = x.astype(jnp.float32)
    y = xf * lax.rsqrt(jnp.mean(xf * xf, axis=-1, keepdims=True) + EPS)
    return (y * w.astype(jnp.float32)).astype(x.dtype)

def l2_norm(x):
    xf = x.astype(jnp.float32)
    return xf * lax.rsqrt(jnp.sum(xf * xf, axis=-1, keepdims=True) + EPS)

def causal_depthwise_conv(x, w):
    return lax.conv_general_dilated(
        x, w.astype(x.dtype), window_strides=(1,), padding=[(CONV_WIDTH - 1, 0)],
        dimension_numbers=('NWC', 'WIO', 'NWC'), feature_group_count=x.shape[-1])

def gated_delta_rule_chunked(q, k, v, g, beta):
    B, T, H, Dk = q.shape
    Dv = v.shape[-1]
    N = T // CHUNK

    def chunks(t):
        t = t.reshape((B, N, CHUNK, H) + t.shape[3:])
        return jnp.moveaxis(t, 3, 1)

    q = chunks(q) * (Dk ** -0.5)
    k, v, g, beta = chunks(k), chunks(v), chunks(g), chunks(beta)
    G = jnp.cumsum(g, axis=-1)
    idx = jnp.arange(CHUNK)
    causal = idx[:, None] >= idx[None, :]
    strict = idx[:, None] > idx[None, :]
    decay = jnp.exp(jnp.where(causal, G[..., :, None] - G[..., None, :], -jnp.inf))
    kb = k * beta[..., None]
    A = jnp.where(strict, jnp.einsum('bhncd,bhnsd->bhncs', kb, k) * decay, 0.0)
    L = A + jnp.eye(CHUNK, dtype=A.dtype)
    rhs = jnp.concatenate([v * beta[..., None], kb * jnp.exp(G)[..., None]], axis=-1)
    sol = lax.linalg.triangular_solve(L, rhs, left_side=True, lower=True, unit_diagonal=True)
    u, w = sol[..., :Dv], sol[..., Dv:]
    qk = jnp.where(causal, jnp.einsum('bhncd,bhnsd->bhncs', q, k) * decay, 0.0)
    q_dec = q * jnp.exp(G)[..., None]
    k_dec = k * jnp.exp(G[..., -1:] - G)[..., None]
    chunk_decay = jnp.exp(G[..., -1])

    xs = tuple(jnp.moveaxis(t, 2, 0) for t in (u, w, qk, q_dec, k_dec, chunk_decay))

    def step(S, inp):
        u_c, w_c, qk_c, qd_c, kd_c, dec_c = inp
        v_new = u_c - jnp.einsum('bhcd,bhde->bhce', w_c, S)
        o = jnp.einsum('bhcd,bhde->bhce', qd_c, S) + jnp.einsum('bhcs,bhse->bhce', qk_c, v_new)
        S = S * dec_c[..., None, None] + jnp.einsum('bhcd,bhce->bhde', kd_c, v_new)
        return S, o

    S0 = jnp.zeros((B, H, Dk, Dv), jnp.float32)
    _, o = lax.scan(step, S0, xs)
    return jnp.transpose(o, (1, 0, 3, 2, 4)).reshape(B, T, H, Dv)

def sliding_window_attention(q, k, v, sinks):
    B, T, Hq, D = q.shape
    NB = T // WINDOW
    qb = q.reshape(B, NB, WINDOW, SWA_KV_HEADS, SWA_GROUP, D)

    def banded(t):
        t = t.reshape(B, NB, WINDOW, SWA_KV_HEADS, D)
        prev = jnp.pad(t, ((0, 0), (1, 0), (0, 0), (0, 0), (0, 0)))[:, :-1]
        return jnp.concatenate([prev, t], axis=2)

    kw, vw = banded(k), banded(v)
    s = jnp.einsum('bnqhgd,bnkhd->bhgnqk', qb, kw).astype(jnp.float32) * (D ** -0.5)
    qi = jnp.arange(WINDOW)[:, None] + WINDOW
    ki = jnp.arange(2 * WINDOW)[None, :]
    dist = (qi - ki).astype(jnp.float32)
    in_window = (qi - ki >= 0) & (qi - ki < WINDOW)
    key_exists = (jnp.arange(NB)[:, None] * WINDOW + ki - WINDOW) >= 0
    mask = in_window[None] & key_exists[:, None, :]
    slopes = 2.0 ** (-8.0 * (jnp.arange(Hq, dtype=jnp.float32) + 1.0) / Hq)
    slopes = slopes.reshape(SWA_KV_HEADS, SWA_GROUP)
    s = s - slopes[:, :, None, None, None] * dist
    s = jnp.where(mask, s, -jnp.inf)
    sink = sinks.astype(jnp.float32).reshape(SWA_KV_HEADS, SWA_GROUP)[None, :, :, None, None, None]
    m = jnp.maximum(jnp.max(s, axis=-1, keepdims=True), sink)
    p = jnp.exp(s - m)
    p = p / (jnp.sum(p, axis=-1, keepdims=True) + jnp.exp(sink - m))
    o = jnp.einsum('bhgnqk,bnkhd->bnqhgd', p.astype(v.dtype), vw)
    return o.reshape(B, T, Hq * D)

def first_inputs(seed: int = 0) -> dict:
    key = jax.random.key(seed)
    ks = jax.random.split(key, 20)
    f32 = jnp.float32
    nrm = lambda k, shape, scale: jax.random.normal(k, shape, f32) * scale
    gain = lambda k, shape: 1.0 + 0.1 * jax.random.normal(k, shape, f32)
    a_init = jax.random.uniform(ks[6], (DEPTH, GDN_HEADS), f32, 1.0, 16.0)
    dt = jnp.exp(jax.random.uniform(ks[7], (DEPTH, GDN_HEADS), f32, np.log(1e-3), np.log(1e-1)))
    return {
        'x': nrm(ks[0], (BATCH, SEQ, D_MODEL), 1.0),
        'c': nrm(ks[1], (BATCH, D_MODEL), 1.0),
        'w_ada': nrm(ks[2], (DEPTH, D_MODEL, 6 * D_MODEL), D_MODEL ** -0.5),
        'b_ada': nrm(ks[3], (DEPTH, 6 * D_MODEL), 0.1),
        'norm1_w': gain(ks[4], (DEPTH, D_MODEL)),
        'w_in': nrm(ks[5], (DEPTH, D_MODEL, PROJ_WIDTH), D_MODEL ** -0.5),
        'conv_w': nrm(ks[8], (DEPTH, CONV_WIDTH, 1, 3 * GDN_WIDTH), CONV_WIDTH ** -0.5),
        'a_log': jnp.log(a_init),
        'dt_bias': dt + jnp.log(-jnp.expm1(-dt)),
        'gdn_norm_w': gain(ks[9], (DEPTH, HEAD_DIM)),
        'q_norm_w': gain(ks[10], (DEPTH, HEAD_DIM)),
        'k_norm_w': gain(ks[11], (DEPTH, HEAD_DIM)),
        'sinks': nrm(ks[12], (DEPTH, SWA_Q_HEADS), 1.0),
        'w_out': nrm(ks[13], (DEPTH, D_MIX, D_MODEL), D_MIX ** -0.5),
        'norm2_w': gain(ks[14], (DEPTH, D_MODEL)),
        'w_gate': nrm(ks[15], (DEPTH, D_MODEL, D_FF), D_MODEL ** -0.5),
        'w_up': nrm(ks[16], (DEPTH, D_MODEL, D_FF), D_MODEL ** -0.5),
        'w_down': nrm(ks[17], (DEPTH, D_FF, D_MODEL), D_FF ** -0.5),
    }

def first_block(x, c, w_ada, b_ada, norm1_w, w_in, conv_w, a_log, dt_bias, gdn_norm_w,
              q_norm_w, k_norm_w, sinks, w_out, norm2_w, w_gate, w_up, w_down):
    B, T, _ = x.shape
    split_sizes = (GDN_WIDTH,) * 4 + (GDN_HEADS,) * 2 + (SWA_WIDTH, SWA_KV_WIDTH, SWA_KV_WIDTH)
    split_points = []
    acc = 0
    for sz in split_sizes[:-1]:
        acc += sz
        split_points.append(acc)
    c_act = jax.nn.silu(c)
    for l in range(DEPTH):
        mod = (c_act @ w_ada[l] + b_ada[l])[:, None, :]
        shift1, scale1, gate1, shift2, scale2, gate2 = jnp.split(mod, 6, axis=-1)

        h = rms_norm(x, norm1_w[l]) * (1.0 + scale1) + shift1
        proj = h @ w_in[l]
        gq, gk, gv, gz, ga, gb, sq, sk, sv = jnp.split(proj, split_points, axis=-1)

        qkv = jax.nn.silu(causal_depthwise_conv(jnp.concatenate([gq, gk, gv], axis=-1), conv_w[l]))
        gq, gk, gv = jnp.split(qkv, 3, axis=-1)
        heads = lambda t: t.reshape(B, T, -1, HEAD_DIM)
        q_g = l2_norm(heads(gq))
        k_g = l2_norm(heads(gk))
        v_g = heads(gv).astype(jnp.float32)
        beta = jax.nn.sigmoid(gb.astype(jnp.float32))
        g = -jnp.exp(a_log[l].astype(jnp.float32)) * jax.nn.softplus(
            ga.astype(jnp.float32) + dt_bias[l].astype(jnp.float32))
        o_g = gated_delta_rule_chunked(q_g, k_g, v_g, g, beta).astype(x.dtype)
        o_g = rms_norm(o_g, gdn_norm_w[l]) * jax.nn.silu(heads(gz))
        o_g = o_g.reshape(B, T, GDN_WIDTH)

        q_s = rms_norm(heads(sq), q_norm_w[l])
        k_s = rms_norm(heads(sk), k_norm_w[l])
        v_s = heads(sv)
        o_s = sliding_window_attention(q_s, k_s, v_s, sinks[l])

        mixed = jnp.concatenate([o_g, o_s], axis=-1) @ w_out[l]
        x = x + gate1 * mixed

        h2 = rms_norm(x, norm2_w[l]) * (1.0 + scale2) + shift2
        ffn = (jax.nn.silu(h2 @ w_gate[l]) * (h2 @ w_up[l])) @ w_down[l]
        x = x + gate2 * ffn
    return x


DEPTH_2 = 2

N_MIXERS = 2
N_HEADS = 16
HEAD_DIM_2 = D_MODEL // N_HEADS
CONV_WIDTH_2 = 3
BRANCHES = ((128, 1), (512, 4), (2048, 16))
NUM_BUCKETS = 32
MAX_DISTANCE = 2048
D_FF_2 = ((8 * D_MODEL // 3 + 255) // 256) * 256
NEG_INF = -1e30


def rms_norm_2(x, g):
    xf = x.astype(jnp.float32)
    y = xf * lax.rsqrt(jnp.mean(xf * xf, axis=-1, keepdims=True) + EPS)
    return (y * g.astype(jnp.float32)).astype(x.dtype)

def t5_bucket(dist):
    exact = NUM_BUCKETS // 2
    df = jnp.maximum(dist, 1).astype(jnp.float32)
    large = exact + (jnp.log(df / exact) / math.log(MAX_DISTANCE / exact)
                     * (NUM_BUCKETS - exact)).astype(jnp.int32)
    large = jnp.minimum(large, NUM_BUCKETS - 1)
    return jnp.where(dist < exact, dist, large)

def short_conv_mixer(h, w_in, conv_k, w_out):
    b, c, u = jnp.split(h @ w_in, 3, axis=-1)
    y = lax.conv_general_dilated(
        c * u, conv_k[:, None, :].astype(u.dtype),
        window_strides=(1,), padding=[(CONV_WIDTH_2 - 1, 0)],
        dimension_numbers=("NWC", "WIO", "NWC"),
        feature_group_count=D_MODEL)
    return (b * y) @ w_out

def dilated_branch(q, k, v, rel_bias, window, dilation):
    bsz, seq, nh, dh = q.shape
    blk = window // dilation
    L = seq // dilation
    nb = -(-L // blk)
    Lp = nb * blk

    def sub(t):
        t = t.reshape(bsz, L, dilation, nh, dh).transpose(0, 2, 1, 3, 4)
        t = jnp.pad(t, ((0, 0), (0, 0), (0, Lp - L), (0, 0), (0, 0)))
        return t.reshape(bsz, dilation, nb, blk, nh, dh)

    def with_prev(t):
        prev = jnp.pad(t, ((0, 0), (0, 0), (1, 0), (0, 0), (0, 0), (0, 0)))[:, :, :-1]
        return jnp.concatenate([prev, t], axis=3)

    qb = sub(q)
    kk = with_prev(sub(k))
    vv = with_prev(sub(v))

    s = jnp.einsum("brnqhd,brnkhd->brnhqk", qb, kk,
                   preferred_element_type=jnp.float32) * (HEAD_DIM_2 ** -0.5)
    qi = jnp.arange(blk)[:, None]
    ki = jnp.arange(2 * blk)[None, :]
    rel = qi + blk - ki
    band = (rel >= 0) & (rel <= blk)
    valid_start = (jnp.arange(nb)[:, None, None] > 0) | (ki >= blk)[None]
    mask = band[None] & valid_start
    bias = rel_bias[t5_bucket(jnp.clip(rel, 0) * dilation)]
    s = s + bias.transpose(2, 0, 1).astype(jnp.float32)
    s = jnp.where(mask[:, None], s, NEG_INF)
    lse = jax.nn.logsumexp(s, axis=-1)
    p = jnp.exp(s - lse[..., None])
    o = jnp.einsum("brnhqk,brnkhd->brnqhd", p.astype(v.dtype), vv,
                   preferred_element_type=jnp.float32)

    o = o.reshape(bsz, dilation, Lp, nh, dh)[:, :, :L]
    o = o.transpose(0, 2, 1, 3, 4).reshape(bsz, seq, nh, dh)
    lse = lse.transpose(0, 1, 2, 4, 3).reshape(bsz, dilation, Lp, nh)[:, :, :L]
    lse = lse.transpose(0, 2, 1, 3).reshape(bsz, seq, nh)
    return o, lse

def dilated_attention_mixer(h, w_qkv, w_out, rel_bias):
    bsz, seq, _ = h.shape
    qkv = (h @ w_qkv).reshape(bsz, seq, 3, N_HEADS, HEAD_DIM_2)
    q, k, v = qkv[:, :, 0], qkv[:, :, 1], qkv[:, :, 2]
    outs, lses = [], []
    for window, dilation in BRANCHES:
        o, l = dilated_branch(q, k, v, rel_bias, window, dilation)
        outs.append(o)
        lses.append(l)
    alpha = jax.nn.softmax(jnp.stack(lses, axis=0), axis=0)
    o = jnp.sum(alpha[..., None] * jnp.stack(outs, axis=0), axis=0)
    return o.reshape(bsz, seq, D_MODEL).astype(h.dtype) @ w_out

def swiglu(h, w_gate, w_up, w_down):
    return (jax.nn.silu(h @ w_gate) * (h @ w_up)) @ w_down

def second_inputs(seed: int = 0) -> dict:
    key = jax.random.key(seed)
    ks = jax.random.split(key, 14)
    n_conv = (DEPTH_2 + 1) // 2
    n_attn = DEPTH_2 // 2
    f32 = jnp.float32
    nrm = lambda k, shape, scale: jax.random.normal(k, shape, f32) * scale
    return {
        "x": nrm(ks[0], (BATCH, SEQ, D_MODEL), 1.0),
        "mix_norm": 1.0 + nrm(ks[1], (DEPTH_2, D_MODEL), 0.05),
        "ffn_norm": 1.0 + nrm(ks[2], (DEPTH_2, D_MODEL), 0.05),
        "final_norm": 1.0 + nrm(ks[3], (D_MODEL,), 0.05),
        "conv_w_in": nrm(ks[4], (n_conv, D_MODEL, 3 * D_MODEL), D_MODEL ** -0.5),
        "conv_kernel": nrm(ks[5], (n_conv, CONV_WIDTH_2, D_MODEL), CONV_WIDTH_2 ** -0.5),
        "conv_w_out": nrm(ks[6], (n_conv, D_MODEL, D_MODEL), D_MODEL ** -0.5),
        "attn_w_qkv": nrm(ks[7], (n_attn, D_MODEL, 3 * D_MODEL), D_MODEL ** -0.5),
        "attn_w_out": nrm(ks[8], (n_attn, D_MODEL, D_MODEL), D_MODEL ** -0.5),
        "rel_bias": nrm(ks[9], (NUM_BUCKETS, N_HEADS), 0.2),
        "ffn_w_gate": nrm(ks[10], (DEPTH_2, D_MODEL, D_FF_2), D_MODEL ** -0.5),
        "ffn_w_up": nrm(ks[11], (DEPTH_2, D_MODEL, D_FF_2), D_MODEL ** -0.5),
        "ffn_w_down": nrm(ks[12], (DEPTH_2, D_FF_2, D_MODEL), D_FF_2 ** -0.5),
    }

def second_block(x, mix_norm, ffn_norm, final_norm, conv_w_in, conv_kernel, conv_w_out,
              attn_w_qkv, attn_w_out, rel_bias, ffn_w_gate, ffn_w_up, ffn_w_down):
    for i in range(DEPTH_2):
        h = rms_norm_2(x, mix_norm[i])
        j = i // N_MIXERS
        if i % N_MIXERS == 0:
            x = x + short_conv_mixer(h, conv_w_in[j], conv_kernel[j], conv_w_out[j])
        else:
            x = x + dilated_attention_mixer(h, attn_w_qkv[j], attn_w_out[j], rel_bias)
        h = rms_norm_2(x, ffn_norm[i])
        x = x + swiglu(h, ffn_w_gate[i], ffn_w_up[i], ffn_w_down[i])
    return rms_norm_2(x, final_norm)


def setup_inputs(seed=0):
    out = dict(first_inputs(seed))
    for name, value in second_inputs(seed + 1).items():
        if name != "x":
            out[name + "_2"] = value
    return out


def reference(
    x, c, w_ada, b_ada, norm1_w, w_in, conv_w, a_log, dt_bias, gdn_norm_w, q_norm_w, k_norm_w,
    sinks, w_out, norm2_w, w_gate, w_up, w_down, mix_norm_2, ffn_norm_2, final_norm_2,
    conv_w_in_2, conv_kernel_2, conv_w_out_2, attn_w_qkv_2, attn_w_out_2, rel_bias_2,
    ffn_w_gate_2, ffn_w_up_2, ffn_w_down_2,
):
    x = first_block(
        x, c, w_ada, b_ada, norm1_w, w_in, conv_w, a_log, dt_bias, gdn_norm_w, q_norm_w,
        k_norm_w, sinks, w_out, norm2_w, w_gate, w_up, w_down,
    )
    return second_block(
        x, mix_norm_2, ffn_norm_2, final_norm_2, conv_w_in_2, conv_kernel_2, conv_w_out_2,
        attn_w_qkv_2, attn_w_out_2, rel_bias_2, ffn_w_gate_2, ffn_w_up_2, ffn_w_down_2,
    )


_drawn_inputs = setup_inputs


def setup_inputs(seed=0):
    import zlib

    import numpy as np

    out = dict(_drawn_inputs(seed))
    spreads = {}
    factors = {'q_norm_w': 3.393, 'k_norm_w': 3.835, 'rel_bias_2': 3.025, 'sinks': 6.881}
    for name, (base, spread) in spreads.items():
        noise = np.random.default_rng([zlib.crc32(name.encode()), seed]).standard_normal(out[name].shape)
        drawn = base * np.exp(spread * noise) if base else spread * noise
        out[name] = __import__('jax').numpy.asarray(drawn.astype(out[name].dtype))
    for name, factor in factors.items():
        out[name] = (out[name] * factor).astype(out[name].dtype)
    return out
```

```python
from contextlib import ExitStack

import numpy as np
import concourse.bass as bass
from concourse import mybir

F32, F32R = mybir.dt.float32, mybir.dt.float32r
ALU, ACT, AX = mybir.AluOpType, mybir.ActivationFunctionType, mybir.AxisListType

P = 128
T = 256
TT = T // P
D = 1024
KD = D // P
FF = 2816
JF = FF // 256
HD = 64
EPS = 1e-6
BIG = 1e30
BLOCK = 2048
RING = 3
NEXP = 6

W_IN, W_OUT = 0, 11
FFN_BASE = [15, 64, 113]
CONV_BASE, CONV_OUT = 48, 60
QKV_BASE, ATT_OUT = 97, 109
N_WEIGHTS = 146
MOD_PARTS, MOD_BLOCKS = 3, 8
MOD_AFTER = [2, 2, 2, 2, 2, 1, 1, 1, 1, 1, 1]


def stream_places():
    at, of_w, of_mod = MOD_BLOCKS, [], list(range(MOD_BLOCKS))
    for n in MOD_AFTER:
        of_w.append(at)
        of_mod += list(range(at + 1, at + 1 + n))
        at += 1 + n
    return of_w, of_mod


RAW_OF_W, RAW_OF_MOD = stream_places()
MOD_TOTAL = MOD_PARTS * MOD_BLOCKS


def raw_index(w):
    return RAW_OF_W[w] if w < W_OUT else w + MOD_TOTAL


CONSTS = dict(ident=P, flip=P, tri=P, future=P, levels=(NEXP + 1) * P, headsel=2, ones=1, alibi=384)
VECS = dict(c=8, norm1=8, norm2=8, mix0=8, mix1=8, ffn0=8, ffn1=8, final=8, b_ada=48, conv_w=48,
            conv_k=24, gdn_w=1, qn_w=1, kn_w=1, dt_bias=8, a_log=8, sinks=8)


def columns(spec):
    out, at = {}, 0
    for name, n in spec.items():
        out[name] = (at, at + n)
        at += n
    return out, at


C_AT, N_CONST = columns(CONSTS)
V_AT, N_VEC = columns(VECS)


BIG_USES = (["kb01", "kb23", "q01", "q23"], ["eg"],
            ["v0", "v1", "kt", "sk", "sq01", "sq23"] + [f"G{g}" for g in range(4)]
            + [f"kk{g}" for g in range(4)] + [f"qk{g}" for g in range(4)],
            [f"tr{g}" for g in range(4)])
BIG_LIST = [(n, "dve") for n in BIG_USES[0]] + [(n, "act") for n in BIG_USES[1]] \
    + [(n, "dve") for n in BIG_USES[2]] + [(n, "act") for n in BIG_USES[3]]
BIG_INDEX = {n: i for i, (n, _) in enumerate(BIG_LIST)}


def big_reads(upto, engine):
    return sum(e == engine for _, e in BIG_LIST[:upto + 1])


class Semaphores:

    def __init__(self, new):
        self.x_loaded = new("x_loaded")
        self.vectors_loaded = new("vectors_loaded")
        self.consts_loaded = new("consts_loaded")
        self.gab_loaded = new("gab_loaded")
        self.t5_loaded = new("t5_loaded")
        self.t5_stored = new("t5_stored")
        self.tables_loaded = new("tables_loaded")
        self.out_stored = new("out_stored")
        self.pool_zeroed = new("pool_zeroed")
        self.c_act = new("c_act")
        self.mod_accumulated = new("mod_accumulated")
        self.mod_summed = new("mod_summed")
        self.mod_ready = new("mod_ready")
        self.dve_step = new("dve_step")
        self.act_step = new("act_step")
        self.hi_ready = new("hi_ready")
        self.lo_ready = new("lo_ready")
        self.block_used = new("block_used")
        self.acc_tile_done = new("acc_tile_done")
        self.x_ready = new("x_ready")
        self.squared = new("squared")
        self.sumsq_ready = new("sumsq_ready")
        self.inv_ready = new("inv_ready")
        self.rms_ready = new("rms_ready")
        self.rstd_ready = new("rstd_ready")
        self.t_ready = new("t_ready")
        self.h_hi_ready = new("h_hi_ready")
        self.h_lo_ready = new("h_lo_ready")
        self.gab_hi = new("gab_hi")
        self.gab_lo = new("gab_lo")
        self.gab_ready = new("gab_ready")
        self.gate_exp = new("gate_exp")
        self.gate_dve = new("gate_dve")
        self.gate_done = new("gate_done")
        self.cum_ready = new("cum_ready")
        self.decay_dve = new("decay_dve")
        self.decay_act = new("decay_act")
        self.proj_evac = new("proj_evac")
        self.pad_ready = new("pad_ready")
        self.conv_done = new("conv_done")
        self.feature_ready = new("feature_ready")
        self.head_squared = new("head_squared")
        self.head_sums = new("head_sums")
        self.head_inv = new("head_inv")
        self.head_rms = new("head_rms")
        self.coef_ready = new("coef_ready")
        self.big_ready = new("big_ready")
        self.big_read_dve = new("big_read_dve")
        self.big_read_act = new("big_read_act")
        self.d_shifted = new("d_shifted")
        self.d_ready = new("d_ready")
        self.at_ready = new("at_ready")
        self.b_ready = new("b_ready")
        self.xt_ready = new("xt_ready")
        self.x_copied = new("x_copied")
        self.p_ready = new("p_ready")
        self.p_copied = new("p_copied")
        self.qt_ready = new("qt_ready")
        self.xtr_ready = new("xtr_ready")
        self.row_scaled = new("row_scaled")
        self.u_ready = new("u_ready")
        self.u_copied = new("u_copied")
        self.s_ready = new("s_ready")
        self.s_copied = new("s_copied")
        self.o0_ready = new("o0_ready")
        self.o_copied = new("o_copied")
        self.r_ready = new("r_ready")
        self.r_done = new("r_done")
        self.vn_ready = new("vn_ready")
        self.vn_copied = new("vn_copied")
        self.o1_ready = new("o1_ready")
        self.o_squared = new("o_squared")
        self.o_sums = new("o_sums")
        self.o_inv = new("o_inv")
        self.o_rms = new("o_rms")
        self.o_rows = new("o_rows")
        self.o_gated = new("o_gated")
        self.o_hi_done = new("o_hi_done")
        self.o_lo_done = new("o_lo_done")
        self.scores_ready = new("scores_ready")
        self.scores_biased = new("scores_biased")
        self.negmax_ready = new("negmax_ready")
        self.exp_ready = new("exp_ready")
        self.probs_ready = new("probs_ready")
        self.ptrans_ready = new("ptrans_ready")
        self.ptrans_copied = new("ptrans_copied")
        self.pv_ready = new("pv_ready")
        self.pv_hi = new("pv_hi")
        self.pv_lo = new("pv_lo")
        self.silu_ready = new("silu_ready")
        self.hid_ready = new("hid_ready")
        self.hid_hi_ready = new("hid_hi_ready")
        self.hid_lo_ready = new("hid_lo_ready")
        self.c_copied = new("c_copied")
        self.cu_ready = new("cu_ready")
        self.by_ready = new("by_ready")
        self.by_hi = new("by_hi")
        self.by_lo = new("by_lo")
        self.qkv_copied = new("qkv_copied")
        self.t5_psum = new("t5_psum")
        self.t5_row = new("t5_row")


def build(nc, stream, x_in, consts_in, vectors_in, gab_in, t5_onehot, t5_log, rel_bias, out):
    t5_scratch = nc.dram_tensor("t5_scratch", (16, 384), F32, kind="Internal")
    with ExitStack() as ctx:
        s = Semaphores(lambda name: ctx.enter_context(nc.semaphore(name)))
        raw_landed = [ctx.enter_context(nc.semaphore(f"raw_landed{i}")) for i in range(RING)]

        def sb(name, shape, dt=F32, stack=ctx):
            return stack.enter_context(nc.sbuf_tensor(name, shape, dt))

        raw = sb("raw", [P, RING, BLOCK])
        w_hi = sb("w_hi", [P, RING, BLOCK], F32R)
        w_lo = sb("w_lo", [P, RING, BLOCK], F32R)
        x = sb("x_res", [P, KD, T])
        nt = sb("norm_tmp", [P, KD, T])
        h_hi = sb("h_hi", [P, KD, T], F32R)
        h_lo = sb("h_lo", [P, KD, T], F32R)
        zero_r = sb("zero_r", [P, 512], F32R)
        consts = sb("consts", [P, N_CONST])
        vec = sb("vec", [P, N_VEC])
        c_act = sb("c_act_sb", [P, 8])
        mods = sb("mods", [P, 48])
        a1 = sb("a1", [P, 8])
        a2 = sb("a2", [P, 8])
        qk_w = sb("qk_w", [P, 1])
        ms = sb("ms", [P, TT])
        inv = sb("inv", [P, TT])
        rms = sb("rms", [P, TT])
        soft = sb("soft", [P, 6, 8])
        sink2 = sb("sink2", [P, 8, 2])

        def const(name):
            a, b = C_AT[name]
            return consts[:, a:b]

        def vecs(name):
            a, b = V_AT[name]
            return vec[:, a:b]

        ident, tri, future, headsel, ones = (const(n) for n in ("ident", "tri", "future", "headsel", "ones"))
        level_mask = [consts[:, C_AT["levels"][0] + P * i:C_AT["levels"][0] + P * (i + 1)] for i in range(NEXP + 1)]

        with ExitStack() as one:
            def p1(name, shape, dt=F32):
                return sb(name, shape, dt, one)
            kT, qT, kbT, zT = (p1(n, [P, 4, T]) for n in ("kT", "qT", "kbT", "zT"))
            kbgT, qdT = (p1(n, [P, 4, P]) for n in ("kbgT", "qdT"))
            kd = p1("kd", [P, 512])
            vb = p1("vb", [P, TT, 512])
            AT, X, qkT, XT = (p1(n, [P, 4, 4 * P]) for n in ("AT", "X_inv", "qkT", "XT"))
            inv_b = p1("inv_b", [P, 4 * 4 * P])
            inv_p = p1("inv_p", [P, 4 * 4 * P])
            qs = p1("qs", [P, 4, T])
            ks = p1("ks", [P, T])
            vs = p1("vs", [P, TT, P])
            pT1 = p1("probsT1", [P, 4, 384])
            gab_w = p1("gab_w", [P, KD * 16])
            gab_wh = p1("gab_wh", [P, KD * 16], F32R)
            gab_wl = p1("gab_wl", [P, KD * 16], F32R)
            gt = p1("gate_tmp", [P, 8, TT * 8])
            beta, g, Gs, coefk, coefq = (p1(n, [P, TT * 8]) for n in ("beta", "g", "Gs", "coefk", "coefq"))
            kds = p1("kds", [P, 2, 8])
            hs = p1("head_stat", [P, 3, TT * 16])
            ss = p1("swa_stat", [P, 3, TT * 10])
            os_ = p1("out_stat", [P, 3, TT * 8])
            rb = p1("rel_bias_sb", [32, 16])
            t5r = p1("t5_row_sb", [16, 384])
        sc1 = nt[:, 0:6, :].rearrange("p a b -> p (a b)").rearrange("p (h c) -> p h c", h=4)
        eg = pT1[:, :, :].rearrange("p a b -> p (a b)")[:, 0:512].rearrange("p (a b) -> p a b", a=4)
        oh = XT[0:32, 2, 0:384]
        t5l = XT[0:16, 3, 0:384]
        DT = X
        mod_acc = inv_b
        vT = inv_p[:, 0:1024].rearrange("p (a b) -> p a b", a=4)
        pad = inv_p[:, 1024:1024 + 2 * 259].rearrange("p (a b) -> p a b", a=2)
        cacc = XT[:, 0, :]
        sqb = XT[:, 1, :]
        u0, vn, r1 = inv_b[:, 0:512], inv_b[:, 512:1024], inv_b[:, 1024:1536]
        S1 = inv_b[:, 1536:1792]
        oT = inv_p[:, 0:1024].rearrange("p (a b) -> p a b", a=4)
        osq = inv_p[:, 1024:2048].rearrange("p (a b) -> p a b", a=4)
        Bm = inv_b[:, :].rearrange("p (g c) -> p g c", g=4)
        Pm = inv_p[:, :].rearrange("p (g c) -> p g c", g=4)

        t5 = sb("t5_tables", [P, 16, 384])
        o_hi = sb("o_hi", [P, KD, T], F32R)
        o_lo = sb("o_lo", [P, KD, T], F32R)
        hid_hi = sb("hid_hi", [P, 2, T], F32R)
        hid_lo = sb("hid_lo", [P, 2, T], F32R)
        sg = sb("silu_gate", [P, 2 * T])
        hid = sb("hid", [P, 2 * T])
        c_sb = sb("c_sb", [P, 2 * T])
        cu = sb("cu_pad", [P, 2, T + 2])
        yb = sb("y_conv", [P, 2, T])
        q2 = sb("q2", [P, 2, 2, T])
        k2 = sb("k2", [P, 2, 2, T])
        v2 = sb("v2", [P, 2, TT, 256])
        sc2 = sb("scores2", [P, 4, 384])
        pT2 = sb("probsT2", [P, 4, 384])

        acc = ctx.enter_context(nc.psum_tensor("acc", [P, 2048], F32))
        A = [acc[:, 512 * i:512 * (i + 1)] for i in range(4)]
        B = [ctx.enter_context(nc.psum_tensor(f"bank{i}", [P, 512], F32)) for i in range(4, 8)]
        STAT = B[2]
        BIGB = [B[0], B[1], B[3]]

        def big(name):
            return BIGB[BIG_INDEX[name] % 3]

        norm_scale = [a1[:, :], a2[:, :], vecs("mix0"), vecs("ffn0"), vecs("mix1"), vecs("ffn1"), vecs("final")]
        norm_shift = [mods[:, 0:8], mods[:, 24:32], None, None, None, None, None]
        gates = [mods[:, 16:24], mods[:, 40:48], None, None, None, None]

        block = ctx.enter_context(nc.Block())

        @block.sync
        def _(sp):
            order = {}
            for w in range(W_OUT):
                order[RAW_OF_W[w]] = ("w", w)
            for m in range(MOD_TOTAL):
                order[RAW_OF_MOD[m]] = ("mod", m)
            for r in range(W_OUT + MOD_TOTAL):
                if r >= RING:
                    kind, n = order[r - RING]
                    sp.wait_ge(s.lo_ready if kind == "w" else s.mod_accumulated, n + 1)
                sp.dma_start(raw[:, r % RING, :], stream[r]).then_inc(raw_landed[r % RING], 16)
            r0 = W_OUT + MOD_TOTAL
            for i in range(RING):
                r = r0 + i
                kind, n = order[r - RING]
                sp.wait_ge(s.lo_ready if kind == "w" else s.mod_accumulated, n + 1)
                sp.dma_start(raw[:, r % RING, :], stream[r]).then_inc(raw_landed[r % RING], 16)
            with sp.Fori(1, (N_WEIGHTS - W_OUT) // RING) as it:
                for i in range(RING):
                    r = r0 + i
                    sp.wait_ge(s.lo_ready, it * RING + (W_OUT + i - RING + 1))
                    sp.dma_start(raw[:, r % RING, :], stream[it * RING + r]).then_inc(raw_landed[r % RING], 16)
            for m in range(2):
                sp.wait_ge(s.t_ready, 8 * 6 + 4 * (m + 1))
                sp.dma_start(out[:, 4 * m:4 * m + 4, :], nt[:, 4 * m:4 * m + 4, :]).then_inc(s.out_stored, 16)
            sp.wait_ge(s.out_stored, 32)

        @block.gpsimd
        def _(pool):
            pool.memset(zero_r[:, :].bitcast(F32), 0.0).then_inc(s.pool_zeroed, 1)
            pool.memset(pad[:, :, 0:3], 0.0).then_inc(s.pool_zeroed, 1)
            pool.wait_ge(s.t5_row, 1)
            pool.dma_start(t5_scratch.ap(), t5r[:, :]).then_inc(s.t5_stored, 16)
            for l in range(1, NEXP + 1):
                for gi in range(4):
                    if l == 1:
                        pool.wait_ge(s.at_ready, gi + 1)
                        pool.wait_ge(s.mod_summed, 3)
                    else:
                        pool.wait_ge(s.p_ready, 4 * (l - 2) + gi + 1)
                    pool.tensor_tensor(
                        Bm[:, gi, :].rearrange("p (i c) -> p i c", i=4),
                        AT[:, gi, :].rearrange("p (i c) -> p i c", i=4),
                        level_mask[l].unsqueeze(1).broadcast_to([P, 4, P]), ALU.mult).then_inc(s.b_ready, 1)
            pool.wait_ge(s.t5_stored, 16)
            pool.wait_ge(s.x_ready, 8)
            pool.dma_start(t5[:, :, 0:256], bass.AP(t5_scratch, 0, [[1, P], [384, 16], [1, 256]])).then_inc(s.tables_loaded, 16)
            pool.dma_start(t5[:, :, 256:384], bass.AP(t5_scratch, 128, [[1, P], [384, 16], [1, 128]])).then_inc(s.tables_loaded, 16)
            pool.memset(cu[:, :, 0:2], 0.0).then_inc(s.pool_zeroed, 1)
            pool.wait_ge(s.tables_loaded, 32)

        @block.scalar
        def _(act):
            steps = [0]

            def link(ins):
                steps[0] += 1
                ins.then_inc(s.act_step, 1)
                act.wait_ge(s.act_step, steps[0])

            act.dma_start(vec[:, :], vectors_in).then_inc(s.vectors_loaded, 16)
            act.dma_start(x[:, :, :], x_in).then_inc(s.x_loaded, 16)
            act.dma_start(consts[:, :], consts_in).then_inc(s.consts_loaded, 16)
            act.dma_start(gab_w[:, :], gab_in).then_inc(s.gab_loaded, 16)
            act.dma_start(oh, t5_onehot).then_inc(s.t5_loaded, 16)
            act.dma_start(rb[:, :], rel_bias).then_inc(s.t5_loaded, 16)
            act.dma_start(t5l, t5_log).then_inc(s.t5_loaded, 16)

            def hi(w, it=0):
                r = raw_index(w)
                act.wait_ge(raw_landed[r % RING], (it + (r // RING + 1)) * 16)
                if not isinstance(it, int) or w + RING * it >= RING:
                    act.wait_ge(s.block_used, it * RING + (w - RING + 1))
                act.activation(w_hi[:, w % RING, :], raw[:, r % RING, :], ACT.Copy).then_inc(s.hi_ready, 1)

            def squares(n):
                for m in range(KD):
                    if n:
                        act.wait_ge(s.x_ready, 8 * (n - 1) + m + 1)
                    act.activation(nt[:, m, :], x[:, m, :], ACT.Square).then_inc(s.squared, 1)

            def root(n):
                act.wait_ge(s.inv_ready, n + 1)
                act.activation(rms[:, :], inv[:, :], ACT.Sqrt).then_inc(s.rms_ready, 1)

            def h_high(n):
                for k in range(KD):
                    act.wait_ge(s.t_ready, 8 * n + k + 1)
                    if norm_shift[n] is not None:
                        act.activation(h_hi[:, k, :], nt[:, k, :], ACT.Identity, bias=norm_shift[n][:, k:k + 1]).then_inc(s.h_hi_ready, 1)
                    else:
                        act.activation(h_hi[:, k, :], nt[:, k, :], ACT.Copy).then_inc(s.h_hi_ready, 1)

            act.wait_ge(s.vectors_loaded, 16)
            act.activation(c_act[:, :], vecs("c"), ACT.Silu).then_inc(s.c_act, 1)
            act.wait_ge(s.gab_loaded, 16)
            act.activation(gab_wh[:, :], gab_w[:, :], ACT.Copy).then_inc(s.gab_hi, 1)
            act.wait_ge(s.x_loaded, 16)
            squares(0)
            root(0)
            hi(0)
            h_high(0)
            hi(1)

            dest = [kT[:, 0:2, :], kT[:, 2:4, :], qT[:, 0:2, :], qT[:, 2:4, :], vT[:, 0:2, :], vT[:, 2:4, :]]

            def feature(w):
                act.wait_ge(s.conv_done, w + 1)
                act.activation(dest[w], cacc.rearrange("p (a b) -> p a b", a=2), ACT.Silu).then_inc(s.feature_ready, 1)
                if w < 4:
                    act.wait_ge(s.feature_ready, w + 1)
                    if w:
                        act.wait_ge(s.head_sums, w)
                    act.activation(sqb.rearrange("p (a b) -> p a b", a=2), dest[w], ACT.Square).then_inc(s.head_squared, 1)

            for w in range(6):
                hi(w + 2)
                act.wait_ge(s.block_used, w + 1)
                if w == 0:
                    act.wait_ge(s.pool_zeroed, 2)
                if w:
                    act.wait_ge(s.conv_done, w)
                act.activation(pad[:, :, 3:259], A[w % 4].rearrange("p (a b) -> p a b", a=2), ACT.Copy).then_inc(s.pad_ready, 1)
                if w:
                    feature(w - 1)
                if w == 1:
                    act.wait_ge(s.gate_dve, 1)
                    act.activation(gt[:, 1, :], gt[:, 0, :], ACT.Exp).then_inc(s.gate_exp, 1)
                    act.activation(gt[:, 3, :], gt[:, 2, :], ACT.Exp).then_inc(s.gate_exp, 1)
                    act.activation(gt[:, 4, 0:8], vecs("a_log"), ACT.Exp).then_inc(s.gate_exp, 1)
                    act.wait_ge(s.gate_dve, 2)
                    act.activation(gt[:, 5, :], gt[:, 7, :], ACT.Ln).then_inc(s.gate_exp, 1)
            feature(5)
            act.wait_ge(s.decay_dve, 1)
            act.activation(kds[:, 1, :], kds[:, 0, :], ACT.Exp).then_inc(s.decay_act, 1)
            for w in (6, 7):
                hi(w + 2)
                act.wait_ge(s.block_used, w + 1)
                act.activation(zT[:, 2 * (w - 6):2 * (w - 6) + 2, :], A[w % 4].rearrange("p (a b) -> p a b", a=2),
                               ACT.Silu).then_inc(s.proj_evac, 1)
            act.wait_ge(s.head_inv, 1)
            act.activation(hs[:, 2, :], hs[:, 1, :], ACT.Sqrt).then_inc(s.head_rms, 1)
            for w in (8, 9):
                hi(w + 2)
                act.wait_ge(s.block_used, w + 1)
                link(act.activation(qs[:, 2 * (w - 8):2 * (w - 8) + 2, :], A[w % 4].rearrange("p (a b) -> p a b", a=2), ACT.Copy))
                act.wait_ge(s.head_sums, w - 4)
                act.activation(sqb, A[w % 4], ACT.Square).then_inc(s.head_squared, 1)
            act.wait_ge(s.block_used, 11)
            act.activation(ks[:, :], A[2][:, 0:256], ACT.Copy).then_inc(s.proj_evac, 1)
            act.activation(vs[:, :, :].rearrange("p t c -> p (t c)"), A[2][:, 256:512], ACT.Copy).then_inc(s.proj_evac, 1)
            act.wait_ge(s.head_sums, 6)
            act.activation(sqb[:, 0:256], A[2][:, 0:256], ACT.Square).then_inc(s.head_squared, 1)
            hi(12)
            act.wait_ge(s.big_ready, BIG_INDEX["eg"] + 1)
            act.activation(eg.rearrange("p a b -> p (a b)"), big("eg")[:, :], ACT.Exp).then_inc(s.big_read_act, 1)
            act.wait_ge(s.head_inv, 2)
            act.activation(ss[:, 2, :], ss[:, 1, :], ACT.Sqrt).then_inc(s.head_rms, 1)
            hi(13)

            def exps(a, sc):
                act.wait_ge(s.negmax_ready, a + 1)
                for hh in range(4):
                    for part, (c0, c1) in enumerate(((0, 256), (256, 384))):
                        act.activation(sc[:, hh, c0:c1], sc[:, hh, c0:c1], ACT.Exp,
                                       bias=soft[:, 1, 2 * hh + part:2 * hh + part + 1],
                                       accum_out=soft[:, 2, 2 * hh + part:2 * hh + part + 1]).then_inc(s.exp_ready, 1)
                if a < 2:
                    act.activation(soft[:, 3, :], soft[:, 3, :], ACT.Exp).then_inc(s.exp_ready, 1)

            def probs_copy(a, bank, pT):
                if a == 0:
                    act.wait_ge(s.row_scaled, 2)
                for hh in range(4):
                    act.wait_ge(s.ptrans_ready, 4 * a + hh + 1)
                    act.activation(pT[:, hh, :], bank[hh][:, 0:384], ACT.Copy).then_inc(s.ptrans_copied, 1)

            def pv_high(a, bank, dst):
                act.wait_ge(s.pv_ready, a + 1)
                act.activation(dst, bank[0].rearrange("p (a b) -> p a b", a=2), ACT.Copy).then_inc(s.pv_hi, 1)

            exps(0, sc1)
            for gi in range(4):
                act.wait_ge(s.d_shifted, gi + 1)
                act.activation(DT[:, gi, :], DT[:, gi, :], ACT.Exp).then_inc(s.d_ready, 1)
            def x_copy(l, gi, bank):
                act.wait_ge(s.xtr_ready, 4 * l + gi + 1)
                return act.activation(X[:, gi, :], bank[:, :], ACT.Copy)

            for gi in range(4):
                if gi == 0:
                    act.wait_ge(s.big_read_dve, big_reads(BIG_INDEX["qk3"], "dve"))
                x_copy(0, gi, big(f"tr{gi}")).then_inc(s.x_copied, 1)
            probs_copy(0, A, pT1)
            pv_high(0, A, h_hi[:, 4:6, :])
            for l in range(1, NEXP + 1):
                for gi in range(4):
                    act.wait_ge(s.p_ready, 4 * (l - 1) + gi + 1)
                    act.activation(Pm[:, gi, :], B[gi][:, :], ACT.Copy).then_inc(s.p_copied, 1)
                if l < NEXP:
                    for gi in range(4):
                        x_copy(l, gi, B[gi]).then_inc(s.x_copied, 1)
                if l == 1:
                    exps(1, sc1)
                if l == 3:
                    probs_copy(1, A, pT1)
                if l == 4:
                    pv_high(1, A, h_hi[:, 6:8, :])
            act.wait_ge(s.u_ready, 1)
            act.activation(u0, B[0][:, :], ACT.Copy).then_inc(s.u_copied, 1)
            hi(14)
            act.wait_ge(s.o0_ready, 1)
            for par in range(2):
                rows = slice(64 * par, 64 * par + 64)
                act.activation(oT[rows, :, 0:P], B[2 + par][rows, :].rearrange("p (a b) -> p a b", a=4), ACT.Copy).then_inc(s.o_copied, 1)
            act.wait_ge(s.vn_ready, 1)
            act.activation(vn, B[0][:, :], ACT.Copy).then_inc(s.vn_copied, 1)
            act.wait_ge(s.o1_ready, 1)
            for par in range(2):
                rows = slice(64 * par, 64 * par + 64)
                act.activation(oT[rows, :, P:T], B[par][rows, :].rearrange("p (a b) -> p a b", a=4), ACT.Copy).then_inc(s.o_copied, 1)
            act.wait_ge(s.o_copied, 4)
            act.activation(osq, oT, ACT.Square).then_inc(s.o_squared, 1)
            act.wait_ge(s.o_inv, 1)
            act.activation(os_[:, 2, :], os_[:, 1, :], ACT.Sqrt).then_inc(s.o_rms, 1)
            for i in range(2):
                act.wait_ge(s.o_gated, i + 1)
                act.activation(h_hi[:, 2 * i:2 * i + 2, :], oT[:, 2 * i:2 * i + 2, :], ACT.Copy).then_inc(s.o_hi_done, 1)
            hi(15)
            hi(16)

            def norm(n):
                squares(n)
                root(n)
                h_high(n)

            def ffn(f):
                F = FFN_BASE[f]

                def silu(j, used):
                    act.wait_ge(s.block_used, used)
                    if not (isinstance(j, int) and f + j == 0):
                        act.wait_ge(s.hid_ready, j + JF * f)
                    act.activation(sg[:, :], B[0][:, :], ACT.Silu).then_inc(s.silu_ready, 1)

                def hid_high(j, used):
                    act.wait_ge(s.hid_ready, j + (JF * f + 1))
                    if used is not None:
                        act.wait_ge(s.block_used, used)
                    act.activation(hid_hi[:, :, :].rearrange("p a b -> p (a b)"), hid[:, :], ACT.Copy).then_inc(s.hid_hi_ready, 1)

                norm(2 * f + 1)
                hi(F + 2)
                silu(0, F + 1)
                hi(F + 3)
                hid_high(0, None)

                def body(j, it):
                    hi(F + 4, it)
                    silu(j, it * RING + (F + 3))
                    hi(F + 5, it)
                    if f < 2 or not isinstance(j, int):
                        hi(F + 6, it)
                    hid_high(j, it * RING + (F + 5))

                with act.Fori(1, JF - 1) as j:
                    body(j, j - 1)
                body(JF - 1, JF - 2)
                if f < 2:
                    hi(F + 34)

            ffn(0)
            norm(2)
            for i in range(4):
                w = CONV_BASE + 3 * i
                hi(w + 2)
                act.wait_ge(s.block_used, w + 2)
                if i:
                    act.wait_ge(s.cu_ready, i)
                hi(w + 3)
                act.activation(c_sb[:, :], B[1][:, :], ACT.Copy).then_inc(s.c_copied, 1)
                hi(w + 4)
                act.wait_ge(s.by_ready, i + 1)
                act.activation(o_hi[:, 2 * i:2 * i + 2, :], yb[:, :, :], ACT.Copy).then_inc(s.by_hi, 1)
            for w in range(CONV_OUT + 2, CONV_OUT + 6):
                hi(w)
            ffn(1)
            norm(4)
            for i in range(5):
                w, a = QKV_BASE + 3 * i, i + 1
                if i < 4:
                    hi(w + 2)
                    act.wait_ge(s.block_used, w + 1)
                    act.mul(q2[:, i % 2, :, :].rearrange("p a (t c) -> p (a t) c", t=TT), A[0].rearrange("p (a c) -> p a c", a=2 * TT)[:, :, ::-1], HD ** -0.5).then_inc(s.qkv_copied, 1)
                if i:
                    exps(a, sc2)
                if i < 4:
                    hi(w + 3)
                    act.wait_ge(s.block_used, w + 2)
                    act.activation(k2[:, i % 2, :, :].rearrange("p a b -> p (a b)"), A[1], ACT.Copy).then_inc(s.qkv_copied, 1)
                    hi(w + 4)
                if i:
                    probs_copy(a, B, pT2)
                if i < 4:
                    act.wait_ge(s.block_used, w + 3)
                    act.activation(v2[:, i % 2, :, :].rearrange("p a b -> p (a b)"), A[2], ACT.Copy).then_inc(s.qkv_copied, 1)
                if i:
                    pv_high(a, B, o_hi[:, 2 * i - 2:2 * i, :])
            for w in range(ATT_OUT + 2, ATT_OUT + 6):
                hi(w)
            ffn(2)
            squares(6)
            root(6)

        @block.vector
        def _(dve):
            steps = [0]

            def link(ins):
                steps[0] += 1
                ins.then_inc(s.dve_step, 1)
                dve.wait_ge(s.dve_step, steps[0])

            def lo(w, it=0):
                dve.wait_ge(s.hi_ready, it * RING + (w + 1))
                dve.tensor_tensor(w_lo[:, w % RING, :], raw[:, raw_index(w) % RING, :], w_hi[:, w % RING, :],
                                  ALU.subtract).then_inc(s.lo_ready, 1)

            def accumulate(m):
                k, r = m % MOD_BLOCKS, RAW_OF_MOD[m]
                dve.wait_ge(raw_landed[r % RING], 16 * (r // RING + 1))
                if k == 0:
                    if m:
                        dve.wait_ge(s.mod_summed, m // MOD_BLOCKS)
                    dve.tensor_scalar(mod_acc[:, :], raw[:, r % RING, :], c_act[:, 0:1], None, ALU.mult).then_inc(s.mod_accumulated, 1)
                else:
                    dve.wait_ge(s.mod_accumulated, m)
                    dve.scalar_tensor_tensor(out=mod_acc[:, :], in0=raw[:, r % RING, :], scalar=c_act[:, k:k + 1],
                                             in1=mod_acc[:, :], op0=ALU.mult, op1=ALU.add).then_inc(s.mod_accumulated, 1)

            def modulation(part):
                dve.wait_ge(s.mod_summed, part + 1)
                b0 = V_AT["b_ada"][0] + 16 * part
                link(dve.tensor_tensor(mods[:, 16 * part:16 * part + 16], STAT[:, 480 + 0:496], vec[:, b0:b0 + 16], ALU.add))
                if part == 0:
                    dve.scalar_tensor_tensor(out=a1[:, :], in0=mods[:, 8:16], scalar=1.0, in1=vecs("norm1"),
                                             op0=ALU.add, op1=ALU.mult).then_inc(s.mod_ready, 1)
                elif part == 2:
                    dve.scalar_tensor_tensor(out=a2[:, :], in0=mods[:, 32:40], scalar=1.0, in1=vecs("norm2"),
                                             op0=ALU.add, op1=ALU.mult).then_inc(s.mod_ready, 1)

            def inverse_mean(n):
                dve.wait_ge(s.sumsq_ready, n + 1)
                link(dve.tensor_scalar(ms[:, :], B[3][:, 0:TT], 1.0 / D, EPS, ALU.mult, ALU.add))
                dve.reciprocal(inv[:, :], ms[:, :]).then_inc(s.inv_ready, 1)

            def h_parts(n):
                dve.wait_ge(s.rstd_ready, n + 1)
                rstd = B[3][:, 256:512]

                def scaled(k):
                    dve.scalar_tensor_tensor(out=nt[:, k, :], in0=x[:, k, :], scalar=norm_scale[n][:, k:k + 1],
                                             in1=rstd, op0=ALU.mult, op1=ALU.mult).then_inc(s.t_ready, 1)

                def low(k):
                    dve.wait_ge(s.h_hi_ready, 8 * n + k + 1)
                    if norm_shift[n] is not None:
                        dve.scalar_tensor_tensor(out=h_lo[:, k, :], in0=nt[:, k, :], scalar=norm_shift[n][:, k:k + 1],
                                                 in1=h_hi[:, k, :], op0=ALU.add, op1=ALU.subtract).then_inc(s.h_lo_ready, 1)
                    else:
                        dve.tensor_tensor(h_lo[:, k, :], nt[:, k, :], h_hi[:, k, :], ALU.subtract).then_inc(s.h_lo_ready, 1)

                for k in range(KD):
                    scaled(k)
                    if n < 6 and k >= 1:
                        low(k - 1)
                if n < 6:
                    low(KD - 1)

            def residual(r, last):
                for m in range(KD):
                    if m < KD - 2:
                        dve.wait_ge(s.acc_tile_done, 3 * r + m // 2 + 1)
                    else:
                        dve.wait_ge(s.block_used, last + 1)
                    a = acc[:, 256 * m:256 * m + 256]
                    if gates[r] is not None:
                        dve.scalar_tensor_tensor(out=x[:, m, :], in0=a, scalar=gates[r][:, m:m + 1], in1=x[:, m, :],
                                                 op0=ALU.mult, op1=ALU.add).then_inc(s.x_ready, 1)
                    else:
                        dve.tensor_tensor(x[:, m, :], a, x[:, m, :], ALU.add).then_inc(s.x_ready, 1)

            dve.wait_ge(s.vectors_loaded, 16)
            dve.wait_ge(s.c_act, 1)
            link(dve.tensor_scalar(qk_w[:, :], vecs("qn_w"), HD ** -0.5, None, ALU.mult))
            link(dve.tensor_copy(sink2[:, :, 0], vecs("sinks")))
            link(dve.tensor_copy(sink2[:, :, 1], vecs("sinks")))
            dve.wait_ge(s.gab_hi, 1)
            dve.tensor_tensor(gab_wl[:, :], gab_w[:, :], gab_wh[:, :], ALU.subtract).then_inc(s.gab_lo, 1)
            dve.wait_ge(s.t5_psum, 1)
            dve.wait_ge(s.t5_loaded, 48)
            dve.tensor_tensor(t5r[:, :], A[0][0:16, 0:384], t5l, ALU.add).then_inc(s.t5_row, 1)
            inverse_mean(0)
            for m in range(MOD_BLOCKS):
                accumulate(m)
            lo(0)
            modulation(0)
            dve.wait_ge(s.mod_ready, 1)
            h_parts(0)
            lo(1)

            at = MOD_BLOCKS
            for w in range(11):
                if w == 4:
                    dve.wait_ge(s.cum_ready, 1)
                    modulation(1)
                    link(dve.tensor_copy(Gs[:, :], STAT[:, 32:48]))
                    dve.tensor_tensor(kds[:, 0, :], STAT[:, 48:56], Gs[:, 0:8], ALU.subtract).then_inc(s.decay_dve, 1)
                for _ in range(MOD_AFTER[w]):
                    accumulate(at)
                    at += 1
                lo(w + 2)
                if w < 6:
                    dve.wait_ge(s.pad_ready, w + 1)
                    if w:
                        dve.wait_ge(s.feature_ready, w)
                    tile0 = (4, 6, 0, 2, 8, 10)[w]
                    for mt in range(2):
                        o = cacc[:, 256 * mt:256 * mt + 256]
                        cw = V_AT["conv_w"][0] + 4 * (tile0 + mt)
                        dve.tensor_scalar(o, pad[:, mt, 0:256], vec[:, cw:cw + 1], None, ALU.mult).then_inc(s.dve_step, 1)
                        steps[0] += 1
                    for tap in range(1, 4):
                        for mt in range(2):
                            o = cacc[:, 256 * mt:256 * mt + 256]
                            cw = V_AT["conv_w"][0] + 4 * (tile0 + mt) + tap
                            dve.wait_ge(s.dve_step, steps[0] - 1)
                            ins = dve.scalar_tensor_tensor(out=o, in0=pad[:, mt, tap:tap + 256], scalar=vec[:, cw:cw + 1],
                                                           in1=o, op0=ALU.mult, op1=ALU.add)
                            if tap == 3 and mt == 1:
                                dve.wait_ge(s.dve_step, steps[0])
                                ins.then_inc(s.conv_done, 1)
                            else:
                                ins.then_inc(s.dve_step, 1)
                                steps[0] += 1
                if w == 0:
                    dve.wait_ge(s.gab_ready, 1)
                    ga = STAT[:, 0:32].rearrange("p (t c) -> p t c", t=TT)
                    v8 = lambda a: a.rearrange("p (t c) -> p t c", t=TT)
                    link(dve.tensor_tensor(v8(gt[:, 6, :]), ga[:, :, 0:8],
                                           vecs("dt_bias").unsqueeze(1).broadcast_to([P, TT, 8]), ALU.add))
                    link(dve.tensor_scalar(v8(gt[:, 0, :]), ga[:, :, 8:16], -1.0, None, ALU.mult))
                    dve.scalar_tensor_tensor(out=gt[:, 2, :], in0=gt[:, 6, :], scalar=-1.0, in1=gt[:, 6, :],
                                             op0=ALU.mult, op1=ALU.min).then_inc(s.gate_dve, 1)
                if w == 1:
                    dve.wait_ge(s.gate_exp, 3)
                    dve.tensor_scalar(gt[:, 7, :], gt[:, 3, :], 1.0, None, ALU.add).then_inc(s.gate_dve, 1)
                    link(dve.tensor_scalar(gt[:, 2, :], gt[:, 1, :], 1.0, None, ALU.add))
                    link(dve.reciprocal(beta[:, :], gt[:, 2, :]))
                    dve.wait_ge(s.gate_exp, 4)
                    link(dve.scalar_tensor_tensor(out=gt[:, 6, :], in0=gt[:, 6, :], scalar=0.0, in1=gt[:, 5, :],
                                                  op0=ALU.max, op1=ALU.add))
                    dve.scalar_tensor_tensor(out=v8(g[:, :]), in0=v8(gt[:, 6, :]), scalar=-1.0,
                                             in1=gt[:, 4, 0:8].unsqueeze(1).broadcast_to([P, TT, 8]),
                                             op0=ALU.mult, op1=ALU.mult).then_inc(s.gate_done, 1)
                if w == 7:
                    dve.wait_ge(s.head_sums, 4)
                    link(dve.tensor_scalar(hs[:, 0, :], STAT[:, 64:96], EPS, None, ALU.add))
                    dve.reciprocal(hs[:, 1, :], hs[:, 0, :]).then_inc(s.head_inv, 1)
                if w == 8:
                    hsv = hs[:, 2, :].rearrange("p (t c) -> p t c", t=TT)
                    dve.wait_ge(s.head_rms, 1)
                    dve.tensor_tensor(v8(coefk[:, :]), v8(beta[:, :]), hsv[:, :, 0:8], ALU.mult).then_inc(s.coef_ready, 1)
                    dve.tensor_scalar(v8(coefq[:, :]), hsv[:, :, 8:16], HD ** -0.5, None, ALU.mult).then_inc(s.coef_ready, 1)
                    dve.wait_ge(s.decay_act, 1)
                    link(dve.tensor_tensor(kds[:, 1, :], kds[:, 1, :], hsv[:, 0, 0:8], ALU.mult))
            modulation(2)

            def big_read(name, ins):
                assert ("dve" == BIG_LIST[BIG_INDEX[name]][1])
                ins.then_inc(s.big_read_dve, 1)

            def wait_big(name):
                dve.wait_ge(s.big_ready, BIG_INDEX[name] + 1)

            two = lambda b: b[:, :].rearrange("p (a b) -> p a b", a=2)
            for i, name in enumerate(("kb01", "kb23")):
                wait_big(name)
                big_read(name, dve.tensor_tensor(kbT[:, 2 * i:2 * i + 2, :], kT[:, 2 * i:2 * i + 2, :], two(big(name)), ALU.mult))
            for i, name in enumerate(("q01", "q23")):
                wait_big(name)
                big_read(name, dve.tensor_tensor(qT[:, 2 * i:2 * i + 2, :], qT[:, 2 * i:2 * i + 2, :], two(big(name)), ALU.mult))
            dve.wait_ge(s.big_read_act, big_reads(BIG_INDEX["eg"], "act"))
            dve.wait_ge(s.big_read_dve, 4)
            dve.tensor_tensor(kbgT[:, :, :], kbT[:, :, P:T], eg, ALU.mult).then_inc(s.row_scaled, 1)
            dve.tensor_tensor(qdT[:, :, :], qT[:, :, P:T], eg, ALU.mult).then_inc(s.row_scaled, 1)
            for t in range(TT):
                wait_big(f"v{t}")
                big_read(f"v{t}", dve.tensor_tensor(
                    vb[:, t, :].rearrange("p (h e) -> p h e", h=8), big(f"v{t}")[:, :].rearrange("p (h e) -> p h e", h=8),
                    beta[:, 8 * t:8 * t + 8].unsqueeze(2).broadcast_to([P, 8, HD]), ALU.mult))
            wait_big("kt")
            big_read("kt", dve.tensor_tensor(
                kd[:, :].rearrange("p (h e) -> p h e", h=8), big("kt")[:, :].rearrange("p (h e) -> p h e", h=8),
                kds[:, 1, :].unsqueeze(2).broadcast_to([P, 8, HD]), ALU.mult))
            dve.wait_ge(s.head_sums, 7)
            link(dve.tensor_scalar(ss[:, 0, :], STAT[:, 96:116], 1.0 / HD, EPS, ALU.mult, ALU.add))
            dve.reciprocal(ss[:, 1, :], ss[:, 0, :]).then_inc(s.head_inv, 1)
            lo(13)
            wait_big("sk")
            dve.wait_ge(s.proj_evac, 3)
            big_read("sk", dve.scalar_tensor_tensor(out=ks[:, :], in0=ks[:, :], scalar=vecs("kn_w"), in1=big("sk")[:, 0:256],
                                                    op0=ALU.mult, op1=ALU.mult))
            for i, name in enumerate(("sq01", "sq23")):
                wait_big(name)
                big_read(name, dve.scalar_tensor_tensor(out=qs[:, 2 * i:2 * i + 2, :], in0=qs[:, 2 * i:2 * i + 2, :],
                                                        scalar=qk_w[:, :], in1=two(big(name)), op0=ALU.mult, op1=ALU.mult))

            def softmax_max(a, bank, sc):
                for hh in range(4):
                    dve.wait_ge(s.scores_ready, 4 * a + hh + 1)
                    if a < 2:
                        head = 2 * a + hh // 2 + 4 * (hh % 2)
                        ins = dve.scalar_tensor_tensor(out=sc[:, hh, :], in0=const("alibi"), scalar=2.0 ** -(head + 1),
                                                       in1=bank[hh][:, 0:384], op0=ALU.mult, op1=ALU.add)
                    else:
                        ins = dve.tensor_tensor(sc[:, hh, :], t5[:, 4 * (a - 2) + hh, :], bank[hh][:, 0:384], ALU.add)
                    ins.then_inc(s.scores_biased, 1)
                    dve.wait_ge(s.scores_biased, 4 * a + hh + 1)
                    for part, (c0, c1) in enumerate(((0, 256), (256, 384))):
                        link(dve.tensor_reduce(soft[:, 0, 2 * hh + part:2 * hh + part + 1], sc[:, hh, c0:c1], AX.X, ALU.max))
                if a < 2:
                    sk = sink2[:, 4 * a:4 * a + 4, :].rearrange("p h t -> p (h t)")
                    link(dve.tensor_tensor(soft[:, 0, :], soft[:, 0, :], sk, ALU.max))
                    link(dve.tensor_tensor(soft[:, 3, :], sk, soft[:, 0, :], ALU.subtract))
                dve.tensor_scalar(soft[:, 1, :], soft[:, 0, :], -1.0, None, ALU.mult).then_inc(s.negmax_ready, 1)

            def softmax_div(a, sc):
                dve.wait_ge(s.exp_ready, 8 * (a + 1) + min(a + 1, 2))
                if a < 2:
                    link(dve.tensor_tensor(soft[:, 4, :], soft[:, 2, :], soft[:, 3, :], ALU.add))
                    link(dve.reciprocal(soft[:, 5, :], soft[:, 4, :]))
                else:
                    link(dve.reciprocal(soft[:, 5, :], soft[:, 2, :]))
                for hh in range(4):
                    for part, (c0, c1) in enumerate(((0, 256), (256, 384))):
                        dve.tensor_scalar(sc[:, hh, c0:c1], sc[:, hh, c0:c1], soft[:, 5, 2 * hh + part:2 * hh + part + 1],
                                          None, ALU.mult).then_inc(s.probs_ready, 1)

            def pv_low(a, bank, dst, high):
                dve.wait_ge(s.pv_hi, a + 1)
                dve.tensor_tensor(dst, bank[0].rearrange("p (a b) -> p a b", a=2), high, ALU.subtract).then_inc(s.pv_lo, 1)

            softmax_max(0, A, sc1)
            for gi in range(4):
                t, par = gi // 2, gi % 2
                Gcol = Gs[:, :].rearrange("p (t i two) -> p t i two", t=TT, two=2)[:, t, :, par]
                wait_big(f"G{gi}")
                four = lambda b: b.rearrange("p (i c) -> p i c", i=4)
                ins = dve.tensor_tensor(four(DT[:, gi, :]), four(big(f"G{gi}")[:, :]), Gcol.unsqueeze(2).broadcast_to([P, 4, P]), ALU.subtract)
                big_read(f"G{gi}", ins)
                dve.wait_ge(s.big_read_dve, big_reads(BIG_INDEX[f"G{gi}"], "dve"))
                dve.tensor_tensor(four(DT[:, gi, :]), four(DT[:, gi, :]), future.unsqueeze(1).broadcast_to([P, 4, P]),
                                  ALU.add).then_inc(s.d_shifted, 1)
            for gi in range(4):
                t, par = gi // 2, gi % 2
                rk = hs[:, 2, 16 * t:16 * t + 8].rearrange("p (i two) -> p i two", two=2)[:, :, par]
                dve.wait_ge(s.d_ready, gi + 1)
                link(dve.tensor_tensor(four(DT[:, gi, :]), four(DT[:, gi, :]), rk.unsqueeze(2).broadcast_to([P, 4, P]), ALU.mult))
            for gi in range(4):
                wait_big(f"kk{gi}")
                if gi == 0:
                    dve.wait_ge(s.big_read_dve, big_reads(BIG_INDEX["G3"], "dve"))
                ins = dve.tensor_tensor(AT[:, gi, :], big(f"kk{gi}")[:, :], DT[:, gi, :], ALU.mult)
                big_read(f"kk{gi}", ins)
                dve.wait_ge(s.big_read_dve, big_reads(BIG_INDEX[f"kk{gi}"], "dve"))
                dve.tensor_tensor(four(XT[:, gi, :]), four(AT[:, gi, :]), level_mask[0].unsqueeze(1).broadcast_to([P, 4, P]),
                                  ALU.mult).then_inc(s.at_ready, 1)
                dve.wait_ge(s.at_ready, gi + 1)
                dve.tensor_tensor(four(XT[:, gi, :]), ident.unsqueeze(1).broadcast_to([P, 4, P]), four(XT[:, gi, :]),
                                  ALU.subtract).then_inc(s.xt_ready, 1)
            for gi in range(4):
                wait_big(f"qk{gi}")
                ins = dve.tensor_tensor(qkT[:, gi, :], big(f"qk{gi}")[:, :], DT[:, gi, :], ALU.mult)
                big_read(f"qk{gi}", ins)
            softmax_div(0, sc1)
            pv_low(0, A, h_lo[:, 4:6, :], h_hi[:, 4:6, :])
            for l in range(1, NEXP + 1):
                for gi in range(4):
                    dve.wait_ge(s.qt_ready, 4 * (l - 1) + gi + 1)
                    dve.wait_ge(s.xt_ready, 4 * (l - 1) + gi + 1)
                    dve.tensor_tensor(XT[:, gi, :], XT[:, gi, :], B[gi][:, :], ALU.subtract).then_inc(s.xt_ready, 1)
                if l == 1:
                    softmax_max(1, A, sc1)
                if l == 2:
                    softmax_div(1, sc1)
                if l == 4:
                    pv_low(1, A, h_lo[:, 6:8, :], h_hi[:, 6:8, :])
            dve.wait_ge(s.s_ready, 1)
            dve.tensor_copy(S1, B[1][:, 0:256]).then_inc(s.s_copied, 1)
            lo(14)
            dve.wait_ge(s.r_ready, 1)
            v4 = lambda ap, par: ap.rearrange("p (i two e) -> p i two e", two=2, e=HD)[:, :, par, :]
            for par in range(2):
                dve.tensor_tensor(v4(r1, par), v4(vb[:, 1, :], par), B[par][:, 0:256].rearrange("p (i e) -> p i e", e=HD),
                                  ALU.subtract).then_inc(s.r_done, 1)
            dve.wait_ge(s.o_sums, 1)
            link(dve.tensor_scalar(os_[:, 0, :], B[2][:, 0:16], 1.0 / HD, EPS, ALU.mult, ALU.add))
            dve.reciprocal(os_[:, 1, :], os_[:, 0, :]).then_inc(s.o_inv, 1)
            for i in range(2):
                dve.wait_ge(s.o_rows, i + 1)
                o = oT[:, 2 * i:2 * i + 2, :]
                link(dve.scalar_tensor_tensor(out=o, in0=o, scalar=vecs("gdn_w"), in1=two(B[i]), op0=ALU.mult, op1=ALU.mult))
                dve.tensor_tensor(o, o, zT[:, 2 * i:2 * i + 2, :], ALU.mult).then_inc(s.o_gated, 1)
            for i in range(2):
                dve.wait_ge(s.o_hi_done, i + 1)
                dve.tensor_tensor(h_lo[:, 2 * i:2 * i + 2, :], oT[:, 2 * i:2 * i + 2, :], h_hi[:, 2 * i:2 * i + 2, :],
                                  ALU.subtract).then_inc(s.o_lo_done, 1)
            lo(15)
            lo(16)
            residual(0, 14)

            def norm(n):
                inverse_mean(n)
                h_parts(n)

            def ffn(f):
                F = FFN_BASE[f]

                def product(j, used):
                    dve.wait_ge(s.silu_ready, j + (JF * f + 1))
                    dve.wait_ge(s.block_used, used)
                    if not (isinstance(j, int) and f + j == 0):
                        dve.wait_ge(s.hid_lo_ready, j + JF * f)
                    dve.tensor_tensor(hid[:, :], sg[:, :], B[1][:, :], ALU.mult).then_inc(s.hid_ready, 1)

                def hid_low(j):
                    dve.wait_ge(s.hid_hi_ready, j + (JF * f + 1))
                    dve.tensor_tensor(hid_lo[:, :, :].rearrange("p a b -> p (a b)"), hid[:, :],
                                      hid_hi[:, :, :].rearrange("p a b -> p (a b)"), ALU.subtract).then_inc(s.hid_lo_ready, 1)

                norm(2 * f + 1)
                lo(F + 2)
                lo(F + 3)
                product(0, F + 2)
                hid_low(0)

                def body(j, it):
                    lo(F + 4, it)
                    lo(F + 5, it)
                    product(j, it * RING + (F + 4))
                    if f < 2 or not isinstance(j, int):
                        lo(F + 6, it)
                    hid_low(j)

                with dve.Fori(1, JF - 1) as j:
                    body(j, j - 1)
                body(JF - 1, JF - 2)
                if f < 2:
                    lo(F + 34)
                residual(2 * f + 1, F + 32)

            ffn(0)
            norm(2)
            dve.wait_ge(s.pool_zeroed, 3)
            for i in range(4):
                w = CONV_BASE + 3 * i
                lo(w + 2)
                lo(w + 3)
                dve.wait_ge(s.c_copied, i + 1)
                dve.wait_ge(s.block_used, w + 3)
                cu_in = cu[:, :, 2:T + 2]
                dve.tensor_tensor(cu_in, c_sb[:, :].rearrange("p (a b) -> p a b", a=2), two(B[2]), ALU.mult).then_inc(s.cu_ready, 1)
                dve.wait_ge(s.cu_ready, i + 1)
                for tap in range(3):
                    for mt in range(2):
                        ck = V_AT["conv_k"][0] + 3 * (2 * i + mt) + tap
                        if tap == 0:
                            if i:
                                dve.wait_ge(s.by_hi, i)
                            link(dve.tensor_scalar(yb[:, mt, :], cu[:, mt, 0:T], vec[:, ck:ck + 1], None, ALU.mult))
                        else:
                            link(dve.scalar_tensor_tensor(out=yb[:, mt, :], in0=cu[:, mt, tap:tap + T], scalar=vec[:, ck:ck + 1],
                                                          in1=yb[:, mt, :], op0=ALU.mult, op1=ALU.add))
                dve.tensor_tensor(yb[:, :, :], yb[:, :, :], two(B[0]), ALU.mult).then_inc(s.by_ready, 1)
                lo(w + 4)
                dve.wait_ge(s.by_hi, i + 1)
                dve.tensor_tensor(o_lo[:, 2 * i:2 * i + 2, :], yb[:, :, :], o_hi[:, 2 * i:2 * i + 2, :], ALU.subtract).then_inc(s.by_lo, 1)
            for w in range(CONV_OUT + 2, CONV_OUT + 6):
                lo(w)
            residual(2, CONV_OUT + 3)
            ffn(1)
            norm(4)
            dve.wait_ge(s.tables_loaded, 32)
            for i in range(5):
                w, a = QKV_BASE + 3 * i, i + 1
                if i < 4:
                    lo(w + 2)
                if i:
                    softmax_max(a, B, sc2)
                if i < 4:
                    lo(w + 3)
                if i:
                    softmax_div(a, sc2)
                if i < 4:
                    lo(w + 4)
                if i:
                    pv_low(a, B, o_lo[:, 2 * i - 2:2 * i, :], o_hi[:, 2 * i - 2:2 * i, :])
            for w in range(ATT_OUT + 2, ATT_OUT + 6):
                lo(w)
            residual(4, ATT_OUT + 3)
            ffn(2)
            inverse_mean(6)
            h_parts(6)

        @block.tensor
        def _(pe):
            def mm(o, l, r, start, stop):
                return pe.matmul(o, l, r, start=start, stop=stop, skip_group_check=True)

            def three(o, wh, wl, xh, xl, first, last):
                mm(o, wh, xh, first, False)
                mm(o, wh, xl, False, False)
                return mm(o, wl, xh, False, last)

            def column_block(w, bank, it=0, n=None):
                pe.wait_ge(s.lo_ready, it * RING + (w + 1))
                wh = w_hi[:, w % RING, :].rearrange("p (k c) -> p k c", k=KD)
                wl = w_lo[:, w % RING, :].rearrange("p (k c) -> p k c", k=KD)
                order = [(k, mt) for k in range(KD) for mt in range(2)] if n is not None else \
                    [(k, mt) for mt in range(2) for k in range(KD)]
                for k, mt in order:
                    if n is not None and mt == 0:
                        pe.wait_ge(s.h_lo_ready, 8 * n + k + 1)
                    c = slice(P * mt, P * mt + P)
                    ins = three(bank[:, 256 * mt:256 * mt + 256], wh[:, k, c], wl[:, k, c], h_hi[:, k, :], h_lo[:, k, :],
                                k == 0 and mt == 0, k == KD - 1)
                ins.then_inc(s.block_used, 1)

            def row_block(w, oh_, ol_, k0, it=0, first=False, done=None):
                pe.wait_ge(s.lo_ready, it * RING + (w + 1))
                wh = w_hi[:, w % RING, :].rearrange("p (k c) -> p k c", k=2)
                wl = w_lo[:, w % RING, :].rearrange("p (k c) -> p k c", k=2)
                for m in range(KD):
                    for k in range(2):
                        ins = three(acc[:, 256 * m:256 * m + 256], wh[:, k, P * m:P * m + P], wl[:, k, P * m:P * m + P],
                                    oh_[:, k0 + k, :], ol_[:, k0 + k, :], first and k == 0 and m % 2 == 0, False)
                    if done and m % 2 and m < KD - 1:
                        ins.then_inc(s.acc_tile_done, 1)
                ins.then_inc(s.block_used, 1)

            def norm(n):
                for m in range(KD):
                    pe.wait_ge(s.squared, 8 * n + m + 1)
                    for t in range(TT):
                        ins = mm(B[3][:, t:t + 1], nt[:, m, P * t:P * t + P], ones, m == 0 and t == 0, m == KD - 1)
                ins.then_inc(s.sumsq_ready, 1)
                pe.wait_ge(s.rms_ready, n + 1)
                for t in range(TT):
                    ins = mm(B[3][:, 256 + P * t:256 + P * t + P], rms[:, t:t + 1].broadcast_to([P, P]), ident, True, True)
                ins.then_inc(s.rstd_ready, 1)

            pe.wait_ge(s.t5_loaded, 48)
            mm(A[0][0:16, 0:384], rb[:, :], oh, True, True).then_inc(s.t5_psum, 1)
            pe.wait_ge(s.consts_loaded, 16)
            norm(0)

            def modulation(part):
                pe.wait_ge(s.mod_accumulated, MOD_BLOCKS * (part + 1))
                if part:
                    pe.wait_ge(s.mod_ready, 1)
                for j in range(16):
                    ins = mm(STAT[:, 480 + j:481 + j], mod_acc[:, P * j:P * j + P], ones, True, True)
                ins.then_inc(s.mod_summed, 1)

            modulation(0)
            pe.wait_ge(s.t5_row, 1)

            def head_sums(src, tiles, col, width):
                for t in range(TT):
                    for i in range(tiles):
                        o = STAT[:, col + t * width + 2 * i:col + t * width + 2 * i + 2]
                        ins = mm(o, src(i, t), headsel, True, True)
                return ins

            def wait_bank(w):
                v = w - 4
                if 0 <= v < 6:
                    pe.wait_ge(s.pad_ready, v + 1)
                elif v >= 6:
                    pe.wait_ge(s.proj_evac, v - 5)

            def squares_of(w):
                pe.wait_ge(s.head_squared, w + 1)
                if w == 0:
                    pe.wait_ge(s.gate_dve, 1)
                if w == 2:
                    pe.wait_ge(s.decay_dve, 1)
                head_sums(lambda i, t: sqb[:, 256 * i + P * t:256 * i + P * t + P], 2, 64 + 4 * w, 16).then_inc(s.head_sums, 1)

            for w in range(10):
                wait_bank(w)
                column_block(w, A[w % 4], n=0 if w == 0 else None)
                if w == 0:
                    pe.wait_ge(s.gab_lo, 1)
                    for t in range(TT):
                        for k in range(KD):
                            tok = slice(P * t, P * t + P)
                            a, b = gab_wh[:, 16 * k:16 * k + 16], gab_wl[:, 16 * k:16 * k + 16]
                            ins = three(STAT[:, 16 * t:16 * t + 16], h_hi[:, k, tok], h_lo[:, k, tok], a, b,
                                        k == 0 and t == 0, k == KD - 1)
                    ins.then_inc(s.gab_ready, 1)
                if 2 <= w < 6:
                    squares_of(w - 2)
                if w == 3:
                    pe.wait_ge(s.gate_done, 1)
                    for t in range(TT):
                        mm(STAT[:, 32 + 8 * t:40 + 8 * t], tri, g[:, 8 * t:8 * t + 8], True, True)
                    mm(STAT[:, 48:56], ones.broadcast_to([P, P]), g[:, 0:8], True, True).then_inc(s.cum_ready, 1)
                if w == 3:
                    modulation(1)
            wait_bank(10)
            pe.wait_ge(s.lo_ready, 11)
            wh = w_hi[:, 10 % RING, :].rearrange("p (k c) -> p k c", k=KD)
            wl = w_lo[:, 10 % RING, :].rearrange("p (k c) -> p k c", k=KD)
            for k in range(KD):
                three(A[2][:, 0:256], wh[:, k, 0:P], wl[:, k, 0:P], h_hi[:, k, :], h_lo[:, k, :], k == 0, k == KD - 1)
            for t in range(TT):
                tok = slice(P * t, P * t + P)
                for k in range(KD):
                    ins = three(A[2][:, 256 + P * t:256 + P * t + P], h_hi[:, k, tok], h_lo[:, k, tok],
                                wh[:, k, P:2 * P], wl[:, k, P:2 * P], False, k == KD - 1)
            ins.then_inc(s.block_used, 1)

            def before(name):
                u = BIG_INDEX[name] - 3
                if u >= 0:
                    who = BIG_LIST[u][1]
                    pe.wait_ge(s.big_read_dve if who == "dve" else s.big_read_act, big_reads(u, who))

            def filled(name, ins):
                ins.then_inc(s.big_ready, 1)

            def rows(name, coef, tiles, heads=None, rhs=ident, tts=range(TT), width=T):
                before(name)
                for i, tile in enumerate(tiles):
                    for par in range(2):
                        for n, t in enumerate(tts):
                            col = coef(2 * tile + par, t)
                            ins = mm(big(name)[64 * par:64 * par + 64, width * i + P * n:width * i + P * n + P],
                                     col.broadcast_to([P, HD]), rhs, True, True)
                filled(name, ins)

            for w in (8, 9):
                pe.wait_ge(s.head_squared, w - 3)
                pe.wait_ge(s.head_inv, 1)
                head_sums(lambda i, t: sqb[:, 256 * i + P * t:256 * i + P * t + P], 2, 96 + 4 * (w - 8), 10).then_inc(s.head_sums, 1)
            modulation(2)
            pe.wait_ge(s.coef_ready, 2)
            at = lambda c: (lambda h, t: c[:, 8 * t + h:8 * t + h + 1])
            rows("kb01", at(coefk), (0, 1))
            rows("kb23", at(coefk), (2, 3))
            rows("q01", at(coefq), (0, 1))
            rows("q23", at(coefq), (2, 3))
            rows("eg", at(g), range(4), rhs=tri, tts=(1,), width=P)
            pe.wait_ge(s.feature_ready, 6)
            for t in range(TT):
                before(f"v{t}")
                for i in range(4):
                    ins = pe.transpose(big(f"v{t}")[:, P * i:P * i + P], vT[:, i, P * t:P * t + P], ident)
                filled(f"v{t}", ins)
            before("kt")
            for i in range(4):
                ins = pe.transpose(big("kt")[:, P * i:P * i + P], kT[:, i, 0:P], ident)
            filled("kt", ins)
            pe.wait_ge(s.head_squared, 7)
            pe.wait_ge(s.mod_ready, 2)
            head_sums(lambda i, t: sqb[:, P * t:P * t + P], 1, 104, 10).then_inc(s.head_sums, 1)
            pe.wait_ge(s.head_rms, 2)
            sat = lambda h, t: ss[:, 2, 10 * t + h:10 * t + h + 1]
            rows("sk", sat, (4,))
            rows("sq01", sat, (0, 1))
            rows("sq23", sat, (2, 3))

            def scores(a, bank, q, k):
                for hh in range(4):
                    r = slice(64 * (hh % 2), 64 * (hh % 2) + 64)
                    if a > 0:
                        pe.wait_ge(s.ptrans_copied, 4 * a - 4 + hh + 1)
                        if hh == 0:
                            pe.wait_ge(s.pv_lo, a)
                    mm(bank[hh][:, 0:256], q(hh // 2)[r, P:T], k(hh // 2)[r, 0:T], True, True)
                    mm(bank[hh][:, 256:384], q(hh // 2)[r, 0:P], k(hh // 2)[r, 0:P], True, True).then_inc(s.scores_ready, 1)

            def transposes(a, bank, sc, perm):
                for hh in range(4):
                    pe.wait_ge(s.probs_ready, 8 * a + 2 * hh + 2)
                    for i in range(3):
                        ins = pe.transpose(bank[hh][:, P * i:P * i + P], sc[:, hh, P * i:P * i + P], perm)
                    ins.then_inc(s.ptrans_ready, 1)

            def values(a, bank, pT, v):
                for hh in range(4):
                    pe.wait_ge(s.ptrans_copied, 4 * a + hh + 1)
                    o = bank[0][64 * (hh % 2):64 * (hh % 2) + 64, 256 * (hh // 2):256 * (hh // 2) + 256]
                    mm(o[:, 0:P], v(0, hh), pT[:, hh, 256:384], True, True)
                    mm(o[:, P:T], v(0, hh), pT[:, hh, 0:P], True, False)
                    ins = mm(o[:, P:T], v(1, hh), pT[:, hh, P:2 * P], False, True)
                ins.then_inc(s.pv_ready, 1)

            swa_q = lambda a: (lambda i: qs[:, 2 * a + i, :])
            swa_k = lambda i: ks[:, :]
            swa_v = lambda t, hh: vs[:, t, 64 * (hh % 2):64 * (hh % 2) + 64]
            pe.wait_ge(s.big_read_dve, big_reads(BIG_INDEX["sq23"], "dve"))
            pe.wait_ge(s.proj_evac, 4)
            scores(0, A, swa_q(0), swa_k)

            for gi in range(4):
                t, par = gi // 2, gi % 2
                before(f"G{gi}")
                for i in range(4):
                    h = 2 * i + par
                    ins = mm(big(f"G{gi}")[:, P * i:P * i + P], g[:, 8 * t + h:8 * t + h + 1].broadcast_to([P, P]), tri, True, True)
                filled(f"G{gi}", ins)
            for kind, m in (("kk", kbT), ("qk", qT)):
                for gi in range(4):
                    t, par = gi // 2, gi % 2
                    r = slice(64 * par, 64 * par + 64)
                    before(f"{kind}{gi}")
                    for i in range(4):
                        ins = mm(big(f"{kind}{gi}")[:, P * i:P * i + P], kT[r, i, P * t:P * t + P], m[r, i, P * t:P * t + P], True, True)
                    filled(f"{kind}{gi}", ins)
            for gi in range(4):
                if gi < 3:
                    before(f"tr{gi}")
                else:
                    pe.wait_ge(s.x_copied, 1)
                pe.wait_ge(s.xt_ready, gi + 1)
                for i in range(4):
                    ins = pe.transpose(big(f"tr{gi}")[:, P * i:P * i + P], XT[:, gi, P * i:P * i + P], ident)
                ins.then_inc(s.xtr_ready, 1)
            transposes(0, A, sc1, ident)
            values(0, A, pT1, swa_v)

            for l in range(1, NEXP + 1):
                for gi in range(4):
                    pe.wait_ge(s.b_ready, 4 * (l - 1) + gi + 1)
                    pe.wait_ge(s.x_copied, 4 if l == 1 else 4 * (l - 1) + gi + 1)
                    for i in range(4):
                        c = slice(P * i, P * i + P)
                        ins = mm(B[gi][:, c], Bm[:, gi, c], X[:, gi, c], True, True)
                    ins.then_inc(s.p_ready, 1)
                for gi in range(4):
                    pe.wait_ge(s.p_copied, 4 * (l - 1) + gi + 1)
                    for i in range(4):
                        c = slice(P * i, P * i + P)
                        ins = mm(B[gi][:, c], Pm[:, gi, c], XT[:, gi, c], True, True)
                    ins.then_inc(s.qt_ready, 1)
                if l < NEXP:
                    for gi in range(4):
                        pe.wait_ge(s.xt_ready, 4 * l + gi + 1)
                        for i in range(4):
                            c = slice(P * i, P * i + P)
                            ins = pe.transpose(B[gi][:, c], XT[:, gi, c], ident)
                        ins.then_inc(s.xtr_ready, 1)
                if l == 1:
                    scores(1, A, swa_q(1), swa_k)
                if l == 3:
                    transposes(1, A, sc1, ident)
                if l == 4:
                    values(1, A, pT1, swa_v)
            pe.wait_ge(s.pv_lo, 2)
            row_block(W_OUT, h_hi, h_lo, 4, first=True)
            pe.wait_ge(s.xt_ready, 4 * (NEXP + 1))
            pe.wait_ge(s.big_read_dve, big_reads(BIG_INDEX["kt"], "dve"))
            inv_of = lambda h, t: XT[:, 2 * t + h % 2, P * (h // 2):P * (h // 2) + P]
            qk_of = lambda h, t: qkT[:, 2 * t + h % 2, P * (h // 2):P * (h // 2) + P]
            for h in range(8):
                e = slice(HD * h, HD * h + HD)
                ins = mm(B[0][:, e], inv_of(h, 0), vb[:, 0, e], True, True)
            ins.then_inc(s.u_ready, 1)
            row_block(W_OUT + 1, h_hi, h_lo, 6)
            pe.wait_ge(s.u_copied, 1)
            for h in range(8):
                r = slice(64 * (h % 2), 64 * (h % 2) + 64)
                e = slice(HD * h, HD * h + HD)
                ins = mm(B[1][r, HD * (h // 2):HD * (h // 2) + HD], kd[:, e], u0[:, e], True, True)
            ins.then_inc(s.s_ready, 1)
            for h in range(8):
                r = slice(64 * (h % 2), 64 * (h % 2) + 64)
                ins = mm(B[2 + h % 2][r, P * (h // 2):P * (h // 2) + P], u0[:, HD * h:HD * h + HD], qk_of(h, 0), True, True)
            ins.then_inc(s.o0_ready, 1)
            pe.wait_ge(s.s_copied, 1)
            for par in range(2):
                r = slice(64 * par, 64 * par + 64)
                for i in range(4):
                    ins = mm(B[par][:, HD * i:HD * i + HD], kbgT[r, i, :], S1[r, HD * i:HD * i + HD], True, True)
            ins.then_inc(s.r_ready, 1)
            pe.wait_ge(s.r_done, 2)
            for h in range(8):
                e = slice(HD * h, HD * h + HD)
                ins = mm(B[0][:, e], inv_of(h, 1), r1[:, e], True, True)
            ins.then_inc(s.vn_ready, 1)
            pe.wait_ge(s.vn_copied, 1)
            for h in range(8):
                r = slice(64 * (h % 2), 64 * (h % 2) + 64)
                i = h // 2
                o = B[h % 2][r, P * i:P * i + P]
                mm(o, vn[:, HD * h:HD * h + HD], qk_of(h, 1), True, False)
                ins = mm(o, S1[r, HD * i:HD * i + HD], qdT[r, i, :], False, True)
            ins.then_inc(s.o1_ready, 1)
            pe.wait_ge(s.o_squared, 1)
            for t in range(TT):
                for i in range(4):
                    ins = mm(B[2][:, 8 * t + 2 * i:8 * t + 2 * i + 2], osq[:, i, P * t:P * t + P], headsel, True, True)
            ins.then_inc(s.o_sums, 1)
            pe.wait_ge(s.o_rms, 1)
            for j in range(2):
                for i in range(2):
                    for par in range(2):
                        for t in range(TT):
                            h = 2 * (2 * j + i) + par
                            ins = mm(B[j][64 * par:64 * par + 64, T * i + P * t:T * i + P * t + P],
                                     os_[:, 2, 8 * t + h:8 * t + h + 1].broadcast_to([P, HD]), ident, True, True)
                ins.then_inc(s.o_rows, 1)
            pe.wait_ge(s.o_lo_done, 1)
            row_block(W_OUT + 2, h_hi, h_lo, 0)
            pe.wait_ge(s.o_lo_done, 2)
            row_block(W_OUT + 3, h_hi, h_lo, 2, done=True)

            def ffn(f):
                F = FFN_BASE[f]
                norm(2 * f + 1)
                pe.wait_ge(s.pool_zeroed, 1)
                for i in range(4):
                    mm(A[i], zero_r[:, 0:P], zero_r[:, :], True, True)
                column_block(F, B[0], n=2 * f + 1)
                column_block(F + 1, B[1])

                def body(j, it):
                    pe.wait_ge(s.silu_ready, j + JF * f)
                    column_block(F + 2, B[0], it)
                    pe.wait_ge(s.hid_ready, j + JF * f)
                    column_block(F + 3, B[1], it)
                    pe.wait_ge(s.hid_lo_ready, j + JF * f)
                    row_block(F + 4, hid_hi, hid_lo, 0, it)

                with pe.Fori(1, JF - 1) as j:
                    body(j, j - 1)
                body(JF - 1, JF - 2)
                pe.wait_ge(s.hid_lo_ready, JF * f + JF)
                row_block(F + 32, hid_hi, hid_lo, 0, done=True)

            ffn(0)
            norm(2)
            for i in range(4):
                w = CONV_BASE + 3 * i
                if i:
                    pe.wait_ge(s.by_ready, i)
                for j in range(3):
                    column_block(w + j, B[j], n=2 if i + j == 0 else None)
            for i in range(4):
                pe.wait_ge(s.by_lo, i + 1)
                row_block(CONV_OUT + i, o_hi, o_lo, 2 * i, first=i == 0, done=i == 3)
            ffn(1)
            norm(4)
            for i in range(5):
                w, a, b = QKV_BASE + 3 * i, i + 1, (i - 1) % 2
                if i < 4:
                    if i:
                        pe.wait_ge(s.qkv_copied, 3 * i - 2)
                    column_block(w, A[0], n=4 if i == 0 else None)
                if i:
                    pe.wait_ge(s.qkv_copied, 3 * i)
                    scores(a, B, lambda t: q2[:, b, t, :], lambda t: k2[:, b, t, :])
                if i < 4:
                    column_block(w + 1, A[1])
                if i:
                    transposes(a, B, sc2, const("flip"))
                if i < 4:
                    pe.wait_ge(s.lo_ready, w + 3)
                    wh = w_hi[:, (w + 2) % RING, :].rearrange("p (k c) -> p k c", k=KD)
                    wl = w_lo[:, (w + 2) % RING, :].rearrange("p (k c) -> p k c", k=KD)
                    for t in range(TT):
                        tok = slice(P * t, P * t + P)
                        for k in range(KD):
                            ins = three(A[2][:, 256 * t:256 * t + 256], h_hi[:, k, tok], h_lo[:, k, tok], wh[:, k, :], wl[:, k, :],
                                        k == 0 and t == 0, k == KD - 1)
                    ins.then_inc(s.block_used, 1)
                if i:
                    values(a, B, pT2, lambda t, hh: v2[:, b, t, HD * hh:HD * hh + HD])
            pe.wait_ge(s.qkv_copied, 12)
            for i in range(4):
                pe.wait_ge(s.pv_lo, 3 + i)
                row_block(ATT_OUT + i, o_hi, o_lo, 2 * i, first=i == 0, done=i == 3)
            ffn(2)
            norm(6)


def shape_constants():
    c = np.zeros((P, N_CONST), np.float32)
    i, j = np.arange(P)[:, None], np.arange(P)[None, :]
    c[:, slice(*C_AT["ident"])] = i == j
    c[:, slice(*C_AT["flip"])] = i + j == P - 1
    c[:, slice(*C_AT["tri"])] = i <= j
    c[:, slice(*C_AT["future"])] = np.where(j >= i, 0.0, -BIG)
    for l in range(NEXP + 1):
        b = 1 << l
        m = (i // (2 * b) == j // (2 * b)) & ((i // b) % 2 == 0) & ((j // b) % 2 == 1)
        c[:, C_AT["levels"][0] + P * l:C_AT["levels"][0] + P * (l + 1)] = m
    c[:, C_AT["headsel"][0]] = np.arange(P) < 64
    c[:, C_AT["headsel"][0] + 1] = np.arange(P) >= 64
    c[:, C_AT["ones"][0]] = 1.0
    k = np.arange(256)[None, :]
    dist = i + 128 - k
    table = np.where((dist >= 0) & (dist < 128), -dist, -BIG)
    c[:, C_AT["alibi"][0]:C_AT["alibi"][1]] = np.concatenate([table, table[:, 128:]], 1)
    return c


def t5_constants():
    d = 255 - np.arange(384)
    exact = 16
    df = np.maximum(d, 1).astype(np.float32)
    large = exact + (np.log(df / np.float32(exact)) / np.float32(np.log(2048 / exact)) * np.float32(32 - exact)).astype(np.int32)
    bucket = np.where(d < exact, np.maximum(d, 0), np.minimum(large, 31))
    onehot = (np.arange(32)[:, None] == bucket[None, :]).astype(np.float32)
    n = ((d >= 0) & (d <= 128)).astype(int) + ((d >= 0) & (d % 4 == 0)) + ((d >= 0) & (d % 16 == 0))
    log = np.where(n > 0, np.log(np.maximum(n, 1)), -BIG).astype(np.float32)
    return onehot, np.ascontiguousarray(np.broadcast_to(log, (16, 384)))


def lay_out(v):
    def cols(w, at):
        return w[:, at].reshape(KD, P, 256).transpose(1, 0, 2).reshape(P, BLOCK)

    def rows(w, at):
        return w[at].reshape(2, P, D).transpose(1, 0, 2).reshape(P, BLOCK)

    def chunk(a):
        return a.reshape(-1, P).T

    r = np.arange
    w_in, w_out, ada = v["w_in"][0], v["w_out"][0], v["w_ada"][0]
    pair = np.concatenate([np.concatenate([r(64) + 64 * j, r(64) + 64 * (4 + j)]) for j in range(4)])
    starts = [512, 768, 0, 256, 1024, 1280, 1536, 1792]
    w = [cols(w_in, r(a, a + 256)) for a in starts]
    w += [cols(w_in, 2064 + pair[0:256]), cols(w_in, 2064 + pair[256:512]), cols(w_in, r(2576, 2832))]
    w += [rows(w_out, 512 + pair[0:256]), rows(w_out, 512 + pair[256:512]), rows(w_out, r(256)), rows(w_out, r(256, 512))]

    def swiglu(wg, wu, wd):
        out = []
        for j in range(JF + 1):
            if j < JF:
                out += [cols(wg, r(256 * j, 256 * j + 256)), cols(wu, r(256 * j, 256 * j + 256))]
            if j:
                out.append(rows(wd, r(256 * j - 256, 256 * j)))
        return out

    def mixer(w1, w2):
        out = [cols(w1, r(D * j + 256 * i, D * j + 256 * i + 256)) for i in range(4) for j in range(3)]
        return out + [rows(w2, r(256 * i, 256 * i + 256)) for i in range(4)]

    w += swiglu(v["w_gate"][0], v["w_up"][0], v["w_down"][0])
    w += mixer(v["conv_w_in_2"][0], v["conv_w_out_2"][0])
    w += swiglu(v["ffn_w_gate_2"][0], v["ffn_w_up_2"][0], v["ffn_w_down_2"][0])
    w += mixer(v["attn_w_qkv_2"][0], v["attn_w_out_2"][0])
    w += swiglu(v["ffn_w_gate_2"][1], v["ffn_w_up_2"][1], v["ffn_w_down_2"][1])
    assert len(w) == N_WEIGHTS
    stream = [None] * (N_WEIGHTS + MOD_TOTAL)
    for n, b in enumerate(w):
        stream[raw_index(n)] = b
    for m, at in enumerate(RAW_OF_MOD):
        k, part = m % MOD_BLOCKS, m // MOD_BLOCKS
        stream[at] = ada[P * k:P * k + P, BLOCK * part:BLOCK * part + BLOCK]

    vec = np.zeros((P, N_VEC), np.float32)

    def put(name, a):
        vec[:, slice(*V_AT[name])] = a

    put("c", chunk(v["c"][0]))
    for name, a in (("norm1", v["norm1_w"][0]), ("norm2", v["norm2_w"][0]), ("mix0", v["mix_norm_2"][0]),
                    ("mix1", v["mix_norm_2"][1]), ("ffn0", v["ffn_norm_2"][0]), ("ffn1", v["ffn_norm_2"][1]),
                    ("final", v["final_norm_2"]), ("b_ada", v["b_ada"][0])):
        put(name, chunk(a))
    put("conv_w", v["conv_w"][0, :, 0, :].reshape(4, 12, P).transpose(2, 1, 0).reshape(P, 48))
    put("conv_k", v["conv_kernel_2"][0].reshape(3, KD, P).transpose(2, 1, 0).reshape(P, 24))
    for name, a in (("gdn_w", v["gdn_norm_w"][0]), ("qn_w", v["q_norm_w"][0]), ("kn_w", v["k_norm_w"][0])):
        put(name, np.tile(a, 2)[:, None])
    put("dt_bias", v["dt_bias"][0][None, :])
    put("a_log", v["a_log"][0][None, :])
    put("sinks", v["sinks"][0][[2 * a + hh // 2 + 4 * (hh % 2) for a in range(2) for hh in range(4)]][None, :])
    onehot, log = t5_constants()
    return {
        "stream": np.stack(stream),
        "x_in": v["x"][0].T.reshape(KD, P, T).transpose(1, 0, 2),
        "consts_in": shape_constants(),
        "vectors_in": vec,
        "gab_in": w_in[:, 2048:2064].reshape(KD, P, 16).transpose(1, 0, 2).reshape(P, KD * 16),
        "t5_onehot": onehot,
        "t5_log": log,
        "rel_bias": v["rel_bias_2"],
    }


def kernel(**inputs):
    import concourse.bacc as bacc
    from concourse.bass_utils import run_bass_kernel_spmd

    nc = bacc.Bacc("TRN2", target_bir_lowering=False, num_devices=1)
    arrays = {k: np.ascontiguousarray(a) for k, a in lay_out({k: np.asarray(a) for k, a in inputs.items()}).items()}
    args = {k: nc.dram_tensor(k, a.shape, mybir.dt.from_np(a.dtype), kind="ExternalInput").ap() for k, a in arrays.items()}
    out = nc.dram_tensor("out", (P, KD, T), F32, kind="ExternalOutput").ap()
    build(nc, out=out, **args)
    r = run_bass_kernel_spmd(nc, [arrays], core_ids=[0])
    y = r.results[0]["out"]
    return np.ascontiguousarray(y.transpose(1, 0, 2).reshape(D, T).T)[None]
```

```python
from contextlib import ExitStack

import numpy as np
import concourse.bass as bass
from concourse import mybir

F32, F32R = mybir.dt.float32, mybir.dt.float32r
ALU, ACT, AX = mybir.AluOpType, mybir.ActivationFunctionType, mybir.AxisListType

P = 128
T = 256
TT = T // P
D = 1024
KD = D // P
FF = 2816
JF = FF // 256
HD = 64
EPS = 1e-6
BIG = 1e30
BLOCK = 2048
RING = 3
LATE = (2, 3, 4, 5)
NEXP = 6

W_IN, W_OUT = 0, 11
FFN_BASE = [15, 64, 113]
CONV_BASE, CONV_OUT = 48, 60
QKV_BASE, ATT_OUT = 97, 109
N_WEIGHTS = 146
MOD_PARTS, MOD_BLOCKS = 3, 8
MOD_TOTAL = MOD_PARTS * MOD_BLOCKS
LOOP_W = 14

def mod_index(m):
    return m if m < MOD_BLOCKS else m + LOOP_W


def raw_index(w):
    return w + (MOD_BLOCKS if w < LOOP_W else MOD_TOTAL)


CONSTS = dict(ident=P, flip=P, tri=P, future=P, levels=(NEXP + 1) * P, headsel=2, ones=1, alibi=384)
VECS = dict(c=8, norm1=8, norm2=8, mix0=8, mix1=8, ffn0=8, ffn1=8, final=8, b_ada=48, conv_w=48,
            conv_k=24, gdn_w=1, qn_w=1, kn_w=1, dt_bias=8, a_log=8, sinks=8)


def columns(spec):
    out, at = {}, 0
    for name, n in spec.items():
        out[name] = (at, at + n)
        at += n
    return out, at


C_AT, N_CONST = columns(CONSTS)
V_AT, N_VEC = columns(VECS)


BIG_LIST = [(n, "dve") for n in ("kb01", "kb23", "q01", "q23")] + [("eg", "act")] \
    + [(n, "dve") for n in ["v0", "v1", "kt"] + [f"{u}{gi}" for u in ("G", "kk", "qk") for gi in range(4)]
       + ["sk", "sq01", "sq23"]] + [(f"tr{gi}", "act") for gi in range(4)]
BIG_INDEX = {n: i for i, (n, _) in enumerate(BIG_LIST)}


def big_reads(upto, engine):
    return sum(e == engine for _, e in BIG_LIST[:upto + 1])


class Semaphores:

    def __init__(self, new):
        self.x_loaded = new("x_loaded")
        self.vectors_loaded = new("vectors_loaded")
        self.consts_loaded = new("consts_loaded")
        self.gab_loaded = new("gab_loaded")
        self.t5_loaded = new("t5_loaded")
        self.t5_stored = new("t5_stored")
        self.tables_loaded = new("tables_loaded")
        self.out_stored = new("out_stored")
        self.pool_zeroed = new("pool_zeroed")
        self.c_act = new("c_act")
        self.mod_accumulated = new("mod_accumulated")
        self.mod_summed = new("mod_summed")
        self.mod_ready = new("mod_ready")
        self.dve_step = new("dve_step")
        self.act_step = new("act_step")
        self.hi_ready = new("hi_ready")
        self.lo_ready = new("lo_ready")
        self.block_used = new("block_used")
        self.acc_tile_done = new("acc_tile_done")
        self.x_ready = new("x_ready")
        self.squared = new("squared")
        self.sumsq_ready = new("sumsq_ready")
        self.squares_added = new("squares_added")
        self.inv_ready = new("inv_ready")
        self.rms_ready = new("rms_ready")
        self.rstd_ready = new("rstd_ready")
        self.t_ready = new("t_ready")
        self.h_hi_ready = new("h_hi_ready")
        self.h_lo_ready = new("h_lo_ready")
        self.gab_hi = new("gab_hi")
        self.gab_lo = new("gab_lo")
        self.gab_ready = new("gab_ready")
        self.gate_exp = new("gate_exp")
        self.gate_dve = new("gate_dve")
        self.gate_done = new("gate_done")
        self.cum_ready = new("cum_ready")
        self.decay_dve = new("decay_dve")
        self.decay_act = new("decay_act")
        self.proj_evac = new("proj_evac")
        self.pad_ready = new("pad_ready")
        self.conv_done = new("conv_done")
        self.feature_ready = new("feature_ready")
        self.head_squared = new("head_squared")
        self.head_sums = new("head_sums")
        self.head_inv = new("head_inv")
        self.head_rms = new("head_rms")
        self.coef_ready = new("coef_ready")
        self.big_ready = new("big_ready")
        self.big_read_dve = new("big_read_dve")
        self.big_read_act = new("big_read_act")
        self.d_shifted = new("d_shifted")
        self.d_ready = new("d_ready")
        self.d_normed = new("d_normed")
        self.at_ready = new("at_ready")
        self.b_ready = new("b_ready")
        self.xt_ready = new("xt_ready")
        self.x_copied = new("x_copied")
        self.p_ready = new("p_ready")
        self.p_copied = new("p_copied")
        self.qt_ready = new("qt_ready")
        self.xtr_ready = new("xtr_ready")
        self.row_scaled = new("row_scaled")
        self.u_ready = new("u_ready")
        self.u_copied = new("u_copied")
        self.s_ready = new("s_ready")
        self.s_copied = new("s_copied")
        self.o0_ready = new("o0_ready")
        self.o_copied = new("o_copied")
        self.r_ready = new("r_ready")
        self.r_done = new("r_done")
        self.vn_ready = new("vn_ready")
        self.vn_copied = new("vn_copied")
        self.o1_ready = new("o1_ready")
        self.o_squared = new("o_squared")
        self.o_sums = new("o_sums")
        self.o_inv = new("o_inv")
        self.o_rms = new("o_rms")
        self.o_rows = new("o_rows")
        self.o_gated = new("o_gated")
        self.o_hi_done = new("o_hi_done")
        self.o_lo_done = new("o_lo_done")
        self.scores_ready = new("scores_ready")
        self.scores_biased = new("scores_biased")
        self.negmax_ready = new("negmax_ready")
        self.exp_ready = new("exp_ready")
        self.probs_ready = new("probs_ready")
        self.ptrans_ready = new("ptrans_ready")
        self.ptrans_copied = new("ptrans_copied")
        self.pv_ready = new("pv_ready")
        self.pv_hi = new("pv_hi")
        self.pv_lo = new("pv_lo")
        self.silu_ready = new("silu_ready")
        self.hid_ready = new("hid_ready")
        self.hid_hi_ready = new("hid_hi_ready")
        self.hid_lo_ready = new("hid_lo_ready")
        self.cu_ready = new("cu_ready")
        self.by_ready = new("by_ready")
        self.by_hi = new("by_hi")
        self.by_lo = new("by_lo")
        self.row_copied = new("row_copied")
        self.gate_scaled = new("gate_scaled")
        self.gated = new("gated")
        self.qk_scaled = new("qk_scaled")
        self.v_scaled = new("v_scaled")
        self.t5_psum = new("t5_psum")
        self.t5_row = new("t5_row")


def build(nc, stream, x_in, consts_in, vectors_in, gab_in, t5_onehot, t5_log, rel_bias, out):
    t5_scratch = nc.dram_tensor("t5_scratch", (16, 384), F32, kind="Internal")
    with ExitStack() as ctx:
        s = Semaphores(lambda name: ctx.enter_context(nc.semaphore(name)))
        raw_landed = [ctx.enter_context(nc.semaphore(f"raw_landed{i}")) for i in range(RING)]

        def sb(name, shape, dt=F32, stack=ctx):
            return stack.enter_context(nc.sbuf_tensor(name, shape, dt))

        raw = sb("raw", [P, RING, BLOCK])
        w_hi = sb("w_hi", [P, RING, BLOCK], F32R)
        w_lo = sb("w_lo", [P, RING, BLOCK], F32R)
        x = sb("x_res", [P, KD, T])
        nt = sb("norm_tmp", [P, KD, T])
        h_hi = sb("h_hi", [P, KD, T], F32R)
        h_lo = sb("h_lo", [P, KD, T], F32R)
        zero_r = sb("zero_r", [P, 512], F32R)
        consts = sb("consts", [P, N_CONST])
        vec = sb("vec", [P, N_VEC])
        c_act = sb("c_act_sb", [P, 8])
        mods = sb("mods", [P, 48])
        a1 = sb("a1", [P, 8])
        a2 = sb("a2", [P, 8])
        qk_w = sb("qk_w", [P, 1])
        root_tmp = sb("root_tmp", [P, 1])
        rrow = sb("rms_row", [P, T])
        rrow2 = sb("rms_row_squared", [P, T])
        ms = sb("ms", [P, TT])
        inv = sb("inv", [P, TT])
        rms = sb("rms", [P, TT])
        soft = sb("soft", [P, 6, 8])
        sink2 = sb("sink2", [P, 8, 2])

        def const(name):
            a, b = C_AT[name]
            return consts[:, a:b]

        def vecs(name):
            a, b = V_AT[name]
            return vec[:, a:b]

        ident, tri, future, headsel, ones = (const(n) for n in ("ident", "tri", "future", "headsel", "ones"))
        level_mask = [consts[:, C_AT["levels"][0] + P * i:C_AT["levels"][0] + P * (i + 1)] for i in range(NEXP + 1)]

        with ExitStack() as one:
            def p1(name, shape, dt=F32):
                return sb(name, shape, dt, one)
            kqb = p1("keys_queries", [P, 12, T])
            zT = p1("zT", [P, 4, T])
            kbgT, qdT = (p1(n, [P, 4, P]) for n in ("kbgT", "qdT"))
            kd = p1("kd", [P, 512])
            vb = p1("vb", [P, TT, 512])
            AT, X, qkT, XT = (p1(n, [P, 4, 4 * P]) for n in ("AT", "X_inv", "qkT", "XT"))
            inv_b = p1("inv_b", [P, 4 * 4 * P])
            inv_p = p1("inv_p", [P, 4 * 4 * P])
            qs = p1("qs", [P, 4, T])
            ks = p1("ks", [P, T])
            vs = p1("vs", [P, TT, P])
            pT1 = p1("probsT1", [P, 4, 384])
            gab_w = p1("gab_w", [P, KD * 16])
            gab_wh = p1("gab_wh", [P, KD * 16], F32R)
            gab_wl = p1("gab_wl", [P, KD * 16], F32R)
            gt = p1("gate_tmp", [P, 8, TT * 8])
            beta, g, Gs, coefk, coefq = (p1(n, [P, TT * 8]) for n in ("beta", "g", "Gs", "coefk", "coefq"))
            kds = p1("kds", [P, 2, 8])
            hs = p1("head_stat", [P, 3, TT * 16])
            ss = p1("swa_stat", [P, 3, TT * 10])
            os_ = p1("out_stat", [P, 3, TT * 8])
            rb = p1("rel_bias_sb", [32, 16])
            t5r = p1("t5_row_sb", [16, 384])
        sc1 = nt[:, 0:6, :].rearrange("p a b -> p (a b)").rearrange("p (h c) -> p h c", h=4)
        eg = pT1[:, :, :].rearrange("p a b -> p (a b)")[:, 0:512].rearrange("p (a b) -> p a b", a=4)
        oh = XT[0:32, 2, 0:384]
        t5l = XT[0:16, 3, 0:384]
        DT = X
        kT, qT, kbT = kqb[:, 0:4, :], kqb[:, 4:8, :], kqb[:, 8:12, :]
        mod_accs = [inv_b[:, :]] + [kqb[:, 0:8, :].rearrange("p a b -> p (a b)")] * 2
        head_sq = [X[:, w, :] for w in range(4)] + [qkT[:, w, :] for w in range(3)]
        vT = inv_p[:, 0:1024].rearrange("p (a b) -> p a b", a=4)
        pad = inv_p[:, 1024:1024 + 2 * 259].rearrange("p (a b) -> p a b", a=2)
        cacc = XT[:, 0, :]
        u0, vn, r1 = inv_b[:, 0:512], inv_b[:, 512:1024], inv_b[:, 1024:1536]
        S1 = inv_b[:, 1536:1792]
        oT = inv_p[:, 0:1024].rearrange("p (a b) -> p a b", a=4)
        osq = inv_p[:, 1024:2048].rearrange("p (a b) -> p a b", a=4)
        Bm = inv_b[:, :].rearrange("p (g c) -> p g c", g=4)
        Pm = inv_p[:, :].rearrange("p (g c) -> p g c", g=4)

        t5 = sb("t5_tables", [P, 16, 384])
        o_hi = sb("o_hi", [P, KD, T], F32R)
        o_lo = sb("o_lo", [P, KD, T], F32R)
        hid_hi = sb("hid_hi", [P, 2, T], F32R)
        hid_lo = sb("hid_lo", [P, 2, T], F32R)
        sg = sb("silu_gate", [P, 2 * T])
        hid = sb("hid", [P, 2 * T])
        c_sb = sb("c_sb", [P, 2 * T])
        cu = sb("cu_pad", [P, 2, T + 2])
        yb = sb("y_conv", [P, 2, T])
        q2 = sb("q2", [P, 2, 2, T])
        k2 = sb("k2", [P, 2, 2, T])
        v2 = sb("v2", [P, 2, TT, 256])
        sc2 = sb("scores2", [P, 4, 384])
        pT2 = sb("probsT2", [P, 4, 384])

        acc = ctx.enter_context(nc.psum_tensor("acc", [P, 2048], F32))
        A = [acc[:, 512 * i:512 * (i + 1)] for i in range(4)]
        B = [ctx.enter_context(nc.psum_tensor(f"bank{i}", [P, 512], F32)) for i in range(4, 8)]
        STAT = B[2]
        mod_bank = [STAT, A[3], B[2]]
        conv_banks = [A, [b[:, :] for b in B]]
        last_hid = o_hi[:, 0:2, :], o_lo[:, 0:2, :]
        BIGB = [B[0], B[1], B[3]]

        def big(name):
            return BIGB[BIG_INDEX[name] % 3]

        norm_scale = [a1[:, :], a2[:, :], vecs("mix0"), vecs("ffn0"), vecs("mix1"), vecs("ffn1"), vecs("final")]
        norm_shift = [mods[:, 0:8], mods[:, 24:32], None, None, None, None, None]
        gates = [mods[:, 16:24], mods[:, 40:48], None, None, None, None]

        block = ctx.enter_context(nc.Block())

        @block.sync
        def _(sp):
            order = {}
            for w in range(LOOP_W):
                order[raw_index(w)] = ("w", w)
            for m in range(MOD_TOTAL):
                order[mod_index(m)] = ("mod", m)
            r0 = LOOP_W + MOD_TOTAL
            for r in range(r0 + RING):
                if r >= RING:
                    kind, n = order[r - RING]
                    sp.wait_ge(s.lo_ready if kind == "w" else s.mod_accumulated, n + 1)
                sp.dma_start(raw[:, r % RING, :], stream[r]).then_inc(raw_landed[r % RING], 16)
            with sp.Fori(1, (N_WEIGHTS - LOOP_W) // RING) as it:
                for i in range(RING):
                    r = r0 + i
                    sp.wait_ge(s.lo_ready, it * RING + (LOOP_W + i - RING + 1))
                    sp.dma_start(raw[:, r % RING, :], stream[it * RING + r]).then_inc(raw_landed[r % RING], 16)
            for m in range(2):
                sp.wait_ge(s.t_ready, 8 * 2 + 4 * (m + 1))
                sp.dma_start(out[:, 4 * m:4 * m + 4, :], nt[:, 4 * m:4 * m + 4, :]).then_inc(s.out_stored, 16)
            sp.wait_ge(s.out_stored, 32)

        @block.gpsimd
        def _(pool):
            pool.memset(zero_r[:, :].bitcast(F32), 0.0).then_inc(s.pool_zeroed, 1)
            pool.memset(pad[:, :, 0:3], 0.0).then_inc(s.pool_zeroed, 1)
            pool.wait_ge(s.t5_row, 1)
            pool.dma_start(t5_scratch.ap(), t5r[:, :]).then_inc(s.t5_stored, 16)
            for l in range(1, NEXP + 1):
                for gi in range(4):
                    if l == 1:
                        pool.wait_ge(s.at_ready, gi + 1)
                        pool.wait_ge(s.mod_summed, 1)
                    else:
                        pool.wait_ge(s.p_ready, 4 * (l - 2) + gi + 1)
                    pool.tensor_tensor(
                        Bm[:, gi, :].rearrange("p (i c) -> p i c", i=4),
                        AT[:, gi, :].rearrange("p (i c) -> p i c", i=4),
                        level_mask[l].unsqueeze(1).broadcast_to([P, 4, P]), ALU.mult).then_inc(s.b_ready, 1)
            pool.wait_ge(s.t5_stored, 16)
            pool.wait_ge(s.x_ready, 8)
            pool.dma_start(t5[:, :, 0:256], bass.AP(t5_scratch, 0, [[1, P], [384, 16], [1, 256]])).then_inc(s.tables_loaded, 16)
            pool.dma_start(t5[:, :, 256:384], bass.AP(t5_scratch, 128, [[1, P], [384, 16], [1, 128]])).then_inc(s.tables_loaded, 16)
            pool.memset(cu[:, :, 0:2], 0.0).then_inc(s.pool_zeroed, 1)
            pool.wait_ge(s.tables_loaded, 32)
            for i, n in enumerate(LATE):
                acc2, to = nt[:, 0:2, :], nt[:, 0:1, :]
                for j, (a, b, dst, ready) in enumerate(((nt[:, 0:2, :], nt[:, 2:4, :], acc2, 4), (acc2, nt[:, 4:6, :], acc2, 6),
                                                        (acc2, nt[:, 6:8, :], acc2, 8), (nt[:, 0:1, :], nt[:, 1:2, :], to, 8))):
                    pool.wait_ge(s.squared, 8 * n + ready)
                    if j:
                        pool.wait_ge(s.squares_added, 4 * i + j)
                    pool.tensor_tensor(dst, a, b, ALU.add).then_inc(s.squares_added, 1)

        @block.scalar
        def _(act):
            steps = [0]

            def link(ins):
                steps[0] += 1
                ins.then_inc(s.act_step, 1)
                act.wait_ge(s.act_step, steps[0])

            act.dma_start(vec[:, :], vectors_in).then_inc(s.vectors_loaded, 16)
            act.dma_start(x[:, :, :], x_in).then_inc(s.x_loaded, 16)
            act.dma_start(consts[:, :], consts_in).then_inc(s.consts_loaded, 16)
            act.dma_start(gab_w[:, :], gab_in).then_inc(s.gab_loaded, 16)
            act.dma_start(oh, t5_onehot).then_inc(s.t5_loaded, 16)
            act.dma_start(rb[:, :], rel_bias).then_inc(s.t5_loaded, 16)
            act.dma_start(t5l, t5_log).then_inc(s.t5_loaded, 16)

            def hi(w, it=0):
                r = raw_index(w)
                act.wait_ge(raw_landed[r % RING], (it + (r // RING + 1)) * 16)
                if not isinstance(it, int) or w + RING * it >= RING:
                    act.wait_ge(s.block_used, it * RING + (w - RING + 1))
                act.activation(w_hi[:, w % RING, :], raw[:, r % RING, :], ACT.Copy).then_inc(s.hi_ready, 1)

            def squares(n):
                link(act.activation(root_tmp[:, :], ones, ACT.Sqrt))
                for m in range(KD):
                    if n:
                        act.wait_ge(s.x_ready, 8 * (n - 1) + m + 1)
                    act.activation(nt[:, m, :], x[:, m, :], ACT.Square).then_inc(s.squared, 1)

            def root(n):
                act.wait_ge(s.inv_ready, n + 1)
                act.activation(rms[:, :], inv[:, :], ACT.Sqrt).then_inc(s.rms_ready, 1)
                if n in LATE:
                    act.wait_ge(s.rstd_ready, n + 1)
                    act.activation(rrow[:, :], B[3][:, 256:512], ACT.Copy).then_inc(s.row_copied, 1)

            def squares_and_high(n, w):
                link(act.activation(root_tmp[:, :], ones, ACT.Sqrt))
                hi(w)
                for m in range(KD):
                    act.wait_ge(s.x_ready, 8 * (n - 1) + m + 1)
                    act.activation(h_hi[:, m, :], x[:, m, :], ACT.Identity, scale=norm_scale[n][:, m:m + 1]).then_inc(s.h_hi_ready, 1)
                    act.activation(nt[:, m, :], x[:, m, :], ACT.Square).then_inc(s.squared, 1)

            def h_high(n):
                for k in range(KD):
                    act.wait_ge(s.t_ready, 8 * n + k + 1)
                    if norm_shift[n] is not None:
                        act.activation(h_hi[:, k, :], nt[:, k, :], ACT.Identity, bias=norm_shift[n][:, k:k + 1]).then_inc(s.h_hi_ready, 1)
                    else:
                        act.activation(h_hi[:, k, :], nt[:, k, :], ACT.Copy).then_inc(s.h_hi_ready, 1)

            act.wait_ge(s.vectors_loaded, 16)
            act.activation(c_act[:, :], vecs("c"), ACT.Silu).then_inc(s.c_act, 1)
            act.wait_ge(s.x_loaded, 16)
            act.wait_ge(s.consts_loaded, 16)
            squares(0)
            act.wait_ge(s.gab_loaded, 16)
            act.activation(gab_wh[:, :], gab_w[:, :], ACT.Copy).then_inc(s.gab_hi, 1)
            root(0)
            hi(0)
            h_high(0)
            hi(1)

            dest = [kT[:, 0:2, :], kT[:, 2:4, :], qT[:, 0:2, :], qT[:, 2:4, :], vT[:, 0:2, :], vT[:, 2:4, :]]

            def feature(w):
                act.wait_ge(s.conv_done, w + 1)
                act.activation(dest[w], cacc.rearrange("p (a b) -> p a b", a=2), ACT.Silu).then_inc(s.feature_ready, 1)
                if w < 4:
                    act.wait_ge(s.feature_ready, w + 1)
                    act.activation(head_sq[w].rearrange("p (a b) -> p a b", a=2), dest[w], ACT.Square).then_inc(s.head_squared, 1)

            for w in range(6):
                hi(w + 2)
                act.wait_ge(s.block_used, w + 1)
                if w == 0:
                    act.wait_ge(s.pool_zeroed, 2)
                if w:
                    act.wait_ge(s.conv_done, w)
                act.activation(pad[:, :, 3:259], A[w % 4].rearrange("p (a b) -> p a b", a=2), ACT.Copy).then_inc(s.pad_ready, 1)
                if w:
                    feature(w - 1)
                if w == 1:
                    act.wait_ge(s.gate_dve, 1)
                    act.activation(gt[:, 1, :], gt[:, 0, :], ACT.Exp).then_inc(s.gate_exp, 1)
                    act.activation(gt[:, 3, :], gt[:, 2, :], ACT.Exp).then_inc(s.gate_exp, 1)
                    act.activation(gt[:, 4, 0:8], vecs("a_log"), ACT.Exp).then_inc(s.gate_exp, 1)
                    act.wait_ge(s.gate_dve, 2)
                    act.activation(gt[:, 5, :], gt[:, 7, :], ACT.Ln).then_inc(s.gate_exp, 1)
            two = lambda b: b.rearrange("p (a b) -> p a b", a=2)
            hi(8)
            feature(5)
            act.wait_ge(s.block_used, 7)
            act.activation(zT[:, 0:2, :], two(A[2]), ACT.Silu).then_inc(s.proj_evac, 1)
            act.wait_ge(s.head_inv, 1)
            act.activation(hs[:, 2, :], hs[:, 1, :], ACT.Sqrt).then_inc(s.head_rms, 1)
            hi(9)
            act.wait_ge(s.block_used, 8)
            act.activation(zT[:, 2:4, :], two(A[3]), ACT.Silu).then_inc(s.proj_evac, 1)
            act.wait_ge(s.decay_dve, 1)
            act.activation(kds[:, 1, :], kds[:, 0, :], ACT.Exp).then_inc(s.decay_act, 1)
            for w in (8, 9):
                hi(w + 2)
                act.wait_ge(s.block_used, w + 1)
                act.activation(qs[:, 2 * (w - 8):2 * (w - 8) + 2, :], two(A[w % 4]), ACT.Copy).then_inc(s.proj_evac, 1)
                act.activation(head_sq[w - 4], A[w % 4], ACT.Square).then_inc(s.head_squared, 1)
                if w == 8:
                    act.wait_ge(s.big_ready, BIG_INDEX["eg"] + 1)
                    act.activation(eg.rearrange("p a b -> p (a b)"), big("eg")[:, :], ACT.Exp).then_inc(s.big_read_act, 1)
            hi(12)
            act.wait_ge(s.block_used, 11)
            act.activation(ks[:, :], A[2][:, 0:256], ACT.Copy).then_inc(s.proj_evac, 1)
            act.activation(vs[:, :, :].rearrange("p t c -> p (t c)"), A[2][:, 256:512], ACT.Copy).then_inc(s.proj_evac, 1)
            act.activation(head_sq[6][:, 0:256], A[2][:, 0:256], ACT.Square).then_inc(s.head_squared, 1)
            for gi in range(4):
                act.wait_ge(s.d_shifted, gi + 1)
                act.activation(DT[:, gi, :], DT[:, gi, :], ACT.Exp).then_inc(s.d_ready, 1)
            hi(13)
            act.wait_ge(s.head_inv, 2)
            act.activation(ss[:, 2, :], ss[:, 1, :], ACT.Sqrt).then_inc(s.head_rms, 1)

            def exps(a, sc):
                act.wait_ge(s.negmax_ready, a + 1)
                for hh in range(4):
                    for part, (c0, c1) in enumerate(((0, 256), (256, 384))):
                        act.activation(sc[:, hh, c0:c1], sc[:, hh, c0:c1], ACT.Exp,
                                       bias=soft[:, 1, 2 * hh + part:2 * hh + part + 1],
                                       accum_out=soft[:, 2, 2 * hh + part:2 * hh + part + 1]).then_inc(s.exp_ready, 1)
                if a < 2:
                    act.activation(soft[:, 3, :], soft[:, 3, :], ACT.Exp).then_inc(s.exp_ready, 1)

            def probs_copy(a, bank, pT):
                if a == 0:
                    act.wait_ge(s.row_scaled, 2)
                for hh in range(4):
                    act.wait_ge(s.ptrans_ready, 4 * a + hh + 1)
                    act.activation(pT[:, hh, :], bank[hh][:, 0:384], ACT.Copy).then_inc(s.ptrans_copied, 1)

            def pv_high(a, bank, dst):
                act.wait_ge(s.pv_ready, a + 1)
                act.activation(dst, bank.rearrange("p (a b) -> p a b", a=2), ACT.Copy).then_inc(s.pv_hi, 1)

            def x_copy(l, gi, bank):
                act.wait_ge(s.xtr_ready, 4 * l + gi + 1)
                return act.activation(X[:, gi, :], bank[:, :], ACT.Copy)

            for gi in range(4):
                if gi == 0:
                    act.wait_ge(s.big_read_dve, big_reads(BIG_INDEX["qk3"], "dve"))
                x_copy(0, gi, big(f"tr{gi}")).then_inc(s.x_copied, 1)
            exps(0, sc1)
            for l in range(1, NEXP + 1):
                for gi in range(4):
                    act.wait_ge(s.p_ready, 4 * (l - 1) + gi + 1)
                    act.activation(Pm[:, gi, :], B[gi][:, :], ACT.Copy).then_inc(s.p_copied, 1)
                if l < NEXP:
                    for gi in range(4):
                        x_copy(l, gi, B[gi]).then_inc(s.x_copied, 1)
                if l == 2:
                    probs_copy(0, A, pT1)
                    pv_high(0, A[0], h_hi[:, 4:6, :])
                if l == 3:
                    exps(1, sc1)
                if l == 5:
                    probs_copy(1, A, pT1)
            pv_high(1, A[0], h_hi[:, 6:8, :])
            act.wait_ge(s.u_ready, 1)
            act.activation(u0, B[0][:, :], ACT.Copy).then_inc(s.u_copied, 1)
            act.wait_ge(s.o0_ready, 1)
            for par in range(2):
                rows = slice(64 * par, 64 * par + 64)
                act.activation(oT[rows, :, 0:P], B[2 + par][rows, :].rearrange("p (a b) -> p a b", a=4), ACT.Copy).then_inc(s.o_copied, 1)
            act.wait_ge(s.vn_ready, 1)
            act.activation(vn, B[0][:, :], ACT.Copy).then_inc(s.vn_copied, 1)
            act.wait_ge(s.o1_ready, 1)
            for par in range(2):
                rows = slice(64 * par, 64 * par + 64)
                act.activation(oT[rows, :, P:T], B[par][rows, :].rearrange("p (a b) -> p a b", a=4), ACT.Copy).then_inc(s.o_copied, 1)
            act.wait_ge(s.o_copied, 4)
            act.activation(osq, oT, ACT.Square).then_inc(s.o_squared, 1)
            act.wait_ge(s.o_inv, 1)
            act.activation(os_[:, 2, :], os_[:, 1, :], ACT.Sqrt).then_inc(s.o_rms, 1)
            for i in range(2):
                act.wait_ge(s.o_gated, i + 1)
                act.activation(h_hi[:, 2 * i:2 * i + 2, :], oT[:, 2 * i:2 * i + 2, :], ACT.Copy).then_inc(s.o_hi_done, 1)
            hi(14)
            hi(15)
            hi(16)

            def ffn(f):
                F = FFN_BASE[f]

                def silu(j, used):
                    if f:
                        act.wait_ge(s.gate_scaled, j + (JF * (f - 1) + 1))
                        act.activation(sg[:, :], sg[:, :], ACT.Silu).then_inc(s.silu_ready, 1)
                    else:
                        act.wait_ge(s.block_used, used)
                        if not isinstance(j, int) or j:
                            act.wait_ge(s.hid_ready, j)
                        act.activation(sg[:, :], B[0][:, :], ACT.Silu).then_inc(s.silu_ready, 1)

                def hid_high(j, used, dst=hid_hi[:, :, :]):
                    act.wait_ge(s.hid_ready, j + (JF * f + 1))
                    if used is not None:
                        act.wait_ge(s.block_used, used)
                    act.activation(dst.rearrange("p a b -> p (a b)"), hid[:, :], ACT.Copy).then_inc(s.hid_hi_ready, 1)

                if f:
                    squares_and_high(2 * f + 1, F + 1)
                    hi(F + 2)
                    root(2 * f + 1)
                else:
                    squares(1)
                    root(1)
                    h_high(1)
                    hi(F + 2)
                silu(0, F + 1)
                hi(F + 3)
                hid_high(0, None)
                with act.Fori(1, JF - 1) as j:
                    hi(F + 4, j - 1)
                    silu(j, (j - 1) * RING + (F + 3))
                    hi(F + 5, j - 1)
                    hi(F + 6, j - 1)
                    hid_high(j, (j - 1) * RING + (F + 5))
                hi(F + 4, JF - 2)
                silu(JF - 1, (JF - 2) * RING + (F + 3))
                hi(F + 5, JF - 2)
                hid_high(JF - 1, None, last_hid[0])
                if f < 2:
                    hi(F + 6, JF - 2)

            ffn(0)
            squares_and_high(2, CONV_BASE + 1)
            for i in range(4):
                w = CONV_BASE + 3 * i
                hi(w + 2)
                if i == 0:
                    root(2)
                hi(w + 3)
                hi(w + 4)
                act.wait_ge(s.by_ready, i + 1)
                act.activation(o_hi[:, 2 * i:2 * i + 2, :], yb[:, :, :], ACT.Copy).then_inc(s.by_hi, 1)
            for w in range(CONV_OUT + 2, CONV_OUT + 5):
                hi(w)
            ffn(1)
            squares_and_high(4, QKV_BASE + 1)
            for i in range(5):
                w, a = QKV_BASE + 3 * i, i + 1
                if i < 4:
                    hi(w + 2)
                if i == 0:
                    root(4)
                else:
                    exps(a, sc2)
                if i < 4:
                    hi(w + 3)
                    hi(w + 4)
                    act.wait_ge(s.block_used, w + 3)
                    for t in range(TT):
                        act.activation(v2[:, i % 2, t, :], A[2][:, 256 * t:256 * t + 256], ACT.Copy, scale=rms[:, t:t + 1]).then_inc(s.v_scaled, 1)
                else:
                    for v in range(ATT_OUT + 2, ATT_OUT + 4):
                        hi(v)
                if i:
                    probs_copy(a, B, pT2)
                    pv_high(a, A[3] if i < 4 else B[0], o_hi[:, 2 * i - 2:2 * i, :])
            hi(ATT_OUT + 4)
            ffn(2)
            squares(6)
            root(6)

        @block.vector
        def _(dve):
            steps = [0]

            def link(ins):
                steps[0] += 1
                ins.then_inc(s.dve_step, 1)
                dve.wait_ge(s.dve_step, steps[0])

            def lo(w, it=0):
                dve.wait_ge(s.hi_ready, it * RING + (w + 1))
                dve.tensor_tensor(w_lo[:, w % RING, :], raw[:, raw_index(w) % RING, :], w_hi[:, w % RING, :],
                                  ALU.subtract).then_inc(s.lo_ready, 1)

            def accumulate(m):
                k, r = m % MOD_BLOCKS, mod_index(m)
                mod_acc = mod_accs[m // MOD_BLOCKS]
                dve.wait_ge(raw_landed[r % RING], 16 * (r // RING + 1))
                if k == 0:
                    if m:
                        dve.wait_ge(s.mod_summed, m // MOD_BLOCKS)
                    dve.tensor_scalar(mod_acc, raw[:, r % RING, :], c_act[:, 0:1], None, ALU.mult).then_inc(s.mod_accumulated, 1)
                else:
                    dve.wait_ge(s.mod_accumulated, m)
                    dve.scalar_tensor_tensor(out=mod_acc, in0=raw[:, r % RING, :], scalar=c_act[:, k:k + 1],
                                             in1=mod_acc, op0=ALU.mult, op1=ALU.add).then_inc(s.mod_accumulated, 1)

            def modulation(part):
                dve.wait_ge(s.mod_summed, part + 1)
                b0 = V_AT["b_ada"][0] + 16 * part
                link(dve.tensor_tensor(mods[:, 16 * part:16 * part + 16], mod_bank[part][:, 480:496], vec[:, b0:b0 + 16], ALU.add))
                if part == 1:
                    dve.tensor_copy(qk_w[:, :], qk_w[:, :]).then_inc(s.mod_ready, 1)
                elif part == 0:
                    dve.scalar_tensor_tensor(out=a1[:, :], in0=mods[:, 8:16], scalar=1.0, in1=vecs("norm1"),
                                             op0=ALU.add, op1=ALU.mult).then_inc(s.mod_ready, 1)
                elif part == 2:
                    dve.scalar_tensor_tensor(out=a2[:, :], in0=mods[:, 32:40], scalar=1.0, in1=vecs("norm2"),
                                             op0=ALU.add, op1=ALU.mult).then_inc(s.mod_ready, 1)

            def inverse_mean(n):
                dve.wait_ge(s.sumsq_ready, n + 1)
                link(dve.tensor_scalar(ms[:, :], B[3][:, 0:TT], 1.0 / D, EPS, ALU.mult, ALU.add))
                dve.reciprocal(inv[:, :], ms[:, :]).then_inc(s.inv_ready, 1)

            def h_parts(n):
                dve.wait_ge(s.rstd_ready, n + 1)
                rstd = B[3][:, 256:512]

                def scaled(k):
                    dve.scalar_tensor_tensor(out=nt[:, k, :], in0=x[:, k, :], scalar=norm_scale[n][:, k:k + 1],
                                             in1=rstd, op0=ALU.mult, op1=ALU.mult).then_inc(s.t_ready, 1)

                def low(k):
                    dve.wait_ge(s.h_hi_ready, 8 * n + k + 1)
                    if norm_shift[n] is not None:
                        dve.scalar_tensor_tensor(out=h_lo[:, k, :], in0=nt[:, k, :], scalar=norm_shift[n][:, k:k + 1],
                                                 in1=h_hi[:, k, :], op0=ALU.add, op1=ALU.subtract).then_inc(s.h_lo_ready, 1)
                    else:
                        dve.tensor_tensor(h_lo[:, k, :], nt[:, k, :], h_hi[:, k, :], ALU.subtract).then_inc(s.h_lo_ready, 1)

                for k in range(KD):
                    scaled(k)
                    if n < 6 and k >= 1:
                        low(k - 1)
                if n < 6:
                    low(KD - 1)

            def low_of_x(n, k):
                dve.wait_ge(s.h_hi_ready, 8 * n + k + 1)
                dve.scalar_tensor_tensor(out=h_lo[:, k, :], in0=x[:, k, :], scalar=norm_scale[n][:, k:k + 1],
                                         in1=h_hi[:, k, :], op0=ALU.mult, op1=ALU.subtract).then_inc(s.h_lo_ready, 1)

            def residual(r, last):
                for m in range(KD):
                    if m < KD - 2:
                        dve.wait_ge(s.acc_tile_done, 3 * r + m // 2 + 1)
                    else:
                        dve.wait_ge(s.block_used, last + 1)
                    a = acc[:, 256 * m:256 * m + 256]
                    if gates[r] is not None:
                        dve.scalar_tensor_tensor(out=x[:, m, :], in0=a, scalar=gates[r][:, m:m + 1], in1=x[:, m, :],
                                                 op0=ALU.mult, op1=ALU.add).then_inc(s.x_ready, 1)
                    else:
                        dve.tensor_tensor(x[:, m, :], a, x[:, m, :], ALU.add).then_inc(s.x_ready, 1)
                    if r + 1 in LATE and m >= 2:
                        low_of_x(r + 1, m - 2)
                if r + 1 in LATE:
                    low_of_x(r + 1, KD - 2)
                    low_of_x(r + 1, KD - 1)
                    lo(last + 2)

            dve.wait_ge(s.vectors_loaded, 16)
            dve.wait_ge(s.c_act, 1)
            link(dve.tensor_scalar(qk_w[:, :], vecs("qn_w"), HD ** -0.5, None, ALU.mult))
            link(dve.tensor_copy(sink2[:, :, 0], vecs("sinks")))
            link(dve.tensor_copy(sink2[:, :, 1], vecs("sinks")))
            for m in range(5):
                accumulate(m)
            inverse_mean(0)
            for m in range(5, MOD_BLOCKS):
                accumulate(m)
            lo(0)
            modulation(0)
            dve.wait_ge(s.mod_ready, 1)
            h_parts(0)
            lo(1)
            dve.wait_ge(s.gab_hi, 1)
            dve.tensor_tensor(gab_wl[:, :], gab_w[:, :], gab_wh[:, :], ALU.subtract).then_inc(s.gab_lo, 1)

            for w in range(6):
                if w == 5:
                    dve.wait_ge(s.cum_ready, 1)
                    link(dve.tensor_copy(Gs[:, :], STAT[:, 32:48]))
                    dve.tensor_tensor(kds[:, 0, :], STAT[:, 48:56], Gs[:, 0:8], ALU.subtract).then_inc(s.decay_dve, 1)
                lo(w + 2)
                if w < 6:
                    dve.wait_ge(s.pad_ready, w + 1)
                    if w:
                        dve.wait_ge(s.feature_ready, w)
                    tile0 = (4, 6, 0, 2, 8, 10)[w]
                    for mt in range(2):
                        o = cacc[:, 256 * mt:256 * mt + 256]
                        cw = V_AT["conv_w"][0] + 4 * (tile0 + mt)
                        dve.tensor_scalar(o, pad[:, mt, 0:256], vec[:, cw:cw + 1], None, ALU.mult).then_inc(s.dve_step, 1)
                        steps[0] += 1
                    for tap in range(1, 4):
                        for mt in range(2):
                            o = cacc[:, 256 * mt:256 * mt + 256]
                            cw = V_AT["conv_w"][0] + 4 * (tile0 + mt) + tap
                            dve.wait_ge(s.dve_step, steps[0] - 1)
                            ins = dve.scalar_tensor_tensor(out=o, in0=pad[:, mt, tap:tap + 256], scalar=vec[:, cw:cw + 1],
                                                           in1=o, op0=ALU.mult, op1=ALU.add)
                            if tap == 3 and mt == 1:
                                dve.wait_ge(s.dve_step, steps[0])
                                ins.then_inc(s.conv_done, 1)
                            else:
                                ins.then_inc(s.dve_step, 1)
                                steps[0] += 1
                if w == 0:
                    dve.wait_ge(s.gab_ready, 1)
                    ga = STAT[:, 0:32].rearrange("p (t c) -> p t c", t=TT)
                    v8 = lambda a: a.rearrange("p (t c) -> p t c", t=TT)
                    link(dve.tensor_tensor(v8(gt[:, 6, :]), ga[:, :, 0:8],
                                           vecs("dt_bias").unsqueeze(1).broadcast_to([P, TT, 8]), ALU.add))
                    link(dve.tensor_scalar(v8(gt[:, 0, :]), ga[:, :, 8:16], -1.0, None, ALU.mult))
                    dve.scalar_tensor_tensor(out=gt[:, 2, :], in0=gt[:, 6, :], scalar=-1.0, in1=gt[:, 6, :],
                                             op0=ALU.mult, op1=ALU.min).then_inc(s.gate_dve, 1)
                if w == 1:
                    dve.wait_ge(s.t5_psum, 1)
                    dve.wait_ge(s.t5_loaded, 48)
                    dve.tensor_tensor(t5r[:, :], B[1][0:16, 0:384], t5l, ALU.add).then_inc(s.t5_row, 1)
                    dve.wait_ge(s.gate_exp, 3)
                    dve.tensor_scalar(gt[:, 7, :], gt[:, 3, :], 1.0, None, ALU.add).then_inc(s.gate_dve, 1)
                    link(dve.tensor_scalar(gt[:, 2, :], gt[:, 1, :], 1.0, None, ALU.add))
                    link(dve.reciprocal(beta[:, :], gt[:, 2, :]))
                    dve.wait_ge(s.gate_exp, 4)
                    link(dve.scalar_tensor_tensor(out=gt[:, 6, :], in0=gt[:, 6, :], scalar=0.0, in1=gt[:, 5, :],
                                                  op0=ALU.max, op1=ALU.add))
                    dve.scalar_tensor_tensor(out=v8(g[:, :]), in0=v8(gt[:, 6, :]), scalar=-1.0,
                                             in1=gt[:, 4, 0:8].unsqueeze(1).broadcast_to([P, TT, 8]),
                                             op0=ALU.mult, op1=ALU.mult).then_inc(s.gate_done, 1)

            def big_read(name, ins):
                assert ("dve" == BIG_LIST[BIG_INDEX[name]][1])
                ins.then_inc(s.big_read_dve, 1)

            def wait_big(name):
                dve.wait_ge(s.big_ready, BIG_INDEX[name] + 1)

            def wait_read(name):
                dve.wait_ge(s.big_read_dve, big_reads(BIG_INDEX[name], "dve"))

            two = lambda b: b[:, :].rearrange("p (a b) -> p a b", a=2)
            four = lambda b: b.rearrange("p (i c) -> p i c", i=4)

            lo(8)
            dve.wait_ge(s.head_sums, 1)
            link(dve.tensor_scalar(hs[:, 0, :], STAT[:, 64:96], EPS, None, ALU.add))
            dve.reciprocal(hs[:, 1, :], hs[:, 0, :]).then_inc(s.head_inv, 1)
            lo(9)
            hsv = hs[:, 2, :].rearrange("p (t c) -> p t c", t=TT)
            dve.wait_ge(s.head_rms, 1)
            dve.tensor_tensor(v8(coefk[:, :]), v8(beta[:, :]), hsv[:, :, 0:8], ALU.mult).then_inc(s.coef_ready, 1)
            dve.tensor_scalar(v8(coefq[:, :]), hsv[:, :, 8:16], HD ** -0.5, None, ALU.mult).then_inc(s.coef_ready, 1)

            def row_scale(name, dst, src):
                wait_big(name)
                big_read(name, dve.tensor_tensor(dst, src, two(big(name)), ALU.mult))

            row_scale("kb01", kbT[:, 0:2, :], kT[:, 0:2, :])
            row_scale("kb23", kbT[:, 2:4, :], kT[:, 2:4, :])
            row_scale("q01", qT[:, 0:2, :], qT[:, 0:2, :])
            lo(10)
            row_scale("q23", qT[:, 2:4, :], qT[:, 2:4, :])
            dve.wait_ge(s.decay_act, 1)
            link(dve.tensor_tensor(kds[:, 1, :], kds[:, 1, :], hsv[:, 0, 0:8], ALU.mult))
            dve.wait_ge(s.big_read_act, big_reads(BIG_INDEX["eg"], "act"))
            wait_read("q23")
            dve.tensor_tensor(kbgT[:, :, :], kbT[:, :, P:T], eg, ALU.mult).then_inc(s.row_scaled, 1)
            dve.tensor_tensor(qdT[:, :, :], qT[:, :, P:T], eg, ALU.mult).then_inc(s.row_scaled, 1)

            def by_token(name, dst, factor):
                wait_big(name)
                big_read(name, dve.tensor_tensor(
                    dst.rearrange("p (h e) -> p h e", h=8), big(name)[:, :].rearrange("p (h e) -> p h e", h=8),
                    factor.unsqueeze(2).broadcast_to([P, 8, HD]), ALU.mult))

            by_token("v0", vb[:, 0, :], beta[:, 0:8])
            lo(11)
            by_token("v1", vb[:, 1, :], beta[:, 8:16])
            by_token("kt", kd[:, :], kds[:, 1, :])

            def decay(gi):
                t, par = gi // 2, gi % 2
                Gcol = Gs[:, :].rearrange("p (t i two) -> p t i two", t=TT, two=2)[:, t, :, par]
                wait_big(f"G{gi}")
                big_read(f"G{gi}", dve.tensor_tensor(four(DT[:, gi, :]), four(big(f"G{gi}")[:, :]),
                                                     Gcol.unsqueeze(2).broadcast_to([P, 4, P]), ALU.subtract))
                wait_read(f"G{gi}")
                dve.tensor_tensor(four(DT[:, gi, :]), four(DT[:, gi, :]), future.unsqueeze(1).broadcast_to([P, 4, P]),
                                  ALU.add).then_inc(s.d_shifted, 1)

            def row_norm(gi):
                rk = hs[:, 2, 16 * (gi // 2):16 * (gi // 2) + 8].rearrange("p (i two) -> p i two", two=2)[:, :, gi % 2]
                dve.wait_ge(s.d_ready, gi + 1)
                dve.tensor_tensor(four(DT[:, gi, :]), four(DT[:, gi, :]), rk.unsqueeze(2).broadcast_to([P, 4, P]),
                                  ALU.mult).then_inc(s.d_normed, 1)

            for gi in range(3):
                decay(gi)
            lo(12)
            decay(3)
            for gi in range(4):
                row_norm(gi)
                wait_big(f"kk{gi}")
                dve.wait_ge(s.d_normed, gi + 1)
                big_read(f"kk{gi}", dve.tensor_tensor(AT[:, gi, :], big(f"kk{gi}")[:, :], DT[:, gi, :], ALU.mult))
                wait_read(f"kk{gi}")
                dve.tensor_tensor(four(XT[:, gi, :]), four(AT[:, gi, :]), level_mask[0].unsqueeze(1).broadcast_to([P, 4, P]),
                                  ALU.mult).then_inc(s.at_ready, 1)
                dve.wait_ge(s.at_ready, gi + 1)
                dve.tensor_tensor(four(XT[:, gi, :]), ident.unsqueeze(1).broadcast_to([P, 4, P]), four(XT[:, gi, :]),
                                  ALU.subtract).then_inc(s.xt_ready, 1)
            dve.wait_ge(s.head_sums, 2)
            link(dve.tensor_scalar(ss[:, 0, :], STAT[:, 96:116], 1.0 / HD, EPS, ALU.mult, ALU.add))
            dve.reciprocal(ss[:, 1, :], ss[:, 0, :]).then_inc(s.head_inv, 1)
            for gi in range(4):
                wait_big(f"qk{gi}")
                big_read(f"qk{gi}", dve.tensor_tensor(qkT[:, gi, :], big(f"qk{gi}")[:, :], DT[:, gi, :], ALU.mult))
            lo(13)
            wait_big("sk")
            dve.wait_ge(s.proj_evac, 5)
            big_read("sk", dve.scalar_tensor_tensor(out=ks[:, :], in0=ks[:, :], scalar=vecs("kn_w"), in1=big("sk")[:, 0:256],
                                                    op0=ALU.mult, op1=ALU.mult))
            for i, name in enumerate(("sq01", "sq23")):
                wait_big(name)
                big_read(name, dve.scalar_tensor_tensor(out=qs[:, 2 * i:2 * i + 2, :], in0=qs[:, 2 * i:2 * i + 2, :],
                                                        scalar=qk_w[:, :], in1=two(big(name)), op0=ALU.mult, op1=ALU.mult))

            def softmax_max(a, bank, sc):
                for hh in range(4):
                    dve.wait_ge(s.scores_ready, 4 * a + hh + 1)
                    if a < 2:
                        head = 2 * a + hh // 2 + 4 * (hh % 2)
                        ins = dve.scalar_tensor_tensor(out=sc[:, hh, :], in0=const("alibi"), scalar=2.0 ** -(head + 1),
                                                       in1=bank[hh][:, 0:384], op0=ALU.mult, op1=ALU.add)
                    else:
                        ins = dve.tensor_tensor(sc[:, hh, :], t5[:, 4 * (a - 2) + hh, :], bank[hh][:, 0:384], ALU.add)
                    ins.then_inc(s.scores_biased, 1)
                    dve.wait_ge(s.scores_biased, 4 * a + hh + 1)
                    for part, (c0, c1) in enumerate(((0, 256), (256, 384))):
                        link(dve.tensor_reduce(soft[:, 0, 2 * hh + part:2 * hh + part + 1], sc[:, hh, c0:c1], AX.X, ALU.max))
                if a < 2:
                    sk = sink2[:, 4 * a:4 * a + 4, :].rearrange("p h t -> p (h t)")
                    link(dve.tensor_tensor(soft[:, 0, :], soft[:, 0, :], sk, ALU.max))
                    link(dve.tensor_tensor(soft[:, 3, :], sk, soft[:, 0, :], ALU.subtract))
                dve.tensor_scalar(soft[:, 1, :], soft[:, 0, :], -1.0, None, ALU.mult).then_inc(s.negmax_ready, 1)

            def softmax_div(a, sc):
                dve.wait_ge(s.exp_ready, 8 * (a + 1) + min(a + 1, 2))
                if a < 2:
                    link(dve.tensor_tensor(soft[:, 4, :], soft[:, 2, :], soft[:, 3, :], ALU.add))
                    link(dve.reciprocal(soft[:, 5, :], soft[:, 4, :]))
                else:
                    link(dve.reciprocal(soft[:, 5, :], soft[:, 2, :]))
                for hh in range(4):
                    for part, (c0, c1) in enumerate(((0, 256), (256, 384))):
                        dve.tensor_scalar(sc[:, hh, c0:c1], sc[:, hh, c0:c1], soft[:, 5, 2 * hh + part:2 * hh + part + 1],
                                          None, ALU.mult).then_inc(s.probs_ready, 1)

            def pv_low(a, bank, dst, high):
                dve.wait_ge(s.pv_hi, a + 1)
                dve.tensor_tensor(dst, bank.rearrange("p (a b) -> p a b", a=2), high, ALU.subtract).then_inc(s.pv_lo, 1)

            softmax_max(0, A, sc1)
            at = MOD_BLOCKS
            for l in range(1, NEXP + 1):
                for gi in range(4):
                    dve.wait_ge(s.qt_ready, 4 * (l - 1) + gi + 1)
                    dve.wait_ge(s.xt_ready, 4 * (l - 1) + gi + 1)
                    dve.tensor_tensor(XT[:, gi, :], XT[:, gi, :], B[gi][:, :], ALU.subtract).then_inc(s.xt_ready, 1)
                if l == 1:
                    softmax_div(0, sc1)
                if l == 2:
                    pv_low(0, A[0], h_lo[:, 4:6, :], h_hi[:, 4:6, :])
                    softmax_max(1, A, sc1)
                if l == 4:
                    softmax_div(1, sc1)
                for _ in range((2, 0, 1, 1, 2, 0)[l - 1]):
                    accumulate(at)
                    at += 1
            accumulate(at)
            accumulate(at + 1)
            at += 2
            modulation(1)
            pv_low(1, A[0], h_lo[:, 6:8, :], h_hi[:, 6:8, :])
            for _ in range(3):
                accumulate(at)
                at += 1
            dve.wait_ge(s.s_ready, 1)
            dve.tensor_copy(S1, B[1][:, 0:256]).then_inc(s.s_copied, 1)
            dve.wait_ge(s.r_ready, 1)
            v4 = lambda ap, par: ap.rearrange("p (i two e) -> p i two e", two=2, e=HD)[:, :, par, :]
            for par in range(2):
                dve.tensor_tensor(v4(r1, par), v4(vb[:, 1, :], par), B[par][:, 0:256].rearrange("p (i e) -> p i e", e=HD),
                                  ALU.subtract).then_inc(s.r_done, 1)
            for _ in range(3):
                accumulate(at)
                at += 1
            dve.wait_ge(s.o_sums, 1)
            link(dve.tensor_scalar(os_[:, 0, :], B[2][:, 0:16], 1.0 / HD, EPS, ALU.mult, ALU.add))
            dve.reciprocal(os_[:, 1, :], os_[:, 0, :]).then_inc(s.o_inv, 1)
            for i in range(2):
                dve.wait_ge(s.o_rows, i + 1)
                o = oT[:, 2 * i:2 * i + 2, :]
                link(dve.scalar_tensor_tensor(out=o, in0=o, scalar=vecs("gdn_w"), in1=two(B[i]), op0=ALU.mult, op1=ALU.mult))
                dve.tensor_tensor(o, o, zT[:, 2 * i:2 * i + 2, :], ALU.mult).then_inc(s.o_gated, 1)
            for i in range(2):
                dve.wait_ge(s.o_hi_done, i + 1)
                dve.tensor_tensor(h_lo[:, 2 * i:2 * i + 2, :], oT[:, 2 * i:2 * i + 2, :], h_hi[:, 2 * i:2 * i + 2, :],
                                  ALU.subtract).then_inc(s.o_lo_done, 1)
            for _ in range(2):
                accumulate(at)
                at += 1
            lo(14)
            modulation(2)
            lo(15)
            lo(16)
            residual(0, 14)

            def wait_row(n):
                dve.wait_ge(s.row_copied, LATE.index(n) + 1)

            both = lambda row: row.unsqueeze(1).broadcast_to([P, 2, T])

            def ffn(f):
                F = FFN_BASE[f]

                def scale_gate(j, used):
                    if f:
                        dve.wait_ge(s.block_used, used)
                        dve.tensor_tensor(two(sg), two(B[0]), both(rrow[:, :]), ALU.mult).then_inc(s.gate_scaled, 1)

                def product(j, used):
                    dve.wait_ge(s.silu_ready, j + (JF * f + 1))
                    dve.wait_ge(s.block_used, used)
                    if not (isinstance(j, int) and f + j == 0):
                        dve.wait_ge(s.hid_lo_ready, j + JF * f)
                    if f:
                        dve.tensor_tensor(hid[:, :], sg[:, :], B[1][:, :], ALU.mult).then_inc(s.gated, 1)
                        dve.wait_ge(s.gated, j + (JF * (f - 1) + 1))
                        dve.tensor_tensor(two(hid), two(hid), both(rrow[:, :]), ALU.mult).then_inc(s.hid_ready, 1)
                    else:
                        dve.tensor_tensor(hid[:, :], sg[:, :], B[1][:, :], ALU.mult).then_inc(s.hid_ready, 1)

                def hid_low(j, high=hid_hi[:, :, :], dst=hid_lo[:, :, :]):
                    dve.wait_ge(s.hid_hi_ready, j + (JF * f + 1))
                    dve.tensor_tensor(dst.rearrange("p a b -> p (a b)"), hid[:, :],
                                      high.rearrange("p a b -> p (a b)"), ALU.subtract).then_inc(s.hid_lo_ready, 1)

                if f:
                    lo(F + 2)
                    inverse_mean(2 * f + 1)
                    wait_row(2 * f + 1)
                else:
                    inverse_mean(1)
                    h_parts(1)
                    lo(F + 2)
                scale_gate(0, F + 1)
                lo(F + 3)
                product(0, F + 2)
                hid_low(0)
                with dve.Fori(1, JF - 1) as j:
                    lo(F + 4, j - 1)
                    scale_gate(j, (j - 1) * RING + (F + 3))
                    lo(F + 5, j - 1)
                    product(j, (j - 1) * RING + (F + 4))
                    lo(F + 6, j - 1)
                    hid_low(j)
                lo(F + 4, JF - 2)
                scale_gate(JF - 1, (JF - 2) * RING + (F + 3))
                lo(F + 5, JF - 2)
                product(JF - 1, (JF - 2) * RING + (F + 4))
                hid_low(JF - 1, *last_hid)
                if f < 2:
                    lo(F + 6, JF - 2)
                residual(2 * f + 1, F + 32)

            ffn(0)
            dve.wait_ge(s.pool_zeroed, 3)
            for i in range(4):
                w = CONV_BASE + 3 * i
                lo(w + 2)
                if i == 0:
                    inverse_mean(2)
                    wait_row(2)
                    link(dve.tensor_tensor(rrow2[:, :], rrow[:, :], rrow[:, :], ALU.mult))
                lo(w + 3)
                dve.wait_ge(s.block_used, w + 2)
                link(dve.tensor_tensor(two(c_sb), two(conv_banks[i % 2][1]), both(rrow2[:, :]), ALU.mult))
                lo(w + 4)
                dve.wait_ge(s.block_used, w + 3)
                cu_in = cu[:, :, 2:T + 2]
                dve.tensor_tensor(cu_in, c_sb[:, :].rearrange("p (a b) -> p a b", a=2), two(conv_banks[i % 2][2]), ALU.mult).then_inc(s.cu_ready, 1)
                dve.wait_ge(s.cu_ready, i + 1)
                for tap in range(3):
                    for mt in range(2):
                        ck = V_AT["conv_k"][0] + 3 * (2 * i + mt) + tap
                        if tap == 0:
                            if i:
                                dve.wait_ge(s.by_hi, i)
                            link(dve.tensor_scalar(yb[:, mt, :], cu[:, mt, 0:T], vec[:, ck:ck + 1], None, ALU.mult))
                        else:
                            link(dve.scalar_tensor_tensor(out=yb[:, mt, :], in0=cu[:, mt, tap:tap + T], scalar=vec[:, ck:ck + 1],
                                                          in1=yb[:, mt, :], op0=ALU.mult, op1=ALU.add))
                link(dve.tensor_tensor(yb[:, :, :], yb[:, :, :], two(conv_banks[i % 2][0]), ALU.mult))
                dve.tensor_tensor(yb[:, :, :], yb[:, :, :], both(rrow[:, :]), ALU.mult).then_inc(s.by_ready, 1)
                dve.wait_ge(s.by_hi, i + 1)
                dve.tensor_tensor(o_lo[:, 2 * i:2 * i + 2, :], yb[:, :, :], o_hi[:, 2 * i:2 * i + 2, :], ALU.subtract).then_inc(s.by_lo, 1)
            for w in range(CONV_OUT + 2, CONV_OUT + 5):
                lo(w)
            residual(2, CONV_OUT + 3)
            ffn(1)
            dve.wait_ge(s.tables_loaded, 32)
            back = lambda ap, n: ap.rearrange("p (n c) -> p n c", n=n)[:, :, ::-1]
            for i in range(5):
                w, a = QKV_BASE + 3 * i, i + 1
                if i:
                    softmax_max(a, B, sc2)
                if i < 4:
                    lo(w + 2)
                    if i == 0:
                        inverse_mean(4)
                        wait_row(4)
                        link(dve.tensor_scalar(back(rrow2[:, :], TT), rrow[:, :].rearrange("p (n c) -> p n c", n=TT), HD ** -0.5, None, ALU.mult))
                    dve.wait_ge(s.block_used, w + 1)
                    for mt in range(2):
                        dve.tensor_tensor(q2[:, i % 2, mt, :].rearrange("p (n c) -> p n c", n=TT), back(A[0][:, T * mt:T * mt + T], TT),
                                          rrow2[:, :].rearrange("p (n c) -> p n c", n=TT), ALU.mult).then_inc(s.qk_scaled, 1)
                    lo(w + 3)
                if i:
                    softmax_div(a, sc2)
                if i < 4:
                    dve.wait_ge(s.block_used, w + 2)
                    dve.tensor_tensor(k2[:, i % 2, :, :], two(A[1]), both(rrow[:, :]), ALU.mult).then_inc(s.qk_scaled, 1)
                    lo(w + 4)
                else:
                    for v in range(ATT_OUT + 2, ATT_OUT + 4):
                        lo(v)
                if i:
                    pv_low(a, A[3] if i < 4 else B[0], o_lo[:, 2 * i - 2:2 * i, :], o_hi[:, 2 * i - 2:2 * i, :])
            lo(ATT_OUT + 4)
            residual(4, ATT_OUT + 3)
            ffn(2)
            inverse_mean(6)
            h_parts(6)

        @block.tensor
        def _(pe):
            def mm(o, l, r, start, stop):
                return pe.matmul(o, l, r, start=start, stop=stop, skip_group_check=True)

            def three(o, wh, wl, xh, xl, first, last):
                mm(o, wh, xh, first, False)
                mm(o, wh, xl, False, False)
                return mm(o, wl, xh, False, last)

            def column_block(w, bank, it=0, n=None, halfway=None):
                pe.wait_ge(s.lo_ready, it * RING + (w + 1))
                wh = w_hi[:, w % RING, :].rearrange("p (k c) -> p k c", k=KD)
                wl = w_lo[:, w % RING, :].rearrange("p (k c) -> p k c", k=KD)
                order = [(k, mt) for k in range(KD) for mt in range(2)] if n is not None else \
                    [(k, mt) for mt in range(2) for k in range(KD)]
                for k, mt in order:
                    if n is not None and mt == 0:
                        pe.wait_ge(s.h_lo_ready, 8 * n + k + 1)
                    if halfway is not None and mt == 1 and k == 0:
                        halfway()
                    c = slice(P * mt, P * mt + P)
                    ins = three(bank[:, 256 * mt:256 * mt + 256], wh[:, k, c], wl[:, k, c], h_hi[:, k, :], h_lo[:, k, :],
                                k == 0 and mt == 0, k == KD - 1)
                ins.then_inc(s.block_used, 1)

            def row_block(w, oh_, ol_, k0, it=0, first=False, n=None, before_last=None):
                pe.wait_ge(s.lo_ready, it * RING + (w + 1))
                wh = w_hi[:, w % RING, :].rearrange("p (k c) -> p k c", k=2)
                wl = w_lo[:, w % RING, :].rearrange("p (k c) -> p k c", k=2)
                for m in range(KD):
                    if m == KD - 2 and before_last is not None:
                        before_last()
                    for k in range(2):
                        ins = three(acc[:, 256 * m:256 * m + 256], wh[:, k, P * m:P * m + P], wl[:, k, P * m:P * m + P],
                                    oh_[:, k0 + k, :], ol_[:, k0 + k, :], first and k == 0 and m % 2 == 0, False)
                    if n is not None and m % 2 and m < KD - 1:
                        ins.then_inc(s.acc_tile_done, 1)
                        if m >= 5 and n not in LATE:
                            square_sums(n, m - 5)
                            square_sums(n, m - 4)
                ins.then_inc(s.block_used, 1)

            def square_sums(n, m):
                pe.wait_ge(s.squared, 8 * n + m + 1)
                for t in range(TT):
                    ins = mm(B[3][:, t:t + 1], nt[:, m, P * t:P * t + P], ones, m == 0 and t == 0, m == KD - 1)
                return ins

            def norm(n):
                sums(n, 2 if n else 0)
                rstd(n)

            def sums(n, m0=0):
                if n in LATE:
                    pe.wait_ge(s.squares_added, 4 * (LATE.index(n) + 1))
                    for t in range(TT):
                        ins = mm(B[3][:, t:t + 1], nt[:, 0, P * t:P * t + P], ones, True, True)
                else:
                    for m in range(m0, KD):
                        ins = square_sums(n, m)
                ins.then_inc(s.sumsq_ready, 1)

            def rstd(n):
                pe.wait_ge(s.rms_ready, n + 1)
                for t in range(TT):
                    ins = mm(B[3][:, 256 + P * t:256 + P * t + P], rms[:, t:t + 1].broadcast_to([P, P]), ident, True, True)
                ins.then_inc(s.rstd_ready, 1)

            pe.wait_ge(s.consts_loaded, 16)
            norm(0)

            def modulation(part):
                pe.wait_ge(s.mod_accumulated, MOD_BLOCKS * (part + 1))
                for j in range(16):
                    ins = mm(mod_bank[part][:, 480 + j:481 + j], mod_accs[part][:, P * j:P * j + P], ones, True, True)
                ins.then_inc(s.mod_summed, 1)

            modulation(0)

            def head_sums(src, tiles, col, width):
                for t in range(TT):
                    for i in range(tiles):
                        o = STAT[:, col + t * width + 2 * i:col + t * width + 2 * i + 2]
                        ins = mm(o, src(i, t), headsel, True, True)
                return ins

            def wait_bank(w):
                v = w - 4
                if 0 <= v < 6:
                    pe.wait_ge(s.pad_ready, v + 1)
                elif v >= 6:
                    pe.wait_ge(s.proj_evac, v - 5)

            def project(w):
                wait_bank(w)
                column_block(w, A[w % 4], n=0 if w == 0 else None)

            for w in range(6):
                project(w)
                if w == 0:
                    pe.wait_ge(s.gab_lo, 1)
                    for t in range(TT):
                        for k in range(KD):
                            tok = slice(P * t, P * t + P)
                            a, b = gab_wh[:, 16 * k:16 * k + 16], gab_wl[:, 16 * k:16 * k + 16]
                            ins = three(STAT[:, 16 * t:16 * t + 16], h_hi[:, k, tok], h_lo[:, k, tok], a, b,
                                        k == 0 and t == 0, k == KD - 1)
                    ins.then_inc(s.gab_ready, 1)
                    pe.wait_ge(s.t5_loaded, 48)
                    mm(B[1][0:16, 0:384], rb[:, :], oh, True, True).then_inc(s.t5_psum, 1)
                if w == 3:
                    pe.wait_ge(s.gate_done, 1)
                    for t in range(TT):
                        mm(STAT[:, 32 + 8 * t:40 + 8 * t], tri, g[:, 8 * t:8 * t + 8], True, True)
                    mm(STAT[:, 48:56], ones.broadcast_to([P, P]), g[:, 0:8], True, True).then_inc(s.cum_ready, 1)

            def before(name):
                u = BIG_INDEX[name] - 3
                if u >= 0:
                    who = BIG_LIST[u][1]
                    pe.wait_ge(s.big_read_dve if who == "dve" else s.big_read_act, big_reads(u, who))

            def filled(name, ins):
                ins.then_inc(s.big_ready, 1)

            def rows(name, coef, tiles, rhs=ident, tts=range(TT), width=T):
                before(name)
                for i, tile in enumerate(tiles):
                    for par in range(2):
                        for n, t in enumerate(tts):
                            col = coef(2 * tile + par, t)
                            ins = mm(big(name)[64 * par:64 * par + 64, width * i + P * n:width * i + P * n + P],
                                     col.broadcast_to([P, HD]), rhs, True, True)
                filled(name, ins)

            def by_token(name, src, t):
                before(name)
                for i in range(4):
                    ins = pe.transpose(big(name)[:, P * i:P * i + P], src[:, i, P * t:P * t + P], ident)
                filled(name, ins)

            def decay(gi):
                before(f"G{gi}")
                for i in range(4):
                    col = 8 * (gi // 2) + 2 * i + gi % 2
                    ins = mm(big(f"G{gi}")[:, P * i:P * i + P], g[:, col:col + 1].broadcast_to([P, P]), tri, True, True)
                filled(f"G{gi}", ins)

            def products(kind, m, gi):
                t, r = gi // 2, slice(64 * (gi % 2), 64 * (gi % 2) + 64)
                before(f"{kind}{gi}")
                for i in range(4):
                    ins = mm(big(f"{kind}{gi}")[:, P * i:P * i + P], kT[r, i, P * t:P * t + P], m[r, i, P * t:P * t + P], True, True)
                filled(f"{kind}{gi}", ins)

            at = lambda c: (lambda h, t: c[:, 8 * t + h:8 * t + h + 1])
            project(6)
            pe.wait_ge(s.head_squared, 4)
            pe.wait_ge(s.decay_dve, 1)
            for w in range(4):
                ins = head_sums(lambda i, t: head_sq[w][:, 256 * i + P * t:256 * i + P * t + P], 2, 64 + 4 * w, 16)
            ins.then_inc(s.head_sums, 1)
            project(7)
            pe.wait_ge(s.coef_ready, 2)
            pe.wait_ge(s.t5_row, 1)
            rows("kb01", at(coefk), (0, 1))
            rows("kb23", at(coefk), (2, 3))
            rows("q01", at(coefq), (0, 1))
            project(8)
            rows("q23", at(coefq), (2, 3))
            rows("eg", at(g), range(4), rhs=tri, tts=(1,), width=P)
            pe.wait_ge(s.feature_ready, 6)
            by_token("v0", vT, 0)
            project(9)
            by_token("v1", vT, 1)
            by_token("kt", kT, 0)
            for gi in range(3):
                decay(gi)
            wait_bank(10)
            pe.wait_ge(s.lo_ready, 11)
            wh = w_hi[:, 10 % RING, :].rearrange("p (k c) -> p k c", k=KD)
            wl = w_lo[:, 10 % RING, :].rearrange("p (k c) -> p k c", k=KD)
            for k in range(KD):
                three(A[2][:, 0:256], wh[:, k, 0:P], wl[:, k, 0:P], h_hi[:, k, :], h_lo[:, k, :], k == 0, k == KD - 1)
            for t in range(TT):
                tok = slice(P * t, P * t + P)
                for k in range(KD):
                    ins = three(A[2][:, 256 + P * t:256 + P * t + P], h_hi[:, k, tok], h_lo[:, k, tok],
                                wh[:, k, P:2 * P], wl[:, k, P:2 * P], False, k == KD - 1)
            ins.then_inc(s.block_used, 1)

            decay(3)
            for gi in range(4):
                products("kk", kbT, gi)
            pe.wait_ge(s.head_squared, 7)
            pe.wait_ge(s.head_inv, 1)
            for w in range(4, 7):
                ins = head_sums(lambda i, t: head_sq[w][:, 256 * i + P * t:256 * i + P * t + P],
                                2 if w < 6 else 1, 96 + 4 * (w - 4), 10)
            ins.then_inc(s.head_sums, 1)
            for gi in range(4):
                products("qk", qT, gi)
            pe.wait_ge(s.head_rms, 2)
            sat = lambda h, t: ss[:, 2, 10 * t + h:10 * t + h + 1]
            rows("sk", sat, (4,))
            rows("sq01", sat, (0, 1))
            rows("sq23", sat, (2, 3))
            for gi in range(4):
                if gi < 3:
                    before(f"tr{gi}")
                else:
                    pe.wait_ge(s.x_copied, 1)
                pe.wait_ge(s.xt_ready, gi + 1)
                for i in range(4):
                    ins = pe.transpose(big(f"tr{gi}")[:, P * i:P * i + P], XT[:, gi, P * i:P * i + P], ident)
                ins.then_inc(s.xtr_ready, 1)

            def scores(a, bank, q, k):
                for hh in range(4):
                    r = slice(64 * (hh % 2), 64 * (hh % 2) + 64)
                    if a > 0:
                        pe.wait_ge(s.ptrans_copied, 4 * a - 4 + hh + 1)
                        if a == 1 and hh == 0:
                            pe.wait_ge(s.pv_lo, a)
                    mm(bank[hh][:, 0:256], q(hh // 2)[r, P:T], k(hh // 2)[r, 0:T], True, True)
                    mm(bank[hh][:, 256:384], q(hh // 2)[r, 0:P], k(hh // 2)[r, 0:P], True, True).then_inc(s.scores_ready, 1)

            def transposes(a, bank, sc, perm):
                for hh in range(4):
                    pe.wait_ge(s.probs_ready, 8 * a + 2 * hh + 2)
                    for i in range(3):
                        ins = pe.transpose(bank[hh][:, P * i:P * i + P], sc[:, hh, P * i:P * i + P], perm)
                    ins.then_inc(s.ptrans_ready, 1)

            def values(a, bank, pT, v, out=None):
                out = bank[0] if out is None else out
                if a > 2:
                    pe.wait_ge(s.pv_lo, a)
                elif a == 2:
                    pe.wait_ge(s.v_scaled, TT)
                for hh in range(4):
                    pe.wait_ge(s.ptrans_copied, 4 * a + hh + 1)
                    o = out[64 * (hh % 2):64 * (hh % 2) + 64, 256 * (hh // 2):256 * (hh // 2) + 256]
                    mm(o[:, 0:P], v(0, hh), pT[:, hh, 256:384], True, True)
                    mm(o[:, P:T], v(0, hh), pT[:, hh, 0:P], True, False)
                    ins = mm(o[:, P:T], v(1, hh), pT[:, hh, P:2 * P], False, True)
                ins.then_inc(s.pv_ready, 1)

            swa_q = lambda a: (lambda i: qs[:, 2 * a + i, :])
            swa_k = lambda i: ks[:, :]
            swa_v = lambda t, hh: vs[:, t, 64 * (hh % 2):64 * (hh % 2) + 64]
            pe.wait_ge(s.big_read_dve, big_reads(BIG_INDEX["sq23"], "dve"))
            pe.wait_ge(s.proj_evac, 6)
            scores(0, A, swa_q(0), swa_k)

            for l in range(1, NEXP + 1):
                for gi in range(4):
                    pe.wait_ge(s.b_ready, 4 * (l - 1) + gi + 1)
                    pe.wait_ge(s.x_copied, 4 if l == 1 else 4 * (l - 1) + gi + 1)
                    for i in range(4):
                        c = slice(P * i, P * i + P)
                        ins = mm(B[gi][:, c], Bm[:, gi, c], X[:, gi, c], True, True)
                    ins.then_inc(s.p_ready, 1)
                for gi in range(4):
                    pe.wait_ge(s.p_copied, 4 * (l - 1) + gi + 1)
                    for i in range(4):
                        c = slice(P * i, P * i + P)
                        ins = mm(B[gi][:, c], Pm[:, gi, c], XT[:, gi, c], True, True)
                    ins.then_inc(s.qt_ready, 1)
                if l < NEXP:
                    for gi in range(4):
                        pe.wait_ge(s.xt_ready, 4 * l + gi + 1)
                        for i in range(4):
                            c = slice(P * i, P * i + P)
                            ins = pe.transpose(B[gi][:, c], XT[:, gi, c], ident)
                        ins.then_inc(s.xtr_ready, 1)
                if l == 2:
                    transposes(0, A, sc1, ident)
                    values(0, A, pT1, swa_v)
                    scores(1, A, swa_q(1), swa_k)
                if l == 5:
                    transposes(1, A, sc1, ident)
            pe.wait_ge(s.ptrans_copied, 8)
            modulation(1)
            values(1, A, pT1, swa_v)
            pe.wait_ge(s.mod_ready, 2)
            pe.wait_ge(s.pv_lo, 2)
            row_block(W_OUT, h_hi, h_lo, 4, first=True)
            pe.wait_ge(s.xt_ready, 4 * (NEXP + 1))
            pe.wait_ge(s.big_read_dve, big_reads(BIG_INDEX["kt"], "dve"))
            inv_of = lambda h, t: XT[:, 2 * t + h % 2, P * (h // 2):P * (h // 2) + P]
            qk_of = lambda h, t: qkT[:, 2 * t + h % 2, P * (h // 2):P * (h // 2) + P]
            for h in range(8):
                e = slice(HD * h, HD * h + HD)
                ins = mm(B[0][:, e], inv_of(h, 0), vb[:, 0, e], True, True)
            ins.then_inc(s.u_ready, 1)
            row_block(W_OUT + 1, h_hi, h_lo, 6)
            pe.wait_ge(s.u_copied, 1)
            for h in range(8):
                r = slice(64 * (h % 2), 64 * (h % 2) + 64)
                e = slice(HD * h, HD * h + HD)
                ins = mm(B[1][r, HD * (h // 2):HD * (h // 2) + HD], kd[:, e], u0[:, e], True, True)
            ins.then_inc(s.s_ready, 1)
            for h in range(8):
                r = slice(64 * (h % 2), 64 * (h % 2) + 64)
                ins = mm(B[2 + h % 2][r, P * (h // 2):P * (h // 2) + P], u0[:, HD * h:HD * h + HD], qk_of(h, 0), True, True)
            ins.then_inc(s.o0_ready, 1)
            pe.wait_ge(s.s_copied, 1)
            for par in range(2):
                r = slice(64 * par, 64 * par + 64)
                for i in range(4):
                    ins = mm(B[par][:, HD * i:HD * i + HD], kbgT[r, i, :], S1[r, HD * i:HD * i + HD], True, True)
            ins.then_inc(s.r_ready, 1)
            pe.wait_ge(s.r_done, 2)
            for h in range(8):
                e = slice(HD * h, HD * h + HD)
                ins = mm(B[0][:, e], inv_of(h, 1), r1[:, e], True, True)
            ins.then_inc(s.vn_ready, 1)
            pe.wait_ge(s.vn_copied, 1)
            for h in range(8):
                r = slice(64 * (h % 2), 64 * (h % 2) + 64)
                i = h // 2
                o = B[h % 2][r, P * i:P * i + P]
                mm(o, vn[:, HD * h:HD * h + HD], qk_of(h, 1), True, False)
                ins = mm(o, S1[r, HD * i:HD * i + HD], qdT[r, i, :], False, True)
            ins.then_inc(s.o1_ready, 1)
            pe.wait_ge(s.o_squared, 1)
            for t in range(TT):
                for i in range(4):
                    ins = mm(B[2][:, 8 * t + 2 * i:8 * t + 2 * i + 2], osq[:, i, P * t:P * t + P], headsel, True, True)
            ins.then_inc(s.o_sums, 1)
            pe.wait_ge(s.o_rms, 1)
            for j in range(2):
                for i in range(2):
                    for par in range(2):
                        for t in range(TT):
                            h = 2 * (2 * j + i) + par
                            ins = mm(B[j][64 * par:64 * par + 64, T * i + P * t:T * i + P * t + P],
                                     os_[:, 2, 8 * t + h:8 * t + h + 1].broadcast_to([P, HD]), ident, True, True)
                ins.then_inc(s.o_rows, 1)
            pe.wait_ge(s.o_lo_done, 1)
            row_block(W_OUT + 2, h_hi, h_lo, 0)
            pe.wait_ge(s.o_lo_done, 2)
            modulation(2)
            row_block(W_OUT + 3, h_hi, h_lo, 2, n=1)

            def ffn(f):
                F, n = FFN_BASE[f], 2 * f + 1
                if not f:
                    norm(n)
                column_block(F, B[0], n=n)
                if f:
                    sums(n)
                pe.wait_ge(s.pool_zeroed, 1)
                for i in range(4):
                    mm(A[i], zero_r[:, 0:P], zero_r[:, :], True, True)
                column_block(F + 1, B[1], halfway=(lambda: rstd(n)) if f else None)

                def body(j, it):
                    if f:
                        pe.wait_ge(s.gate_scaled, j + JF * (f - 1))
                    else:
                        pe.wait_ge(s.silu_ready, j)
                    column_block(F + 2, B[0], it)
                    pe.wait_ge(s.hid_ready, j + JF * f)
                    column_block(F + 3, B[1], it)
                    pe.wait_ge(s.hid_lo_ready, j + JF * f)
                    row_block(F + 4, hid_hi, hid_lo, 0, it)

                with pe.Fori(1, JF - 1) as j:
                    body(j, j - 1)
                body(JF - 1, JF - 2)
                pe.wait_ge(s.hid_lo_ready, JF * f + JF)
                row_block(F + 32, *last_hid, 0, n=2 * f + 2)

            ffn(0)
            for i in range(4):
                w = CONV_BASE + 3 * i
                if i >= 2:
                    pe.wait_ge(s.by_ready, i - 1)
                column_block(w, conv_banks[i % 2][0], n=2 if i == 0 else None)
                if i == 0:
                    sums(2)
                column_block(w + 1, conv_banks[i % 2][1], halfway=(lambda: rstd(2)) if i == 0 else None)
                column_block(w + 2, conv_banks[i % 2][2])
            for i in range(4):
                if i == 0:
                    pe.wait_ge(s.by_ready, 3)
                pe.wait_ge(s.by_lo, i + 1)
                row_block(CONV_OUT + i, o_hi, o_lo, 2 * i, first=i == 0, n=3 if i == 3 else None)
            ffn(1)
            dil_q = lambda b: (lambda t: q2[:, b, t, :])
            dil_k = lambda b: (lambda t: k2[:, b, t, :])
            dil_v = lambda b: (lambda t, hh: v2[:, b, t, HD * hh:HD * hh + HD])
            for i in range(5):
                w, a, b = QKV_BASE + 3 * i, i + 1, (i - 1) % 2
                if i:
                    pe.wait_ge(s.qk_scaled, 3 * i)
                    scores(a, B, dil_q(b), dil_k(b))
                if i < 4:
                    column_block(w, A[0], n=4 if i == 0 else None)
                    if i == 0:
                        sums(4)
                    column_block(w + 1, A[1], halfway=(lambda: rstd(4)) if i == 0 else None)
                    pe.wait_ge(s.lo_ready, w + 3)
                    if i:
                        pe.wait_ge(s.v_scaled, TT * i)
                    wh = w_hi[:, (w + 2) % RING, :].rearrange("p (k c) -> p k c", k=KD)
                    wl = w_lo[:, (w + 2) % RING, :].rearrange("p (k c) -> p k c", k=KD)
                    for t in range(TT):
                        tok = slice(P * t, P * t + P)
                        for k in range(KD):
                            ins = three(A[2][:, 256 * t:256 * t + 256], h_hi[:, k, tok], h_lo[:, k, tok], wh[:, k, :], wl[:, k, :],
                                        k == 0 and t == 0, k == KD - 1)
                    ins.then_inc(s.block_used, 1)
                else:
                    pe.wait_ge(s.v_scaled, TT * i)
                    row_block(ATT_OUT, o_hi, o_lo, 0, first=True,
                              before_last=lambda: pe.wait_ge(s.pv_lo, 5))
                    row_block(ATT_OUT + 1, o_hi, o_lo, 2)
                if i:
                    transposes(a, B, sc2, const("flip"))
                    values(a, B, pT2, dil_v(b), out=A[3] if i < 4 else B[0])
            row_block(ATT_OUT + 2, o_hi, o_lo, 4)
            pe.wait_ge(s.pv_lo, 6)
            row_block(ATT_OUT + 3, o_hi, o_lo, 6, n=5)
            ffn(2)
            norm(6)


def shape_constants():
    c = np.zeros((P, N_CONST), np.float32)
    i, j = np.arange(P)[:, None], np.arange(P)[None, :]
    c[:, slice(*C_AT["ident"])] = i == j
    c[:, slice(*C_AT["flip"])] = i + j == P - 1
    c[:, slice(*C_AT["tri"])] = i <= j
    c[:, slice(*C_AT["future"])] = np.where(j >= i, 0.0, -BIG)
    for l in range(NEXP + 1):
        b = 1 << l
        m = (i // (2 * b) == j // (2 * b)) & ((i // b) % 2 == 0) & ((j // b) % 2 == 1)
        c[:, C_AT["levels"][0] + P * l:C_AT["levels"][0] + P * (l + 1)] = m
    c[:, C_AT["headsel"][0]] = np.arange(P) < 64
    c[:, C_AT["headsel"][0] + 1] = np.arange(P) >= 64
    c[:, C_AT["ones"][0]] = 1.0
    k = np.arange(256)[None, :]
    dist = i + 128 - k
    table = np.where((dist >= 0) & (dist < 128), -dist, -BIG)
    c[:, C_AT["alibi"][0]:C_AT["alibi"][1]] = np.concatenate([table, table[:, 128:]], 1)
    return c


def t5_constants():
    d = 255 - np.arange(384)
    exact = 16
    df = np.maximum(d, 1).astype(np.float32)
    large = exact + (np.log(df / np.float32(exact)) / np.float32(np.log(2048 / exact)) * np.float32(32 - exact)).astype(np.int32)
    bucket = np.where(d < exact, np.maximum(d, 0), np.minimum(large, 31))
    onehot = (np.arange(32)[:, None] == bucket[None, :]).astype(np.float32)
    n = ((d >= 0) & (d <= 128)).astype(int) + ((d >= 0) & (d % 4 == 0)) + ((d >= 0) & (d % 16 == 0))
    log = np.where(n > 0, np.log(np.maximum(n, 1)), -BIG).astype(np.float32)
    return onehot, np.ascontiguousarray(np.broadcast_to(log, (16, 384)))


def lay_out(v):
    def cols(w, at):
        return w[:, at].reshape(KD, P, 256).transpose(1, 0, 2).reshape(P, BLOCK)

    def rows(w, at):
        return w[at].reshape(2, P, D).transpose(1, 0, 2).reshape(P, BLOCK)

    def chunk(a):
        return a.reshape(-1, P).T

    r = np.arange
    w_in, w_out, ada = v["w_in"][0], v["w_out"][0], v["w_ada"][0]
    pair = np.concatenate([np.concatenate([r(64) + 64 * j, r(64) + 64 * (4 + j)]) for j in range(4)])
    starts = [512, 768, 0, 256, 1024, 1280, 1536, 1792]
    w = [cols(w_in, r(a, a + 256)) for a in starts]
    w += [cols(w_in, 2064 + pair[0:256]), cols(w_in, 2064 + pair[256:512]), cols(w_in, r(2576, 2832))]
    w += [rows(w_out, 512 + pair[0:256]), rows(w_out, 512 + pair[256:512]), rows(w_out, r(256)), rows(w_out, r(256, 512))]

    def swiglu(wg, wu, wd):
        out = []
        for j in range(JF + 1):
            if j < JF:
                out += [cols(wg, r(256 * j, 256 * j + 256)), cols(wu, r(256 * j, 256 * j + 256))]
            if j:
                out.append(rows(wd, r(256 * j - 256, 256 * j)))
        return out

    def mixer(w1, w2):
        out = [cols(w1, r(D * j + 256 * i, D * j + 256 * i + 256)) for i in range(4) for j in range(3)]
        return out + [rows(w2, r(256 * i, 256 * i + 256)) for i in range(4)]

    w += swiglu(v["w_gate"][0], v["w_up"][0], v["w_down"][0])
    w += mixer(v["conv_w_in_2"][0], v["conv_w_out_2"][0])
    w += swiglu(v["ffn_w_gate_2"][0], v["ffn_w_up_2"][0], v["ffn_w_down_2"][0])
    w += mixer(v["attn_w_qkv_2"][0], v["attn_w_out_2"][0])
    w += swiglu(v["ffn_w_gate_2"][1], v["ffn_w_up_2"][1], v["ffn_w_down_2"][1])
    assert len(w) == N_WEIGHTS
    stream = [None] * (N_WEIGHTS + MOD_TOTAL)
    for n, b in enumerate(w):
        stream[raw_index(n)] = b
    for m in range(MOD_TOTAL):
        k, part = m % MOD_BLOCKS, m // MOD_BLOCKS
        stream[mod_index(m)] = ada[P * k:P * k + P, BLOCK * part:BLOCK * part + BLOCK]

    vec = np.zeros((P, N_VEC), np.float32)

    def put(name, a):
        vec[:, slice(*V_AT[name])] = a

    put("c", chunk(v["c"][0]))
    for name, a in (("norm1", v["norm1_w"][0]), ("norm2", v["norm2_w"][0]), ("mix0", v["mix_norm_2"][0]),
                    ("mix1", v["mix_norm_2"][1]), ("ffn0", v["ffn_norm_2"][0]), ("ffn1", v["ffn_norm_2"][1]),
                    ("final", v["final_norm_2"]), ("b_ada", v["b_ada"][0])):
        put(name, chunk(a))
    put("conv_w", v["conv_w"][0, :, 0, :].reshape(4, 12, P).transpose(2, 1, 0).reshape(P, 48))
    put("conv_k", v["conv_kernel_2"][0].reshape(3, KD, P).transpose(2, 1, 0).reshape(P, 24))
    for name, a in (("gdn_w", v["gdn_norm_w"][0]), ("qn_w", v["q_norm_w"][0]), ("kn_w", v["k_norm_w"][0])):
        put(name, np.tile(a, 2)[:, None])
    put("dt_bias", v["dt_bias"][0][None, :])
    put("a_log", v["a_log"][0][None, :])
    put("sinks", v["sinks"][0][[2 * a + hh // 2 + 4 * (hh % 2) for a in range(2) for hh in range(4)]][None, :])
    onehot, log = t5_constants()
    return {
        "stream": np.stack(stream),
        "x_in": v["x"][0].T.reshape(KD, P, T).transpose(1, 0, 2),
        "consts_in": shape_constants(),
        "vectors_in": vec,
        "gab_in": w_in[:, 2048:2064].reshape(KD, P, 16).transpose(1, 0, 2).reshape(P, KD * 16),
        "t5_onehot": onehot,
        "t5_log": log,
        "rel_bias": v["rel_bias_2"],
    }


def kernel(**inputs):
    import concourse.bacc as bacc
    from concourse.bass_utils import run_bass_kernel_spmd

    nc = bacc.Bacc("TRN2", target_bir_lowering=False, num_devices=1)
    arrays = {k: np.ascontiguousarray(a) for k, a in lay_out({k: np.asarray(a) for k, a in inputs.items()}).items()}
    args = {k: nc.dram_tensor(k, a.shape, mybir.dt.from_np(a.dtype), kind="ExternalInput").ap() for k, a in arrays.items()}
    out = nc.dram_tensor("out", (P, KD, T), F32, kind="ExternalOutput").ap()
    build(nc, out=out, **args)
    r = run_bass_kernel_spmd(nc, [arrays], core_ids=[0])
    y = r.results[0]["out"]
    return np.ascontiguousarray(y.transpose(1, 0, 2).reshape(D, T).T)[None]
```

```python
from contextlib import ExitStack

import numpy as np
import concourse.bass as bass
from concourse import mybir

F32, F32R = mybir.dt.float32, mybir.dt.float32r
ALU, ACT, AX = mybir.AluOpType, mybir.ActivationFunctionType, mybir.AxisListType

P = 128
T = 256
TT = T // P
D = 1024
KD = D // P
FF = 2816
JF = FF // 256
HD = 64
EPS = 1e-6
BIG = 1e30
BLOCK = 2048
RING = 3
PER_LEVEL = (2, 2, 1, 1, 2, 1)
OUTPUT_BLOCKS = 5
WARM_MOD, WARM_NORM0, WARM_NORM1 = 16, 12, 6
LATE = (2, 3, 4, 5)
NEXP = 6

W_IN, W_OUT = 0, 11
FFN_BASE = [15, 64, 113]
CONV_BASE, CONV_OUT = 48, 60
QKV_BASE, ATT_OUT = 97, 109
N_WEIGHTS = 146
MOD_START = (0, 8, 16, 20, 24)
MOD_COLS = (0, 2048, 4096, 5120)
MOD_TOTAL = MOD_START[-1]
LOOP_W = 14
FIRST_STEP, LAST_STEP = FFN_BASE[0] + 3, FFN_BASE[0] + 31
MOD_AT = ((0, 8), (LOOP_W, 12), (FIRST_STEP, 1), (LAST_STEP, 2), (LAST_STEP + 1, 1))


def raw_index(w):
    return w + sum(n for at, n in MOD_AT if at <= w)


STREAM_ORDER = [(raw_index(w), "w", w) for w in range(N_WEIGHTS)]
STREAM_ORDER += list(zip([r for r in range(N_WEIGHTS + MOD_TOTAL) if r not in {q for q, _, _ in STREAM_ORDER}],
                         ["mod"] * MOD_TOTAL, range(MOD_TOTAL)))
STREAM_ORDER.sort()


def mod_index(m):
    return next(r for r, kind, n in STREAM_ORDER if kind == "mod" and n == m)


CONSTS = dict(ident=P, headsel=2, ones=1, flip=P, tri=P, future=P, levels=(NEXP + 1) * P, alibi=384)
VECS = dict(c=8, norm1=8, norm2=8, mix0=8, mix1=8, ffn0=8, ffn1=8, final=8, b_ada=48, conv_w=48,
            conv_k=24, gdn_w=1, qn_w=1, kn_w=1, dt_bias=8, a_log=8, sinks=8)


def columns(spec):
    out, at = {}, 0
    for name, n in spec.items():
        out[name] = (at, at + n)
        at += n
    return out, at


C_AT, N_CONST = columns(CONSTS)
N_FIRST = C_AT["ones"][1]
V_AT, N_VEC = columns(VECS)


BIG_LIST = [(n, "dve") for n in ("kb01", "kb23", "q01", "q23")] + [("eg", "act")] \
    + [(n, "dve") for n in ["v0", "v1", "kt"] + [f"{u}{gi}" for u in ("G", "kk", "qk") for gi in range(4)]
       + ["sk", "sq01", "sq23"]] + [(f"tr{gi}", "act") for gi in range(4)]
BIG_INDEX = {n: i for i, (n, _) in enumerate(BIG_LIST)}


def big_reads(upto, engine):
    return sum(e == engine for _, e in BIG_LIST[:upto + 1])


class Semaphores:

    def __init__(self, new):
        self.x_loaded = new("x_loaded")
        self.vectors_loaded = new("vectors_loaded")
        self.consts_loaded = new("consts_loaded")
        self.masks_loaded = new("masks_loaded")
        self.gab_loaded = new("gab_loaded")
        self.t5_loaded = new("t5_loaded")
        self.t5_stored = new("t5_stored")
        self.tables_loaded = new("tables_loaded")
        self.out_stored = new("out_stored")
        self.pool_zeroed = new("pool_zeroed")
        self.c_act = new("c_act")
        self.mod_accumulated = new("mod_accumulated")
        self.mod_summed = new("mod_summed")
        self.mod_ready = new("mod_ready")
        self.dve_step = new("dve_step")
        self.act_step = new("act_step")
        self.hi_ready = new("hi_ready")
        self.lo_ready = new("lo_ready")
        self.block_used = new("block_used")
        self.acc_tile_done = new("acc_tile_done")
        self.x_ready = new("x_ready")
        self.squared = new("squared")
        self.sumsq_ready = new("sumsq_ready")
        self.squares_added = new("squares_added")
        self.inv_ready = new("inv_ready")
        self.rms_ready = new("rms_ready")
        self.rstd_ready = new("rstd_ready")
        self.t_ready = new("t_ready")
        self.h_hi_ready = new("h_hi_ready")
        self.h_lo_ready = new("h_lo_ready")
        self.gab_hi = new("gab_hi")
        self.gab_lo = new("gab_lo")
        self.gab_product = new("gab_product")
        self.gab_copied = new("gab_copied")
        self.gab_ready = new("gab_ready")
        self.gate_exp = new("gate_exp")
        self.gate_dve = new("gate_dve")
        self.gate_done = new("gate_done")
        self.cum_ready = new("cum_ready")
        self.decay_dve = new("decay_dve")
        self.decay_act = new("decay_act")
        self.proj_evac = new("proj_evac")
        self.pad_ready = new("pad_ready")
        self.conv_done = new("conv_done")
        self.feature_ready = new("feature_ready")
        self.head_squared = new("head_squared")
        self.head_sums = new("head_sums")
        self.head_inv = new("head_inv")
        self.head_rms = new("head_rms")
        self.coef_ready = new("coef_ready")
        self.big_ready = new("big_ready")
        self.big_read_dve = new("big_read_dve")
        self.big_read_act = new("big_read_act")
        self.d_shifted = new("d_shifted")
        self.d_ready = new("d_ready")
        self.d_normed = new("d_normed")
        self.x_masked = new("x_masked")
        self.b_ready = new("b_ready")
        self.xt_ready = new("xt_ready")
        self.x_copied = new("x_copied")
        self.x_updated = new("x_updated")
        self.p_ready = new("p_ready")
        self.p_copied = new("p_copied")
        self.qt_ready = new("qt_ready")
        self.xtr_ready = new("xtr_ready")
        self.row_scaled = new("row_scaled")
        self.u_ready = new("u_ready")
        self.u_copied = new("u_copied")
        self.s_ready = new("s_ready")
        self.s_copied = new("s_copied")
        self.o0_ready = new("o0_ready")
        self.o_copied = new("o_copied")
        self.r_ready = new("r_ready")
        self.r_done = new("r_done")
        self.vn_ready = new("vn_ready")
        self.vn_copied = new("vn_copied")
        self.o1_ready = new("o1_ready")
        self.o_squared = new("o_squared")
        self.o_sums = new("o_sums")
        self.o_inv = new("o_inv")
        self.o_rms = new("o_rms")
        self.o_rows = new("o_rows")
        self.o_gated = new("o_gated")
        self.o_hi_done = new("o_hi_done")
        self.o_lo_done = new("o_lo_done")
        self.v_transposed = new("v_transposed")
        self.v_ready = new("v_ready")
        self.scores_ready = new("scores_ready")
        self.scores_biased = new("scores_biased")
        self.negmax_ready = new("negmax_ready")
        self.exp_ready = new("exp_ready")
        self.probs_ready = new("probs_ready")
        self.ptrans_ready = new("ptrans_ready")
        self.ptrans_copied = new("ptrans_copied")
        self.pv_ready = new("pv_ready")
        self.pv_hi = new("pv_hi")
        self.pv_lo = new("pv_lo")
        self.silu_ready = new("silu_ready")
        self.hid_ready = new("hid_ready")
        self.hid_hi_ready = new("hid_hi_ready")
        self.hid_lo_ready = new("hid_lo_ready")
        self.cu_ready = new("cu_ready")
        self.by_ready = new("by_ready")
        self.by_hi = new("by_hi")
        self.by_lo = new("by_lo")
        self.row_copied = new("row_copied")
        self.gate_scaled = new("gate_scaled")
        self.gated = new("gated")
        self.qk_scaled = new("qk_scaled")
        self.v_scaled = new("v_scaled")
        self.t5_psum = new("t5_psum")
        self.t5_row = new("t5_row")


def build(nc, stream, x_in, consts_in, vectors_in, gab_in, t5_onehot, t5_log, rel_bias, out):
    t5_scratch = nc.dram_tensor("t5_scratch", (16, 384), F32, kind="Internal")
    with ExitStack() as ctx:
        s = Semaphores(lambda name: ctx.enter_context(nc.semaphore(name)))
        raw_landed = [ctx.enter_context(nc.semaphore(f"raw_landed{i}")) for i in range(RING)]

        def sb(name, shape, dt=F32, stack=ctx):
            return stack.enter_context(nc.sbuf_tensor(name, shape, dt))

        raw = sb("raw", [P, RING, BLOCK])
        w_hi = sb("w_hi", [P, RING, BLOCK], F32R)
        w_lo = sb("w_lo", [P, RING, BLOCK], F32R)
        x = sb("x_res", [P, KD, T])
        nt = sb("norm_tmp", [P, KD, T])
        h_hi = sb("h_hi", [P, KD, T], F32R)
        h_lo = sb("h_lo", [P, KD, T], F32R)
        zero_r = sb("zero_r", [P, 512], F32R)
        consts = sb("consts", [P, N_CONST])
        vec = sb("vec", [P, N_VEC])
        c_act = sb("c_act_sb", [P, 8])
        mods = sb("mods", [P, 48])
        a1 = sb("a1", [P, 8])
        a2 = sb("a2", [P, 8])
        qk_w = sb("qk_w", [P, 1])
        root_tmp = sb("root_tmp", [P, 1])
        rrow = sb("rms_row", [P, T])
        rrow2 = sb("rms_row_squared", [P, T])
        ms = sb("ms", [P, TT])
        inv = sb("inv", [P, TT])
        rms = sb("rms", [P, TT])
        soft = sb("soft", [P, 6, 8])
        sink2 = sb("sink2", [P, 8, 2])

        def const(name):
            a, b = C_AT[name]
            return consts[:, a:b]

        def vecs(name):
            a, b = V_AT[name]
            return vec[:, a:b]

        ident, tri, future, headsel, ones = (const(n) for n in ("ident", "tri", "future", "headsel", "ones"))
        level_mask = [consts[:, C_AT["levels"][0] + P * i:C_AT["levels"][0] + P * (i + 1)] for i in range(NEXP + 1)]

        with ExitStack() as one:
            def p1(name, shape, dt=F32):
                return sb(name, shape, dt, one)
            kqb = p1("keys_queries", [P, 12, T])
            zT = p1("zT", [P, 4, T])
            kbgT, qdT = (p1(n, [P, 4, P]) for n in ("kbgT", "qdT"))
            kd = p1("kd", [P, 512])
            vb = p1("vb", [P, TT, 512])
            AT, X, qkT, XT = (p1(n, [P, 4, 4 * P]) for n in ("AT", "X_inv", "qkT", "XT"))
            inv_b = p1("inv_b", [P, 4 * 4 * P])
            inv_p = p1("inv_p", [P, 4 * 4 * P])
            qs = p1("qs", [P, 4, T])
            ks = p1("ks", [P, T])
            vs = p1("vs", [P, TT, P])
            pT1 = p1("probsT1", [P, 4, 384])
            gab_w = p1("gab_w", [P, KD * 16])
            gab_wh = p1("gab_wh", [P, KD * 16], F32R)
            gab_wl = p1("gab_wl", [P, KD * 16], F32R)
            gt = p1("gate_tmp", [P, 8, TT * 8])
            beta, g, Gs, coefk, coefq = (p1(n, [P, TT * 8]) for n in ("beta", "g", "Gs", "coefk", "coefq"))
            kds = p1("kds", [P, 2, 8])
            hs = p1("head_stat", [P, 3, TT * 16])
            ss = p1("swa_stat", [P, 3, TT * 10])
            os_ = p1("out_stat", [P, 3, TT * 8])
            rb = p1("rel_bias_sb", [32, 16])
            t5r = p1("t5_row_sb", [16, 384])
        sc1 = nt[:, 0:6, :].rearrange("p a b -> p (a b)").rearrange("p (h c) -> p h c", h=4)
        eg = pT1[:, :, :].rearrange("p a b -> p (a b)")[:, 0:512].rearrange("p (a b) -> p a b", a=4)
        flat = lambda b: b.rearrange("p a b -> p (a b)")
        mod_accs = [inv_b[:, :], flat(kqb[:, 0:8, :]), flat(kqb[:, 8:12, :]), None]
        gabT, swa_vT = pT1[0:16, 3, 0:T], pT1[:, 3, 0:T]
        oh = XT[0:32, 2, 0:384]
        t5l = XT[0:16, 3, 0:384]
        DT = X
        kT, qT, kbT = kqb[:, 0:4, :], kqb[:, 4:8, :], kqb[:, 8:12, :]
        head_sq = [X[:, w, :] for w in range(4)] + [qkT[:, w, :] for w in range(3)]
        vT = inv_p[:, 0:1024].rearrange("p (a b) -> p a b", a=4)
        pad = inv_p[:, 1024:1024 + 2 * 259].rearrange("p (a b) -> p a b", a=2)
        cacc = XT[:, 0, :]
        u0, vn, r1 = inv_b[:, 0:512], inv_b[:, 512:1024], inv_b[:, 1024:1536]
        S1 = inv_b[:, 1536:1792]
        oT = inv_p[:, 0:1024].rearrange("p (a b) -> p a b", a=4)
        osq = inv_p[:, 1024:2048].rearrange("p (a b) -> p a b", a=4)
        Bm = inv_b[:, :].rearrange("p (g c) -> p g c", g=4)
        Pm = inv_p[:, :].rearrange("p (g c) -> p g c", g=4)

        t5 = sb("t5_tables", [P, 16, 384])
        o_hi = sb("o_hi", [P, KD, T], F32R)
        o_lo = sb("o_lo", [P, KD, T], F32R)
        hid_hi = sb("hid_hi", [P, 2, T], F32R)
        hid_lo = sb("hid_lo", [P, 2, T], F32R)
        sg = sb("silu_gate", [P, 2 * T])
        hid = sb("hid", [P, 2 * T])
        c_sb = sb("c_sb", [P, 2 * T])
        cu = sb("cu_pad", [P, 2, T + 2])
        yb = sb("y_conv", [P, 2, T])
        q2 = sb("q2", [P, 2, 2, T])
        k2 = sb("k2", [P, 2, 2, T])
        v2 = sb("v2", [P, 2, TT, 256])
        sc2 = sb("scores2", [P, 4, 384])
        pT2 = sb("probsT2", [P, 4, 384])

        mod_accs[3] = flat(sc2[:, :, :])[:, 0:BLOCK // 2]
        acc = ctx.enter_context(nc.psum_tensor("acc", [P, 2048], F32))
        A = [acc[:, 512 * i:512 * (i + 1)] for i in range(4)]
        B = [ctx.enter_context(nc.psum_tensor(f"bank{i}", [P, 512], F32)) for i in range(4, 8)]
        STAT = B[2]
        mod_bank = [STAT, B[3], B[2], B[2]]
        conv_banks = [A, [b[:, :] for b in B]]
        last_hid = o_hi[:, 0:2, :], o_lo[:, 0:2, :]
        BIGB = [B[0], B[1], B[3]]

        HALF = P // 2

        def first_halves(ap, l):
            return ap.rearrange("p (n two c) -> p n two c", two=2, c=1 << l)[:, :, 0, :]

        def big(name):
            return BIGB[BIG_INDEX[name] % 3]

        norm_scale = [a1[:, :], a2[:, :], vecs("mix0"), vecs("ffn0"), vecs("mix1"), vecs("ffn1"), vecs("final")]
        norm_shift = [mods[:, 0:8], mods[:, 24:32], None, None, None, None, None]
        gates = [mods[:, 16:24], mods[:, 40:48], None, None, None, None]

        block = ctx.enter_context(nc.Block())

        @block.sync
        def _(sp):
            def load(r):
                if r >= RING:
                    _, kind, n = STREAM_ORDER[r - RING]
                    sp.wait_ge(s.lo_ready if kind == "w" else s.mod_accumulated, n + 1)
                sp.dma_start(raw[:, r % RING, :], stream[r]).then_inc(raw_landed[r % RING], 16)

            def loads(w0, count):
                r0 = raw_index(w0)
                with sp.Fori(0, count // RING) as it:
                    for i in range(RING):
                        sp.wait_ge(s.lo_ready, it * RING + (w0 + i - RING + 1))
                        sp.dma_start(raw[:, (r0 + i) % RING, :], stream[it * RING + (r0 + i)]).then_inc(
                            raw_landed[(r0 + i) % RING], 16)

            w0 = FIRST_STEP + RING
            count = (LAST_STEP - w0) // RING * RING
            for r in range(raw_index(w0)):
                load(r)
            loads(w0, count)
            for r in range(raw_index(w0 + count), raw_index(LAST_STEP + 1 + RING)):
                load(r)
            loads(LAST_STEP + 1 + RING, N_WEIGHTS - (LAST_STEP + 1 + RING))
            for m in range(0, KD, 2):
                sp.wait_ge(s.t_ready, 8 * 2 + m + 2)
                sp.dma_start(out[:, m:m + 2, :], nt[:, m:m + 2, :]).then_inc(s.out_stored, 16)
            sp.wait_ge(s.out_stored, 16 * KD // 2)

        @block.gpsimd
        def _(pool):
            pool.memset(zero_r[:, :].bitcast(F32), 0.0).then_inc(s.pool_zeroed, 1)
            pool.memset(pad[:, :, 0:3], 0.0).then_inc(s.pool_zeroed, 1)
            pool.wait_ge(s.t5_row, 1)
            pool.dma_start(t5_scratch.ap(), t5r[:, :]).then_inc(s.t5_stored, 16)
            four = lambda b: b.rearrange("p (i c) -> p i c", i=4)
            pool.wait_ge(s.masks_loaded, 16)
            pool.wait_ge(s.head_rms, 1)
            for gi in range(4):
                rk = hs[:, 2, 16 * (gi // 2):16 * (gi // 2) + 8].rearrange("p (i two) -> p i two", two=2)[:, :, gi % 2]
                pool.wait_ge(s.d_ready, gi + 1)
                pool.tensor_tensor(four(DT[:, gi, :]), four(DT[:, gi, :]), rk.unsqueeze(2).broadcast_to([P, 4, P]),
                                   ALU.mult).then_inc(s.d_normed, 1)
            for gi in range(4):
                pool.wait_ge(s.big_read_dve, big_reads(BIG_INDEX[f"kk{gi}"], "dve"))
                pool.tensor_tensor(four(XT[:, gi, :]), four(AT[:, gi, :]), level_mask[0].unsqueeze(1).broadcast_to([P, 4, P]),
                                   ALU.mult).then_inc(s.x_masked, 1)
            for l in range(1, NEXP + 1):
                for gi in range(4):
                    if l == 1:
                        pool.wait_ge(s.mod_summed, 1)
                    else:
                        pool.wait_ge(s.p_ready, 4 * (l - 2) + gi + 1)
                    pool.tensor_tensor(
                        Bm[:, gi, :].rearrange("p (i c) -> p i c", i=4),
                        AT[:, gi, :].rearrange("p (i c) -> p i c", i=4),
                        level_mask[l].unsqueeze(1).broadcast_to([P, 4, P]), ALU.mult).then_inc(s.b_ready, 1)
            pool.wait_ge(s.t5_stored, 16)
            pool.wait_ge(s.x_ready, 8)
            pool.dma_start(t5[:, :, 0:256], bass.AP(t5_scratch, 0, [[1, P], [384, 16], [1, 256]])).then_inc(s.tables_loaded, 16)
            pool.dma_start(t5[:, :, 256:384], bass.AP(t5_scratch, 128, [[1, P], [384, 16], [1, 128]])).then_inc(s.tables_loaded, 16)
            pool.memset(cu[:, :, 0:2], 0.0).then_inc(s.pool_zeroed, 1)
            pool.wait_ge(s.tables_loaded, 32)
            for i, n in enumerate(LATE):
                acc2, to = nt[:, 0:2, :], nt[:, 0:1, :]
                for j, (a, b, dst, ready) in enumerate(((nt[:, 0:2, :], nt[:, 2:4, :], acc2, 4), (acc2, nt[:, 4:6, :], acc2, 6),
                                                        (acc2, nt[:, 6:8, :], acc2, 8), (nt[:, 0:1, :], nt[:, 1:2, :], to, 8))):
                    pool.wait_ge(s.squared, 8 * n + ready)
                    if j:
                        pool.wait_ge(s.squares_added, 4 * i + j)
                    pool.tensor_tensor(dst, a, b, ALU.add).then_inc(s.squares_added, 1)

        @block.scalar
        def _(act):
            steps = [0]

            def link(ins):
                steps[0] += 1
                ins.then_inc(s.act_step, 1)
                act.wait_ge(s.act_step, steps[0])

            act.dma_start(vec[:, :], vectors_in).then_inc(s.vectors_loaded, 16)
            act.dma_start(x[:, :, :], x_in).then_inc(s.x_loaded, 16)
            act.dma_start(consts[:, 0:N_FIRST], consts_in[:, 0:N_FIRST]).then_inc(s.consts_loaded, 16)
            act.dma_start(gab_w[:, :], gab_in).then_inc(s.gab_loaded, 16)
            act.dma_start(oh, t5_onehot).then_inc(s.t5_loaded, 16)
            act.dma_start(rb[:, :], rel_bias).then_inc(s.t5_loaded, 16)
            act.dma_start(t5l, t5_log).then_inc(s.t5_loaded, 16)

            def hi(w, it=0):
                if isinstance(it, int):
                    w, it = w + RING * it, 0
                r = raw_index(w)
                act.wait_ge(raw_landed[r % RING], (it + (r // RING + 1)) * 16)
                if w >= RING:
                    act.wait_ge(s.block_used, it * RING + (w - RING + 1))
                act.activation(w_hi[:, w % RING, :], raw[:, r % RING, :], ACT.Copy).then_inc(s.hi_ready, 1)

            def squares(n):
                link(act.activation(root_tmp[:, :], ones, ACT.Sqrt))
                for m in range(KD):
                    if n:
                        act.wait_ge(s.x_ready, 8 * (n - 1) + m + 1)
                    act.activation(nt[:, m, :], x[:, m, :], ACT.Square).then_inc(s.squared, 1)

            def root(n):
                act.wait_ge(s.inv_ready, n + 1)
                act.activation(rms[:, :], inv[:, :], ACT.Sqrt).then_inc(s.rms_ready, 1)
                if n in LATE:
                    act.wait_ge(s.rstd_ready, n + 1)
                    act.activation(rrow[:, :], B[3][:, 256:512], ACT.Copy).then_inc(s.row_copied, 1)

            def squares_and_high(n, w):
                link(act.activation(root_tmp[:, :], ones, ACT.Sqrt))
                hi(w)
                for m in range(KD):
                    act.wait_ge(s.x_ready, 8 * (n - 1) + m + 1)
                    act.activation(h_hi[:, m, :], x[:, m, :], ACT.Identity, scale=norm_scale[n][:, m:m + 1]).then_inc(s.h_hi_ready, 1)
                    act.activation(nt[:, m, :], x[:, m, :], ACT.Square).then_inc(s.squared, 1)

            def h_high(n):
                for k in range(KD):
                    act.wait_ge(s.t_ready, 8 * n + k + 1)
                    if norm_shift[n] is not None:
                        act.activation(h_hi[:, k, :], nt[:, k, :], ACT.Identity, bias=norm_shift[n][:, k:k + 1]).then_inc(s.h_hi_ready, 1)
                    else:
                        act.activation(h_hi[:, k, :], nt[:, k, :], ACT.Copy).then_inc(s.h_hi_ready, 1)

            act.wait_ge(s.vectors_loaded, 16)
            act.activation(c_act[:, :], vecs("c"), ACT.Silu).then_inc(s.c_act, 1)
            act.wait_ge(s.x_loaded, 16)
            act.wait_ge(s.consts_loaded, 16)
            squares(0)
            act.wait_ge(s.gab_loaded, 16)
            act.activation(gab_wh[:, :], gab_w[:, :], ACT.Copy).then_inc(s.gab_hi, 1)
            root(0)
            hi(0)
            act.dma_start(consts[:, N_FIRST:], consts_in[:, N_FIRST:]).then_inc(s.masks_loaded, 16)
            h_high(0)
            hi(1)

            dest = [kT[:, 0:2, :], kT[:, 2:4, :], qT[:, 0:2, :], qT[:, 2:4, :], vT[:, 0:2, :], vT[:, 2:4, :]]

            def feature(w):
                act.wait_ge(s.conv_done, w + 1)
                act.activation(dest[w], cacc.rearrange("p (a b) -> p a b", a=2), ACT.Silu).then_inc(s.feature_ready, 1)
                if w < 4:
                    act.wait_ge(s.feature_ready, w + 1)
                    act.activation(head_sq[w].rearrange("p (a b) -> p a b", a=2), dest[w], ACT.Square).then_inc(s.head_squared, 1)

            for w in range(6):
                hi(w + 2)
                act.wait_ge(s.block_used, w + 1)
                if w == 0:
                    act.wait_ge(s.pool_zeroed, 2)
                if w:
                    act.wait_ge(s.conv_done, w)
                act.activation(pad[:, :, 3:259], A[w % 4].rearrange("p (a b) -> p a b", a=2), ACT.Copy).then_inc(s.pad_ready, 1)
                if w:
                    feature(w - 1)
                if w == 0:
                    act.wait_ge(s.gab_product, 1)
                    act.activation(gabT, B[0][0:16, 0:T], ACT.Copy).then_inc(s.gab_copied, 1)
                if w == 2:
                    act.wait_ge(s.gate_dve, 1)
                    act.activation(gt[:, 1, :], gt[:, 0, :], ACT.Exp).then_inc(s.gate_exp, 1)
                    act.activation(gt[:, 3, :], gt[:, 2, :], ACT.Exp).then_inc(s.gate_exp, 1)
                    act.activation(gt[:, 4, 0:8], vecs("a_log"), ACT.Exp).then_inc(s.gate_exp, 1)
                    act.wait_ge(s.gate_dve, 2)
                    act.activation(gt[:, 5, :], gt[:, 7, :], ACT.Ln).then_inc(s.gate_exp, 1)
            two = lambda b: b.rearrange("p (a b) -> p a b", a=2)
            hi(8)
            feature(5)
            act.wait_ge(s.block_used, 7)
            act.activation(zT[:, 0:2, :], two(A[2]), ACT.Silu).then_inc(s.proj_evac, 1)
            act.wait_ge(s.head_inv, 1)
            act.activation(hs[:, 2, :], hs[:, 1, :], ACT.Sqrt).then_inc(s.head_rms, 1)
            hi(9)
            act.wait_ge(s.block_used, 8)
            act.activation(zT[:, 2:4, :], two(A[3]), ACT.Silu).then_inc(s.proj_evac, 1)
            act.wait_ge(s.decay_dve, 1)
            act.activation(kds[:, 1, :], kds[:, 0, :], ACT.Exp).then_inc(s.decay_act, 1)
            for w in (8, 9):
                hi(w + 2)
                act.wait_ge(s.block_used, w + 1)
                act.activation(qs[:, 2 * (w - 8):2 * (w - 8) + 2, :], two(A[w % 4]), ACT.Copy).then_inc(s.proj_evac, 1)
                act.activation(head_sq[w - 4], A[w % 4], ACT.Square).then_inc(s.head_squared, 1)
                if w == 8:
                    act.wait_ge(s.big_ready, BIG_INDEX["eg"] + 1)
                    act.activation(eg.rearrange("p a b -> p (a b)"), big("eg")[:, :], ACT.Exp).then_inc(s.big_read_act, 1)
            hi(12)
            act.wait_ge(s.block_used, 11)
            act.activation(ks[:, :], A[2][:, 0:256], ACT.Copy).then_inc(s.proj_evac, 1)
            act.activation(swa_vT, A[2][:, 256:512], ACT.Copy).then_inc(s.proj_evac, 1)
            act.activation(head_sq[6][:, 0:256], A[2][:, 0:256], ACT.Square).then_inc(s.head_squared, 1)
            for gi in range(4):
                act.wait_ge(s.d_shifted, gi + 1)
                act.activation(DT[:, gi, :], DT[:, gi, :], ACT.Exp).then_inc(s.d_ready, 1)
            hi(13)
            act.wait_ge(s.head_inv, 2)
            act.activation(ss[:, 2, :], ss[:, 1, :], ACT.Sqrt).then_inc(s.head_rms, 1)
            act.wait_ge(s.v_transposed, 1)
            act.activation(vs[:, :, :].rearrange("p t c -> p (t c)"), A[3][:, 0:T], ACT.Copy).then_inc(s.v_ready, 1)

            def exps(a, sc):
                act.wait_ge(s.negmax_ready, a + 1)
                for hh in range(4):
                    for part, (c0, c1) in enumerate(((0, 256), (256, 384))):
                        act.activation(sc[:, hh, c0:c1], sc[:, hh, c0:c1], ACT.Exp,
                                       bias=soft[:, 1, 2 * hh + part:2 * hh + part + 1],
                                       accum_out=soft[:, 2, 2 * hh + part:2 * hh + part + 1]).then_inc(s.exp_ready, 1)
                if a < 2:
                    act.activation(soft[:, 3, :], soft[:, 3, :], ACT.Exp).then_inc(s.exp_ready, 1)

            def probs_copy(a, bank, pT):
                if a == 0:
                    act.wait_ge(s.row_scaled, 2)
                for hh in range(4):
                    act.wait_ge(s.ptrans_ready, 4 * a + hh + 1)
                    act.activation(pT[:, hh, :], bank[hh][:, 0:384], ACT.Copy).then_inc(s.ptrans_copied, 1)

            def pv_high(a, bank, dst):
                act.wait_ge(s.pv_ready, a + 1)
                act.activation(dst, bank.rearrange("p (a b) -> p a b", a=2), ACT.Copy).then_inc(s.pv_hi, 1)

            def x_copy(l, gi, bank):
                act.wait_ge(s.xtr_ready, 4 * l + gi + 1)
                return act.activation((XT if l else X)[:, gi, :], bank[:, :], ACT.Copy)

            for gi in range(4):
                if gi == 0:
                    act.wait_ge(s.big_read_dve, big_reads(BIG_INDEX["qk3"], "dve"))
                x_copy(0, gi, big(f"tr{gi}")).then_inc(s.x_copied, 1)
            for l in range(1, NEXP + 1):
                for gi in range(4):
                    act.wait_ge(s.p_ready, 4 * (l - 1) + gi + 1)
                    act.activation(Pm[:, gi, 0:T], B[gi][:, 0:T], ACT.Copy).then_inc(s.p_copied, 1)
                if l == 1:
                    exps(0, sc1)
                if l == 3:
                    pv_high(0, A[0], h_hi[:, 4:6, :])
                if l == 4:
                    exps(1, sc1)
                if l == NEXP:
                    pv_high(1, A[0], h_hi[:, 6:8, :])
                if l < NEXP:
                    for gi in range(4):
                        x_copy(l, gi, B[gi]).then_inc(s.x_copied, 1)
                if l == 2:
                    probs_copy(0, A, pT1)
                if l == 5:
                    probs_copy(1, A, pT1)
            act.wait_ge(s.u_ready, 1)
            act.activation(u0, B[0][:, :], ACT.Copy).then_inc(s.u_copied, 1)
            act.wait_ge(s.o0_ready, 1)
            for par in range(2):
                rows = slice(64 * par, 64 * par + 64)
                act.activation(oT[rows, :, 0:P], B[2 + par][rows, :].rearrange("p (a b) -> p a b", a=4), ACT.Copy).then_inc(s.o_copied, 1)
            act.wait_ge(s.vn_ready, 1)
            act.activation(vn, B[0][:, :], ACT.Copy).then_inc(s.vn_copied, 1)
            act.wait_ge(s.o1_ready, 1)
            for par in range(2):
                rows = slice(64 * par, 64 * par + 64)
                act.activation(oT[rows, :, P:T], B[par][rows, :].rearrange("p (a b) -> p a b", a=4), ACT.Copy).then_inc(s.o_copied, 1)
            act.wait_ge(s.o_copied, 4)
            act.activation(osq, oT, ACT.Square).then_inc(s.o_squared, 1)
            act.wait_ge(s.o_inv, 1)
            act.activation(os_[:, 2, :], os_[:, 1, :], ACT.Sqrt).then_inc(s.o_rms, 1)
            for i in range(2):
                act.wait_ge(s.o_gated, i + 1)
                act.activation(h_hi[:, 2 * i:2 * i + 2, :], oT[:, 2 * i:2 * i + 2, :], ACT.Copy).then_inc(s.o_hi_done, 1)
            hi(14)
            hi(15)
            hi(16)

            def ffn(f):
                F = FFN_BASE[f]

                def silu(j, used):
                    if f:
                        act.wait_ge(s.gate_scaled, j + (JF * (f - 1) + 1))
                        act.activation(sg[:, :], sg[:, :], ACT.Silu).then_inc(s.silu_ready, 1)
                    else:
                        act.wait_ge(s.block_used, used)
                        if not isinstance(j, int) or j:
                            act.wait_ge(s.hid_ready, j)
                        act.activation(sg[:, :], B[0][:, :], ACT.Silu).then_inc(s.silu_ready, 1)

                def hid_high(j, used, dst=hid_hi[:, :, :]):
                    act.wait_ge(s.hid_ready, j + (JF * f + 1))
                    if used is not None:
                        act.wait_ge(s.block_used, used)
                    act.activation(dst.rearrange("p a b -> p (a b)"), hid[:, :], ACT.Copy).then_inc(s.hid_hi_ready, 1)

                if f:
                    squares_and_high(2 * f + 1, F + 1)
                    hi(F + 2)
                    root(2 * f + 1)
                else:
                    squares(1)
                    root(1)
                    h_high(1)
                    hi(F + 2)
                silu(0, F + 1)
                hi(F + 3)
                hid_high(0, None)
                with act.Fori(1, JF - 1) as j:
                    hi(F + 4, j - 1)
                    silu(j, (j - 1) * RING + (F + 3))
                    hi(F + 5, j - 1)
                    hi(F + 6, j - 1)
                    hid_high(j, (j - 1) * RING + (F + 5))
                hi(F + 4, JF - 2)
                silu(JF - 1, (JF - 2) * RING + (F + 3))
                if f:
                    hi(F + 5, JF - 2)
                hid_high(JF - 1, None, last_hid[0])
                if not f:
                    hi(F + 5, JF - 2)
                if f < 2:
                    hi(F + 6, JF - 2)

            ffn(0)
            squares_and_high(2, CONV_BASE + 1)
            for i in range(4):
                w = CONV_BASE + 3 * i
                hi(w + 2)
                if i == 0:
                    root(2)
                hi(w + 3)
                hi(w + 4)
                act.wait_ge(s.by_ready, i + 1)
                act.activation(o_hi[:, 2 * i:2 * i + 2, :], yb[:, :, :], ACT.Copy).then_inc(s.by_hi, 1)
            for w in range(CONV_OUT + 2, CONV_OUT + 5):
                hi(w)
            ffn(1)
            squares_and_high(4, QKV_BASE + 1)
            for i in range(5):
                w, a = QKV_BASE + 3 * i, i + 1
                if i < 4:
                    hi(w + 2)
                if i == 0:
                    root(4)
                else:
                    exps(a, sc2)
                if i < 4:
                    hi(w + 3)
                    hi(w + 4)
                    act.wait_ge(s.block_used, w + 3)
                    for t in range(TT):
                        act.activation(v2[:, i % 2, t, :], A[2][:, 256 * t:256 * t + 256], ACT.Copy, scale=rms[:, t:t + 1]).then_inc(s.v_scaled, 1)
                else:
                    for v in range(ATT_OUT + 2, ATT_OUT + 4):
                        hi(v)
                if i:
                    probs_copy(a, B, pT2)
                    pv_high(a, A[3] if i < 4 else B[0], o_hi[:, 2 * i - 2:2 * i, :])
            hi(ATT_OUT + 4)
            ffn(2)
            squares(6)
            root(6)

        @block.vector
        def _(dve):
            steps = [0]

            def link(ins):
                steps[0] += 1
                ins.then_inc(s.dve_step, 1)
                dve.wait_ge(s.dve_step, steps[0])

            def lo(w, it=0):
                if isinstance(it, int):
                    w, it = w + RING * it, 0
                dve.wait_ge(s.hi_ready, it * RING + (w + 1))
                dve.tensor_tensor(w_lo[:, w % RING, :], raw[:, raw_index(w) % RING, :], w_hi[:, w % RING, :],
                                  ALU.subtract).then_inc(s.lo_ready, 1)

            def accumulate(m):
                r = mod_index(m)
                part = max(i for i in range(4) if MOD_START[i] <= m)
                k = m - MOD_START[part]
                mod_acc = mod_accs[part]
                dve.wait_ge(raw_landed[r % RING], 16 * (r // RING + 1))
                if k:
                    dve.wait_ge(s.mod_accumulated, m)
                if part < 2:
                    if k == 0:
                        dve.tensor_scalar(mod_acc, raw[:, r % RING, :], c_act[:, 0:1], None, ALU.mult).then_inc(s.mod_accumulated, 1)
                    else:
                        dve.scalar_tensor_tensor(out=mod_acc, in0=raw[:, r % RING, :], scalar=c_act[:, k:k + 1],
                                                 in1=mod_acc, op0=ALU.mult, op1=ALU.add).then_inc(s.mod_accumulated, 1)
                    return
                lower, upper = raw[:, r % RING, 0:BLOCK // 2], raw[:, r % RING, BLOCK // 2:]
                if k == 0:
                    link(dve.tensor_scalar(mod_acc, lower, c_act[:, 0:1], None, ALU.mult))
                else:
                    link(dve.scalar_tensor_tensor(out=mod_acc, in0=lower, scalar=c_act[:, 2 * k:2 * k + 1],
                                                  in1=mod_acc, op0=ALU.mult, op1=ALU.add))
                dve.scalar_tensor_tensor(out=mod_acc, in0=upper, scalar=c_act[:, 2 * k + 1:2 * k + 2],
                                         in1=mod_acc, op0=ALU.mult, op1=ALU.add).then_inc(s.mod_accumulated, 1)

            def modulation(part):
                dve.wait_ge(s.mod_summed, part + 1)
                m0 = MOD_COLS[part] // P
                n = (16, 16, 8, 8)[part]
                b0 = V_AT["b_ada"][0] + m0
                ins = dve.tensor_tensor(mods[:, m0:m0 + n], mod_bank[part][:, 480:480 + n], vec[:, b0:b0 + n], ALU.add)
                if part % 2 == 0:
                    link(ins)
                    a_scale, scale, norm_w = ((a1, mods[:, 8:16], "norm1"), None, (a2, mods[:, 32:40], "norm2"))[part]
                    ins = dve.scalar_tensor_tensor(out=a_scale[:, :], in0=scale, scalar=1.0, in1=vecs(norm_w),
                                                   op0=ALU.add, op1=ALU.mult)
                ins.then_inc(s.mod_ready, 1)

            def inverse_mean(n):
                dve.wait_ge(s.sumsq_ready, n + 1)
                link(dve.tensor_scalar(ms[:, :], B[3][:, 0:TT], 1.0 / D, EPS, ALU.mult, ALU.add))
                dve.reciprocal(inv[:, :], ms[:, :]).then_inc(s.inv_ready, 1)

            def h_parts(n):
                dve.wait_ge(s.rstd_ready, n + 1)
                rstd = B[3][:, 256:512]

                def scaled(k):
                    dve.scalar_tensor_tensor(out=nt[:, k, :], in0=x[:, k, :], scalar=norm_scale[n][:, k:k + 1],
                                             in1=rstd, op0=ALU.mult, op1=ALU.mult).then_inc(s.t_ready, 1)

                def low(k):
                    dve.wait_ge(s.h_hi_ready, 8 * n + k + 1)
                    if norm_shift[n] is not None:
                        dve.scalar_tensor_tensor(out=h_lo[:, k, :], in0=nt[:, k, :], scalar=norm_shift[n][:, k:k + 1],
                                                 in1=h_hi[:, k, :], op0=ALU.add, op1=ALU.subtract).then_inc(s.h_lo_ready, 1)
                    else:
                        dve.tensor_tensor(h_lo[:, k, :], nt[:, k, :], h_hi[:, k, :], ALU.subtract).then_inc(s.h_lo_ready, 1)

                for k in range(KD):
                    scaled(k)
                    if n < 6 and k >= 1:
                        low(k - 1)
                if n < 6:
                    low(KD - 1)

            def low_of_x(n, k):
                dve.wait_ge(s.h_hi_ready, 8 * n + k + 1)
                dve.scalar_tensor_tensor(out=h_lo[:, k, :], in0=x[:, k, :], scalar=norm_scale[n][:, k:k + 1],
                                         in1=h_hi[:, k, :], op0=ALU.mult, op1=ALU.subtract).then_inc(s.h_lo_ready, 1)

            def residual(r, last):
                for m in range(KD):
                    if m < KD - 2:
                        dve.wait_ge(s.acc_tile_done, 3 * r + m // 2 + 1)
                    else:
                        dve.wait_ge(s.block_used, last + 1)
                    a = acc[:, 256 * m:256 * m + 256]
                    if gates[r] is not None:
                        dve.scalar_tensor_tensor(out=x[:, m, :], in0=a, scalar=gates[r][:, m:m + 1], in1=x[:, m, :],
                                                 op0=ALU.mult, op1=ALU.add).then_inc(s.x_ready, 1)
                    else:
                        dve.tensor_tensor(x[:, m, :], a, x[:, m, :], ALU.add).then_inc(s.x_ready, 1)
                    if r + 1 in LATE and m >= 2:
                        low_of_x(r + 1, m - 2)
                if r + 1 in LATE:
                    low_of_x(r + 1, KD - 2)
                    low_of_x(r + 1, KD - 1)
                    lo(last + 2)

            dve.wait_ge(s.vectors_loaded, 16)
            dve.wait_ge(s.c_act, 1)
            link(dve.tensor_scalar(qk_w[:, :], vecs("qn_w"), HD ** -0.5, None, ALU.mult))
            link(dve.tensor_copy(sink2[:, :, 0], vecs("sinks")))
            link(dve.tensor_copy(sink2[:, :, 1], vecs("sinks")))
            for m in range(5):
                accumulate(m)
            inverse_mean(0)
            dve.wait_ge(s.gab_hi, 1)
            dve.tensor_tensor(gab_wl[:, :], gab_w[:, :], gab_wh[:, :], ALU.subtract).then_inc(s.gab_lo, 1)
            for m in range(5, MOD_START[1]):
                accumulate(m)
            lo(0)
            modulation(0)
            dve.wait_ge(s.mod_ready, 1)
            h_parts(0)
            lo(1)

            for w in range(6):
                if w == 5:
                    dve.wait_ge(s.masks_loaded, 16)
                    dve.wait_ge(s.cum_ready, 1)
                    link(dve.tensor_copy(Gs[:, :], STAT[:, 32:48]))
                    dve.tensor_tensor(kds[:, 0, :], STAT[:, 48:56], Gs[:, 0:8], ALU.subtract).then_inc(s.decay_dve, 1)
                lo(w + 2)
                if w < 6:
                    dve.wait_ge(s.pad_ready, w + 1)
                    if w:
                        dve.wait_ge(s.feature_ready, w)
                    tile0 = (4, 6, 0, 2, 8, 10)[w]
                    for mt in range(2):
                        o = cacc[:, 256 * mt:256 * mt + 256]
                        cw = V_AT["conv_w"][0] + 4 * (tile0 + mt)
                        dve.tensor_scalar(o, pad[:, mt, 0:256], vec[:, cw:cw + 1], None, ALU.mult).then_inc(s.dve_step, 1)
                        steps[0] += 1
                    for tap in range(1, 4):
                        for mt in range(2):
                            o = cacc[:, 256 * mt:256 * mt + 256]
                            cw = V_AT["conv_w"][0] + 4 * (tile0 + mt) + tap
                            dve.wait_ge(s.dve_step, steps[0] - 1)
                            ins = dve.scalar_tensor_tensor(out=o, in0=pad[:, mt, tap:tap + 256], scalar=vec[:, cw:cw + 1],
                                                           in1=o, op0=ALU.mult, op1=ALU.add)
                            if tap == 3 and mt == 1:
                                dve.wait_ge(s.dve_step, steps[0])
                                ins.then_inc(s.conv_done, 1)
                            else:
                                ins.then_inc(s.dve_step, 1)
                                steps[0] += 1
                if w == 1:
                    dve.wait_ge(s.gab_ready, 1)
                    ga = STAT[:, 0:32].rearrange("p (t c) -> p t c", t=TT)
                    v8 = lambda a: a.rearrange("p (t c) -> p t c", t=TT)
                    link(dve.tensor_tensor(v8(gt[:, 6, :]), ga[:, :, 0:8],
                                           vecs("dt_bias").unsqueeze(1).broadcast_to([P, TT, 8]), ALU.add))
                    link(dve.tensor_scalar(v8(gt[:, 0, :]), ga[:, :, 8:16], -1.0, None, ALU.mult))
                    dve.scalar_tensor_tensor(out=gt[:, 2, :], in0=gt[:, 6, :], scalar=-1.0, in1=gt[:, 6, :],
                                             op0=ALU.mult, op1=ALU.min).then_inc(s.gate_dve, 1)
                if w == 2:
                    dve.wait_ge(s.t5_psum, 1)
                    dve.wait_ge(s.t5_loaded, 48)
                    dve.tensor_tensor(t5r[:, :], B[1][0:16, 0:384], t5l, ALU.add).then_inc(s.t5_row, 1)
                    dve.wait_ge(s.gate_exp, 3)
                    dve.tensor_scalar(gt[:, 7, :], gt[:, 3, :], 1.0, None, ALU.add).then_inc(s.gate_dve, 1)
                    link(dve.tensor_scalar(gt[:, 2, :], gt[:, 1, :], 1.0, None, ALU.add))
                    link(dve.reciprocal(beta[:, :], gt[:, 2, :]))
                    dve.wait_ge(s.gate_exp, 4)
                    link(dve.scalar_tensor_tensor(out=gt[:, 6, :], in0=gt[:, 6, :], scalar=0.0, in1=gt[:, 5, :],
                                                  op0=ALU.max, op1=ALU.add))
                    dve.scalar_tensor_tensor(out=v8(g[:, :]), in0=v8(gt[:, 6, :]), scalar=-1.0,
                                             in1=gt[:, 4, 0:8].unsqueeze(1).broadcast_to([P, TT, 8]),
                                             op0=ALU.mult, op1=ALU.mult).then_inc(s.gate_done, 1)

            def big_read(name, ins):
                assert ("dve" == BIG_LIST[BIG_INDEX[name]][1])
                ins.then_inc(s.big_read_dve, 1)

            def wait_big(name):
                dve.wait_ge(s.big_ready, BIG_INDEX[name] + 1)

            def wait_read(name):
                dve.wait_ge(s.big_read_dve, big_reads(BIG_INDEX[name], "dve"))

            two = lambda b: b[:, :].rearrange("p (a b) -> p a b", a=2)
            four = lambda b: b.rearrange("p (i c) -> p i c", i=4)

            lo(8)
            dve.wait_ge(s.head_sums, 1)
            link(dve.tensor_scalar(hs[:, 0, :], STAT[:, 64:96], EPS, None, ALU.add))
            dve.reciprocal(hs[:, 1, :], hs[:, 0, :]).then_inc(s.head_inv, 1)
            lo(9)
            hsv = hs[:, 2, :].rearrange("p (t c) -> p t c", t=TT)
            dve.wait_ge(s.head_rms, 1)
            dve.tensor_tensor(v8(coefk[:, :]), v8(beta[:, :]), hsv[:, :, 0:8], ALU.mult).then_inc(s.coef_ready, 1)
            dve.tensor_scalar(v8(coefq[:, :]), hsv[:, :, 8:16], HD ** -0.5, None, ALU.mult).then_inc(s.coef_ready, 1)

            def row_scale(name, dst, src):
                wait_big(name)
                big_read(name, dve.tensor_tensor(dst, src, two(big(name)), ALU.mult))

            row_scale("kb01", kbT[:, 0:2, :], kT[:, 0:2, :])
            row_scale("kb23", kbT[:, 2:4, :], kT[:, 2:4, :])
            row_scale("q01", qT[:, 0:2, :], qT[:, 0:2, :])
            lo(10)
            row_scale("q23", qT[:, 2:4, :], qT[:, 2:4, :])
            dve.wait_ge(s.decay_act, 1)
            link(dve.tensor_tensor(kds[:, 1, :], kds[:, 1, :], hsv[:, 0, 0:8], ALU.mult))
            dve.wait_ge(s.big_read_act, big_reads(BIG_INDEX["eg"], "act"))
            wait_read("q23")
            dve.tensor_tensor(kbgT[:, :, :], kbT[:, :, P:T], eg, ALU.mult).then_inc(s.row_scaled, 1)
            dve.tensor_tensor(qdT[:, :, :], qT[:, :, P:T], eg, ALU.mult).then_inc(s.row_scaled, 1)

            def by_token(name, dst, factor):
                wait_big(name)
                big_read(name, dve.tensor_tensor(
                    dst.rearrange("p (h e) -> p h e", h=8), big(name)[:, :].rearrange("p (h e) -> p h e", h=8),
                    factor.unsqueeze(2).broadcast_to([P, 8, HD]), ALU.mult))

            by_token("v0", vb[:, 0, :], beta[:, 0:8])
            by_token("v1", vb[:, 1, :], beta[:, 8:16])
            by_token("kt", kd[:, :], kds[:, 1, :])

            def decay(gi):
                t, par = gi // 2, gi % 2
                Gcol = Gs[:, :].rearrange("p (t i two) -> p t i two", t=TT, two=2)[:, t, :, par]
                wait_big(f"G{gi}")
                big_read(f"G{gi}", dve.tensor_tensor(four(DT[:, gi, :]), four(big(f"G{gi}")[:, :]),
                                                     Gcol.unsqueeze(2).broadcast_to([P, 4, P]), ALU.subtract))
                wait_read(f"G{gi}")
                dve.tensor_tensor(four(DT[:, gi, :]), four(DT[:, gi, :]), future.unsqueeze(1).broadcast_to([P, 4, P]),
                                  ALU.add).then_inc(s.d_shifted, 1)

            for gi in range(3):
                decay(gi)
            decay(3)
            for gi in range(4):
                wait_big(f"kk{gi}")
                dve.wait_ge(s.d_normed, gi + 1)
                big_read(f"kk{gi}", dve.tensor_tensor(AT[:, gi, :], big(f"kk{gi}")[:, :], DT[:, gi, :], ALU.mult))
            dve.wait_ge(s.head_sums, 2)
            link(dve.tensor_scalar(ss[:, 0, :], STAT[:, 96:116], 1.0 / HD, EPS, ALU.mult, ALU.add))
            dve.reciprocal(ss[:, 1, :], ss[:, 0, :]).then_inc(s.head_inv, 1)
            for gi in range(4):
                wait_big(f"qk{gi}")
                big_read(f"qk{gi}", dve.tensor_tensor(qkT[:, gi, :], big(f"qk{gi}")[:, :], DT[:, gi, :], ALU.mult))
            for gi in range(4):
                dve.wait_ge(s.x_masked, gi + 1)
                dve.tensor_tensor(four(XT[:, gi, :]), ident.unsqueeze(1).broadcast_to([P, 4, P]), four(XT[:, gi, :]),
                                  ALU.subtract).then_inc(s.xt_ready, 1)
            wait_big("sk")
            dve.wait_ge(s.proj_evac, 5)
            big_read("sk", dve.scalar_tensor_tensor(out=ks[:, :], in0=ks[:, :], scalar=vecs("kn_w"), in1=big("sk")[:, 0:256],
                                                    op0=ALU.mult, op1=ALU.mult))
            for i, name in enumerate(("sq01", "sq23")):
                wait_big(name)
                big_read(name, dve.scalar_tensor_tensor(out=qs[:, 2 * i:2 * i + 2, :], in0=qs[:, 2 * i:2 * i + 2, :],
                                                        scalar=qk_w[:, :], in1=two(big(name)), op0=ALU.mult, op1=ALU.mult))

            def softmax_max(a, bank, sc):
                for hh in range(4):
                    dve.wait_ge(s.scores_ready, 4 * a + hh + 1)
                    if a < 2:
                        head = 2 * a + hh // 2 + 4 * (hh % 2)
                        ins = dve.scalar_tensor_tensor(out=sc[:, hh, :], in0=const("alibi"), scalar=2.0 ** -(head + 1),
                                                       in1=bank[hh][:, 0:384], op0=ALU.mult, op1=ALU.add)
                    else:
                        ins = dve.tensor_tensor(sc[:, hh, :], t5[:, 4 * (a - 2) + hh, :], bank[hh][:, 0:384], ALU.add)
                    ins.then_inc(s.scores_biased, 1)
                    dve.wait_ge(s.scores_biased, 4 * a + hh + 1)
                    for part, (c0, c1) in enumerate(((0, 256), (256, 384))):
                        link(dve.tensor_reduce(soft[:, 0, 2 * hh + part:2 * hh + part + 1], sc[:, hh, c0:c1], AX.X, ALU.max))
                if a < 2:
                    sk = sink2[:, 4 * a:4 * a + 4, :].rearrange("p h t -> p (h t)")
                    link(dve.tensor_tensor(soft[:, 0, :], soft[:, 0, :], sk, ALU.max))
                    link(dve.tensor_tensor(soft[:, 3, :], sk, soft[:, 0, :], ALU.subtract))
                dve.tensor_scalar(soft[:, 1, :], soft[:, 0, :], -1.0, None, ALU.mult).then_inc(s.negmax_ready, 1)

            def softmax_div(a, sc):
                dve.wait_ge(s.exp_ready, 8 * (a + 1) + min(a + 1, 2))
                if a < 2:
                    link(dve.tensor_tensor(soft[:, 4, :], soft[:, 2, :], soft[:, 3, :], ALU.add))
                    link(dve.reciprocal(soft[:, 5, :], soft[:, 4, :]))
                else:
                    link(dve.reciprocal(soft[:, 5, :], soft[:, 2, :]))
                for hh in range(4):
                    for part, (c0, c1) in enumerate(((0, 256), (256, 384))):
                        dve.tensor_scalar(sc[:, hh, c0:c1], sc[:, hh, c0:c1], soft[:, 5, 2 * hh + part:2 * hh + part + 1],
                                          None, ALU.mult).then_inc(s.probs_ready, 1)

            def pv_low(a, bank, dst, high):
                dve.wait_ge(s.pv_hi, a + 1)
                dve.tensor_tensor(dst, bank.rearrange("p (a b) -> p a b", a=2), high, ALU.subtract).then_inc(s.pv_lo, 1)

            softmax_max(0, A, sc1)
            at = MOD_START[1]
            next_w = W_OUT
            for l in range(1, NEXP + 1):
                for gi in range(4):
                    dve.wait_ge(s.qt_ready, 4 * (l - 1) + gi + 1)
                    if l < NEXP:
                        if l > 1:
                            dve.wait_ge(s.x_updated, 4 * (l - 2) + gi + 1)
                        firsts = first_halves(X[:, gi, :], l)
                        dve.tensor_tensor(firsts, firsts, B[gi][:, 0:T].rearrange("p (n c) -> p n c", c=1 << l),
                                          ALU.subtract).then_inc(s.x_updated, 1)
                    else:
                        corner = four(XT[0:HALF, gi, :])[:, :, HALF:P]
                        dve.tensor_tensor(corner, corner, four(B[gi][0:HALF, 0:T]), ALU.subtract).then_inc(s.xt_ready, 1)
                if l == 1:
                    softmax_div(0, sc1)
                if l == 3:
                    pv_low(0, A[0], h_lo[:, 4:6, :], h_hi[:, 4:6, :])
                    softmax_max(1, A, sc1)
                if l == 4:
                    softmax_div(1, sc1)
                if l == NEXP:
                    pv_low(1, A[0], h_lo[:, 6:8, :], h_hi[:, 6:8, :])
                for _ in range(PER_LEVEL[l - 1]):
                    if next_w < LOOP_W:
                        lo(next_w)
                        next_w += 1
                    else:
                        accumulate(at)
                        at += 1
            dve.wait_ge(s.s_ready, 1)
            dve.tensor_copy(S1, B[1][:, 0:256]).then_inc(s.s_copied, 1)
            dve.wait_ge(s.r_ready, 1)
            v4 = lambda ap, par: ap.rearrange("p (i two e) -> p i two e", two=2, e=HD)[:, :, par, :]
            for par in range(2):
                dve.tensor_tensor(v4(r1, par), v4(vb[:, 1, :], par), B[par][:, 0:256].rearrange("p (i e) -> p i e", e=HD),
                                  ALU.subtract).then_inc(s.r_done, 1)
            for _ in range(OUTPUT_BLOCKS):
                accumulate(at)
                at += 1
            dve.wait_ge(s.o_sums, 1)
            link(dve.tensor_scalar(os_[:, 0, :], B[2][:, 0:16], 1.0 / HD, EPS, ALU.mult, ALU.add))
            dve.reciprocal(os_[:, 1, :], os_[:, 0, :]).then_inc(s.o_inv, 1)
            for i in range(2):
                dve.wait_ge(s.o_rows, i + 1)
                o = oT[:, 2 * i:2 * i + 2, :]
                link(dve.scalar_tensor_tensor(out=o, in0=o, scalar=vecs("gdn_w"), in1=two(B[i]), op0=ALU.mult, op1=ALU.mult))
                dve.tensor_tensor(o, o, zT[:, 2 * i:2 * i + 2, :], ALU.mult).then_inc(s.o_gated, 1)
            modulation(1)
            for i in range(2):
                dve.wait_ge(s.o_hi_done, i + 1)
                dve.tensor_tensor(h_lo[:, 2 * i:2 * i + 2, :], oT[:, 2 * i:2 * i + 2, :], h_hi[:, 2 * i:2 * i + 2, :],
                                  ALU.subtract).then_inc(s.o_lo_done, 1)
            while at < MOD_START[3]:
                accumulate(at)
                at += 1
            lo(14)
            modulation(2)
            lo(15)
            residual(0, 14)
            lo(16)

            def wait_row(n):
                dve.wait_ge(s.row_copied, LATE.index(n) + 1)

            both = lambda row: row.unsqueeze(1).broadcast_to([P, 2, T])

            def ffn(f):
                F = FFN_BASE[f]

                def scale_gate(j, used):
                    if f:
                        dve.wait_ge(s.block_used, used)
                        dve.tensor_tensor(two(sg), two(B[0]), both(rrow[:, :]), ALU.mult).then_inc(s.gate_scaled, 1)

                def product(j, used):
                    dve.wait_ge(s.silu_ready, j + (JF * f + 1))
                    dve.wait_ge(s.block_used, used)
                    if not (isinstance(j, int) and f + j == 0):
                        dve.wait_ge(s.hid_lo_ready, j + JF * f)
                    if f:
                        dve.tensor_tensor(hid[:, :], sg[:, :], B[1][:, :], ALU.mult).then_inc(s.gated, 1)
                        dve.wait_ge(s.gated, j + (JF * (f - 1) + 1))
                        dve.tensor_tensor(two(hid), two(hid), both(rrow[:, :]), ALU.mult).then_inc(s.hid_ready, 1)
                    else:
                        dve.tensor_tensor(hid[:, :], sg[:, :], B[1][:, :], ALU.mult).then_inc(s.hid_ready, 1)

                def hid_low(j, high=hid_hi[:, :, :], dst=hid_lo[:, :, :]):
                    dve.wait_ge(s.hid_hi_ready, j + (JF * f + 1))
                    dve.tensor_tensor(dst.rearrange("p a b -> p (a b)"), hid[:, :],
                                      high.rearrange("p a b -> p (a b)"), ALU.subtract).then_inc(s.hid_lo_ready, 1)

                if f:
                    lo(F + 2)
                    inverse_mean(2 * f + 1)
                    wait_row(2 * f + 1)
                else:
                    inverse_mean(1)
                    h_parts(1)
                    lo(F + 2)
                if not f:
                    accumulate(MOD_START[3])
                scale_gate(0, F + 1)
                lo(F + 3)
                product(0, F + 2)
                hid_low(0)
                with dve.Fori(1, JF - 1) as j:
                    lo(F + 4, j - 1)
                    scale_gate(j, (j - 1) * RING + (F + 3))
                    lo(F + 5, j - 1)
                    product(j, (j - 1) * RING + (F + 4))
                    lo(F + 6, j - 1)
                    hid_low(j)
                if not f:
                    accumulate(MOD_START[3] + 1)
                    accumulate(MOD_START[3] + 2)
                lo(F + 4, JF - 2)
                scale_gate(JF - 1, (JF - 2) * RING + (F + 3))
                if not f:
                    accumulate(MOD_START[3] + 3)
                else:
                    lo(F + 5, JF - 2)
                product(JF - 1, (JF - 2) * RING + (F + 4))
                hid_low(JF - 1, *last_hid)
                if not f:
                    lo(F + 5, JF - 2)
                    modulation(3)
                    dve.wait_ge(s.mod_ready, 4)
                if f < 2:
                    lo(F + 6, JF - 2)
                residual(2 * f + 1, F + 32)

            ffn(0)
            dve.wait_ge(s.pool_zeroed, 3)
            for i in range(4):
                w = CONV_BASE + 3 * i
                lo(w + 2)
                if i == 0:
                    inverse_mean(2)
                    wait_row(2)
                    link(dve.tensor_tensor(rrow2[:, :], rrow[:, :], rrow[:, :], ALU.mult))
                lo(w + 3)
                dve.wait_ge(s.block_used, w + 2)
                link(dve.tensor_tensor(two(c_sb), two(conv_banks[i % 2][1]), both(rrow2[:, :]), ALU.mult))
                lo(w + 4)
                dve.wait_ge(s.block_used, w + 3)
                cu_in = cu[:, :, 2:T + 2]
                dve.tensor_tensor(cu_in, c_sb[:, :].rearrange("p (a b) -> p a b", a=2), two(conv_banks[i % 2][2]), ALU.mult).then_inc(s.cu_ready, 1)
                dve.wait_ge(s.cu_ready, i + 1)
                for tap in range(3):
                    for mt in range(2):
                        ck = V_AT["conv_k"][0] + 3 * (2 * i + mt) + tap
                        if tap == 0:
                            if i:
                                dve.wait_ge(s.by_hi, i)
                            link(dve.tensor_scalar(yb[:, mt, :], cu[:, mt, 0:T], vec[:, ck:ck + 1], None, ALU.mult))
                        else:
                            link(dve.scalar_tensor_tensor(out=yb[:, mt, :], in0=cu[:, mt, tap:tap + T], scalar=vec[:, ck:ck + 1],
                                                          in1=yb[:, mt, :], op0=ALU.mult, op1=ALU.add))
                link(dve.tensor_tensor(yb[:, :, :], yb[:, :, :], two(conv_banks[i % 2][0]), ALU.mult))
                dve.tensor_tensor(yb[:, :, :], yb[:, :, :], both(rrow[:, :]), ALU.mult).then_inc(s.by_ready, 1)
                dve.wait_ge(s.by_hi, i + 1)
                dve.tensor_tensor(o_lo[:, 2 * i:2 * i + 2, :], yb[:, :, :], o_hi[:, 2 * i:2 * i + 2, :], ALU.subtract).then_inc(s.by_lo, 1)
            for w in range(CONV_OUT + 2, CONV_OUT + 5):
                lo(w)
            residual(2, CONV_OUT + 3)
            ffn(1)
            dve.wait_ge(s.tables_loaded, 32)
            back = lambda ap, n: ap.rearrange("p (n c) -> p n c", n=n)[:, :, ::-1]
            for i in range(5):
                w, a = QKV_BASE + 3 * i, i + 1
                if i:
                    softmax_max(a, B, sc2)
                if i < 4:
                    lo(w + 2)
                    if i == 0:
                        inverse_mean(4)
                        wait_row(4)
                        link(dve.tensor_scalar(back(rrow2[:, :], TT), rrow[:, :].rearrange("p (n c) -> p n c", n=TT), HD ** -0.5, None, ALU.mult))
                    dve.wait_ge(s.block_used, w + 1)
                    for mt in range(2):
                        dve.tensor_tensor(q2[:, i % 2, mt, :].rearrange("p (n c) -> p n c", n=TT), back(A[0][:, T * mt:T * mt + T], TT),
                                          rrow2[:, :].rearrange("p (n c) -> p n c", n=TT), ALU.mult).then_inc(s.qk_scaled, 1)
                    lo(w + 3)
                if i:
                    softmax_div(a, sc2)
                if i < 4:
                    dve.wait_ge(s.block_used, w + 2)
                    dve.tensor_tensor(k2[:, i % 2, :, :], two(A[1]), both(rrow[:, :]), ALU.mult).then_inc(s.qk_scaled, 1)
                    lo(w + 4)
                else:
                    for v in range(ATT_OUT + 2, ATT_OUT + 4):
                        lo(v)
                if i:
                    pv_low(a, A[3] if i < 4 else B[0], o_lo[:, 2 * i - 2:2 * i, :], o_hi[:, 2 * i - 2:2 * i, :])
            lo(ATT_OUT + 4)
            residual(4, ATT_OUT + 3)
            ffn(2)
            inverse_mean(6)
            h_parts(6)

        @block.tensor
        def _(pe):
            def mm(o, l, r, start, stop):
                return pe.matmul(o, l, r, start=start, stop=stop, skip_group_check=True)

            def three(o, wh, wl, xh, xl, first, last):
                mm(o, wh, xh, first, False)
                mm(o, wh, xl, False, False)
                return mm(o, wl, xh, False, last)

            def column_block(w, bank, it=0, n=None, halfway=None):
                pe.wait_ge(s.lo_ready, it * RING + (w + 1))
                wh = w_hi[:, w % RING, :].rearrange("p (k c) -> p k c", k=KD)
                wl = w_lo[:, w % RING, :].rearrange("p (k c) -> p k c", k=KD)
                order = [(k, mt) for k in range(KD) for mt in range(2)] if n is not None else \
                    [(k, mt) for mt in range(2) for k in range(KD)]
                for k, mt in order:
                    if n is not None and mt == 0:
                        pe.wait_ge(s.h_lo_ready, 8 * n + k + 1)
                    if halfway is not None and mt == 1 and k == 0:
                        halfway()
                    c = slice(P * mt, P * mt + P)
                    ins = three(bank[:, 256 * mt:256 * mt + 256], wh[:, k, c], wl[:, k, c], h_hi[:, k, :], h_lo[:, k, :],
                                k == 0 and mt == 0, k == KD - 1)
                ins.then_inc(s.block_used, 1)

            def row_block(w, oh_, ol_, k0, it=0, first=False, n=None, before_last=None, tiles=range(KD)):
                pe.wait_ge(s.lo_ready, it * RING + (w + 1))
                wh = w_hi[:, w % RING, :].rearrange("p (k c) -> p k c", k=2)
                wl = w_lo[:, w % RING, :].rearrange("p (k c) -> p k c", k=2)
                for m in tiles:
                    if m == KD - 2 and before_last is not None:
                        before_last()
                    for k in range(2):
                        ins = three(acc[:, 256 * m:256 * m + 256], wh[:, k, P * m:P * m + P], wl[:, k, P * m:P * m + P],
                                    oh_[:, k0 + k, :], ol_[:, k0 + k, :], first and k == 0 and m % 2 == 0, False)
                    if n is not None and m % 2 and m < KD - 1:
                        ins.then_inc(s.acc_tile_done, 1)
                        if m >= 5 and n not in LATE:
                            square_sums(n, m - 5)
                            square_sums(n, m - 4)
                if tiles[-1] == KD - 1:
                    ins.then_inc(s.block_used, 1)

            def square_sums(n, m):
                pe.wait_ge(s.squared, 8 * n + m + 1)
                for t in range(TT):
                    ins = mm(B[3][:, t:t + 1], nt[:, m, P * t:P * t + P], ones, m == 0 and t == 0, m == KD - 1)
                return ins

            def norm(n):
                sums(n, 2 if n else 0)
                rstd(n)

            def sums(n, m0=0):
                if n in LATE:
                    pe.wait_ge(s.squares_added, 4 * (LATE.index(n) + 1))
                    for t in range(TT):
                        ins = mm(B[3][:, t:t + 1], nt[:, 0, P * t:P * t + P], ones, True, True)
                else:
                    for m in range(m0, KD):
                        ins = square_sums(n, m)
                ins.then_inc(s.sumsq_ready, 1)

            def rstd(n):
                pe.wait_ge(s.rms_ready, n + 1)
                for t in range(TT):
                    ins = mm(B[3][:, 256 + P * t:256 + P * t + P], rms[:, t:t + 1].broadcast_to([P, P]), ident, True, True)
                ins.then_inc(s.rstd_ready, 1)

            pe.wait_ge(s.consts_loaded, 16)
            norm(0)
            pe.wait_ge(s.mod_accumulated, 6)
            pe.wait_ge(s.pool_zeroed, 1)
            for _ in range(WARM_MOD):
                mm(B[0][:, :], zero_r[:, 0:P], zero_r[:, :], True, True)

            def modulation(part, columns=range(16)):
                pe.wait_ge(s.mod_accumulated, MOD_START[part + 1])
                for j in columns:
                    ins = mm(mod_bank[part][:, 480 + j:481 + j], mod_accs[part][:, P * j:P * j + P], ones, True, True)
                if columns[-1] == (15, 15, 7, 7)[part]:
                    ins.then_inc(s.mod_summed, 1)

            modulation(0)
            for _ in range(WARM_NORM0):
                mm(B[0][:, :], zero_r[:, 0:P], zero_r[:, :], True, True)

            def head_sums(src, tiles, col, width):
                for t in range(TT):
                    for i in range(tiles):
                        o = STAT[:, col + t * width + 2 * i:col + t * width + 2 * i + 2]
                        ins = mm(o, src(i, t), headsel, True, True)
                return ins

            def wait_bank(w):
                v = w - 4
                if 0 <= v < 6:
                    pe.wait_ge(s.pad_ready, v + 1)
                elif v >= 6:
                    pe.wait_ge(s.proj_evac, v - 5)

            def project(w, halfway=None):
                wait_bank(w)
                column_block(w, A[w % 4], n=0 if w == 0 else None, halfway=halfway)

            for w in range(6):
                project(w)
                if w == 0:
                    pe.wait_ge(s.gab_lo, 1)
                    for k in range(KD):
                        a, b = gab_wh[:, 16 * k:16 * k + 16], gab_wl[:, 16 * k:16 * k + 16]
                        ins = three(B[0][0:16, 0:T], a, b, h_hi[:, k, :], h_lo[:, k, :], k == 0, k == KD - 1)
                    ins.then_inc(s.gab_product, 1)
                    pe.wait_ge(s.t5_loaded, 48)
                    mm(B[1][0:16, 0:384], rb[:, :], oh, True, True).then_inc(s.t5_psum, 1)
                if w == 1:
                    pe.wait_ge(s.gab_copied, 1)
                    for t in range(TT):
                        ins = pe.transpose(STAT[:, 16 * t:16 * t + 16], gabT[:, P * t:P * t + P], ident[0:16, 0:16])
                    ins.then_inc(s.gab_ready, 1)
                if w == 4:
                    pe.wait_ge(s.masks_loaded, 16)
                    pe.wait_ge(s.gate_done, 1)
                    for t in range(TT):
                        mm(STAT[:, 32 + 8 * t:40 + 8 * t], tri, g[:, 8 * t:8 * t + 8], True, True)
                    mm(STAT[:, 48:56], ones.broadcast_to([P, P]), g[:, 0:8], True, True).then_inc(s.cum_ready, 1)

            def before(name):
                u = BIG_INDEX[name] - 3
                if u >= 0:
                    who = BIG_LIST[u][1]
                    pe.wait_ge(s.big_read_dve if who == "dve" else s.big_read_act, big_reads(u, who))

            def filled(name, ins):
                ins.then_inc(s.big_ready, 1)

            def rows(name, coef, tiles, rhs=ident, tts=range(TT), width=T):
                before(name)
                for i, tile in enumerate(tiles):
                    for par in range(2):
                        for n, t in enumerate(tts):
                            col = coef(2 * tile + par, t)
                            ins = mm(big(name)[64 * par:64 * par + 64, width * i + P * n:width * i + P * n + P],
                                     col.broadcast_to([P, HD]), rhs, True, True)
                filled(name, ins)

            def by_token(name, src, t):
                before(name)
                for i in range(4):
                    ins = pe.transpose(big(name)[:, P * i:P * i + P], src[:, i, P * t:P * t + P], ident)
                filled(name, ins)

            def decay(gi):
                before(f"G{gi}")
                for i in range(4):
                    col = 8 * (gi // 2) + 2 * i + gi % 2
                    ins = mm(big(f"G{gi}")[:, P * i:P * i + P], g[:, col:col + 1].broadcast_to([P, P]), tri, True, True)
                filled(f"G{gi}", ins)

            def products(kind, m, gi):
                t, r = gi // 2, slice(64 * (gi % 2), 64 * (gi % 2) + 64)
                before(f"{kind}{gi}")
                for i in range(4):
                    ins = mm(big(f"{kind}{gi}")[:, P * i:P * i + P], kT[r, i, P * t:P * t + P], m[r, i, P * t:P * t + P], True, True)
                filled(f"{kind}{gi}", ins)

            at = lambda c: (lambda h, t: c[:, 8 * t + h:8 * t + h + 1])
            def kq_sums(w):
                pe.wait_ge(s.head_squared, w + 1)
                return head_sums(lambda i, t: head_sq[w][:, 256 * i + P * t:256 * i + P * t + P], 2, 64 + 4 * w, 16)

            def window_sums(w):
                pe.wait_ge(s.head_squared, w + 1)
                return head_sums(lambda i, t: head_sq[w][:, 256 * i + P * t:256 * i + P * t + P],
                                 2 if w < 6 else 1, 96 + 4 * (w - 4), 10)

            def first_sums():
                pe.wait_ge(s.decay_dve, 1)
                kq_sums(0)
                kq_sums(1)

            def first_window_sums():
                pe.wait_ge(s.head_inv, 1)
                window_sums(4)
                window_sums(5)

            project(6, first_sums)
            kq_sums(2)
            kq_sums(3).then_inc(s.head_sums, 1)
            project(7)
            pe.wait_ge(s.coef_ready, 2)
            pe.wait_ge(s.t5_row, 1)
            rows("kb01", at(coefk), (0, 1))
            rows("kb23", at(coefk), (2, 3))
            rows("q01", at(coefq), (0, 1))
            project(8)
            rows("q23", at(coefq), (2, 3))
            rows("eg", at(g), range(4), rhs=tri, tts=(1,), width=P)
            pe.wait_ge(s.feature_ready, 6)
            by_token("v0", vT, 0)
            project(9)
            by_token("v1", vT, 1)
            by_token("kt", kT, 0)
            for gi in range(3):
                decay(gi)
            project(10, first_window_sums)
            decay(3)
            for gi in range(4):
                products("kk", kbT, gi)
            window_sums(6).then_inc(s.head_sums, 1)
            for gi in range(4):
                products("qk", qT, gi)
            pe.wait_ge(s.proj_evac, 6)
            for t in range(TT):
                ins = pe.transpose(A[3][:, P * t:P * t + P], swa_vT[:, P * t:P * t + P], ident)
            ins.then_inc(s.v_transposed, 1)
            pe.wait_ge(s.head_rms, 2)
            sat = lambda h, t: ss[:, 2, 10 * t + h:10 * t + h + 1]
            rows("sk", sat, (4,))
            rows("sq01", sat, (0, 1))
            rows("sq23", sat, (2, 3))
            for gi in range(4):
                if gi < 3:
                    before(f"tr{gi}")
                else:
                    pe.wait_ge(s.x_copied, 1)
                pe.wait_ge(s.xt_ready, gi + 1)
                for i in range(4):
                    ins = pe.transpose(big(f"tr{gi}")[:, P * i:P * i + P], XT[:, gi, P * i:P * i + P], ident)
                ins.then_inc(s.xtr_ready, 1)

            def scores(a, bank, q, k):
                for hh in range(4):
                    r = slice(64 * (hh % 2), 64 * (hh % 2) + 64)
                    if a > 0:
                        pe.wait_ge(s.ptrans_copied, 4 * a - 4 + hh + 1)
                        if a == 1 and hh == 0:
                            pe.wait_ge(s.pv_lo, a)
                    mm(bank[hh][:, 0:256], q(hh // 2)[r, P:T], k(hh // 2)[r, 0:T], True, True)
                    mm(bank[hh][:, 256:384], q(hh // 2)[r, 0:P], k(hh // 2)[r, 0:P], True, True).then_inc(s.scores_ready, 1)

            def transposes(a, bank, sc, perm):
                for hh in range(4):
                    pe.wait_ge(s.probs_ready, 8 * a + 2 * hh + 2)
                    for i in range(3):
                        ins = pe.transpose(bank[hh][:, P * i:P * i + P], sc[:, hh, P * i:P * i + P], perm)
                    ins.then_inc(s.ptrans_ready, 1)

            def values(a, bank, pT, v, out=None):
                out = bank[0] if out is None else out
                if a > 2:
                    pe.wait_ge(s.pv_lo, a)
                elif a == 2:
                    pe.wait_ge(s.v_scaled, TT)
                for hh in range(4):
                    pe.wait_ge(s.ptrans_copied, 4 * a + hh + 1)
                    o = out[64 * (hh % 2):64 * (hh % 2) + 64, 256 * (hh // 2):256 * (hh // 2) + 256]
                    mm(o[:, 0:P], v(0, hh), pT[:, hh, 256:384], True, True)
                    mm(o[:, P:T], v(0, hh), pT[:, hh, 0:P], True, False)
                    ins = mm(o[:, P:T], v(1, hh), pT[:, hh, P:2 * P], False, True)
                ins.then_inc(s.pv_ready, 1)

            swa_q = lambda a: (lambda i: qs[:, 2 * a + i, :])
            swa_k = lambda i: ks[:, :]
            swa_v = lambda t, hh: vs[:, t, 64 * (hh % 2):64 * (hh % 2) + 64]
            pe.wait_ge(s.big_read_dve, big_reads(BIG_INDEX["sq23"], "dve"))
            pe.wait_ge(s.v_ready, 1)
            scores(0, A, swa_q(0), swa_k)

            for l in range(1, NEXP + 1):
                for gi in range(4):
                    pe.wait_ge(s.b_ready, 4 * (l - 1) + gi + 1)
                    pe.wait_ge(s.x_copied, 4 if l == 1 else 4 * (l - 1) + gi + 1)
                    for i in range(4):
                        c, o = slice(P * i, P * i + P), B[gi][:, HALF * i:HALF * i + HALF]
                        ins = mm(o.rearrange("p (n c) -> p n c", c=1 << l), Bm[:, gi, c], first_halves(X[:, gi, c], l), True, True)
                    ins.then_inc(s.p_ready, 1)
                if l == 3:
                    values(0, A, pT1, swa_v)
                if l == NEXP:
                    values(1, A, pT1, swa_v)
                for gi in range(4):
                    pe.wait_ge(s.p_copied, 4 * (l - 1) + gi + 1)
                    for i in range(4):
                        c = slice(P * i, P * i + P)
                        half = slice(HALF * i, HALF * i + HALF)
                        if l < NEXP:
                            ins = mm(B[gi][:, half], XT[:, gi, c], Pm[:, gi, half], True, True)
                        else:
                            ins = mm(B[gi][0:HALF, half], Pm[:, gi, half], XT[:, gi, P * i + HALF:P * i + P], True, True)
                    ins.then_inc(s.qt_ready, 1)
                if l < NEXP:
                    for gi in range(4):
                        pe.wait_ge(s.x_updated, 4 * (l - 1) + gi + 1)
                        for i in range(4):
                            c = slice(P * i, P * i + P)
                            ins = pe.transpose(B[gi][:, c], X[:, gi, c], ident)
                        ins.then_inc(s.xtr_ready, 1)
                if l == 2:
                    transposes(0, A, sc1, ident)
                if l == 3:
                    scores(1, A, swa_q(1), swa_k)
                if l == 5:
                    transposes(1, A, sc1, ident)
            pe.wait_ge(s.xt_ready, 4 + 2)
            inv_of = lambda h, t: XT[:, 2 * t + h % 2, P * (h // 2):P * (h // 2) + P]
            qk_of = lambda h, t: qkT[:, 2 * t + h % 2, P * (h // 2):P * (h // 2) + P]
            for h in range(8):
                e = slice(HD * h, HD * h + HD)
                ins = mm(B[0][:, e], inv_of(h, 0), vb[:, 0, e], True, True)
            ins.then_inc(s.u_ready, 1)
            pe.wait_ge(s.pv_lo, 2)
            row_block(W_OUT, h_hi, h_lo, 4, first=True, tiles=range(0, 3))
            pe.wait_ge(s.u_copied, 1)
            for h in range(8):
                r = slice(64 * (h % 2), 64 * (h % 2) + 64)
                e = slice(HD * h, HD * h + HD)
                ins = mm(B[1][r, HD * (h // 2):HD * (h // 2) + HD], kd[:, e], u0[:, e], True, True)
            ins.then_inc(s.s_ready, 1)
            pe.wait_ge(s.xt_ready, 4 + 4)
            for h in range(8):
                r = slice(64 * (h % 2), 64 * (h % 2) + 64)
                ins = mm(B[2 + h % 2][r, P * (h // 2):P * (h // 2) + P], u0[:, HD * h:HD * h + HD], qk_of(h, 0), True, True)
            ins.then_inc(s.o0_ready, 1)
            pe.wait_ge(s.s_copied, 1)
            for par in range(2):
                r = slice(64 * par, 64 * par + 64)
                for i in range(4):
                    ins = mm(B[par][:, HD * i:HD * i + HD], kbgT[r, i, :], S1[r, HD * i:HD * i + HD], True, True)
            ins.then_inc(s.r_ready, 1)
            row_block(W_OUT, h_hi, h_lo, 4, first=True, tiles=range(3, 6))
            pe.wait_ge(s.r_done, 2)
            for h in range(8):
                e = slice(HD * h, HD * h + HD)
                ins = mm(B[0][:, e], inv_of(h, 1), r1[:, e], True, True)
            ins.then_inc(s.vn_ready, 1)
            row_block(W_OUT, h_hi, h_lo, 4, first=True, tiles=range(6, 8))
            pe.wait_ge(s.vn_copied, 1)
            for h in range(8):
                r = slice(64 * (h % 2), 64 * (h % 2) + 64)
                i = h // 2
                o = B[h % 2][r, P * i:P * i + P]
                mm(o, vn[:, HD * h:HD * h + HD], qk_of(h, 1), True, False)
                ins = mm(o, S1[r, HD * i:HD * i + HD], qdT[r, i, :], False, True)
            ins.then_inc(s.o1_ready, 1)
            pe.wait_ge(s.o_copied, 2)
            modulation(1, range(0, 8))
            row_block(W_OUT + 1, h_hi, h_lo, 6, tiles=range(0, 4))
            pe.wait_ge(s.o_squared, 1)
            for t in range(TT):
                for i in range(4):
                    ins = mm(B[2][:, 8 * t + 2 * i:8 * t + 2 * i + 2], osq[:, i, P * t:P * t + P], headsel, True, True)
            ins.then_inc(s.o_sums, 1)
            row_block(W_OUT + 1, h_hi, h_lo, 6, tiles=range(4, 6))
            pe.wait_ge(s.o_rms, 1)
            for j in range(2):
                for i in range(2):
                    for par in range(2):
                        for t in range(TT):
                            h = 2 * (2 * j + i) + par
                            ins = mm(B[j][64 * par:64 * par + 64, T * i + P * t:T * i + P * t + P],
                                     os_[:, 2, 8 * t + h:8 * t + h + 1].broadcast_to([P, HD]), ident, True, True)
                ins.then_inc(s.o_rows, 1)
            modulation(1, range(8, 16))
            row_block(W_OUT + 1, h_hi, h_lo, 6, tiles=range(6, 8))
            pe.wait_ge(s.o_lo_done, 1)
            row_block(W_OUT + 2, h_hi, h_lo, 0)
            pe.wait_ge(s.o_lo_done, 2)
            modulation(2, range(8))
            row_block(W_OUT + 3, h_hi, h_lo, 2, n=1)

            def ffn(f):
                F, n = FFN_BASE[f], 2 * f + 1
                if f:
                    column_block(F, B[0], n=n)
                    sums(n)
                else:
                    sums(n, 2)
                    rstd(n)
                    for _ in range(WARM_NORM1):
                        mm(B[0][:, :], zero_r[:, 0:P], zero_r[:, :], True, True)
                    column_block(F, B[0], n=n)
                column_block(F + 1, B[1], halfway=(lambda: rstd(n)) if f else None)

                def body(j, it, first=False):
                    if f:
                        pe.wait_ge(s.gate_scaled, j + JF * (f - 1))
                    else:
                        pe.wait_ge(s.silu_ready, j)
                    column_block(F + 2, B[0], it)
                    pe.wait_ge(s.hid_ready, j + JF * f)
                    column_block(F + 3, B[1], it)
                    pe.wait_ge(s.hid_lo_ready, j + JF * f)
                    row_block(F + 4, hid_hi, hid_lo, 0, it, first=first)

                body(1, 0, first=True)
                with pe.Fori(2, JF - 1) as j:
                    body(j, j - 1)
                body(JF - 1, JF - 2)
                if not f:
                    modulation(3, range(8))
                pe.wait_ge(s.hid_lo_ready, JF * f + JF)
                row_block(F + 32, *last_hid, 0, n=2 * f + 2)

            ffn(0)
            for i in range(4):
                w = CONV_BASE + 3 * i
                if i >= 2:
                    pe.wait_ge(s.by_ready, i - 1)
                column_block(w, conv_banks[i % 2][0], n=2 if i == 0 else None)
                if i == 0:
                    sums(2)
                column_block(w + 1, conv_banks[i % 2][1], halfway=(lambda: rstd(2)) if i == 0 else None)
                column_block(w + 2, conv_banks[i % 2][2])
            for i in range(4):
                if i == 0:
                    pe.wait_ge(s.by_ready, 3)
                pe.wait_ge(s.by_lo, i + 1)
                row_block(CONV_OUT + i, o_hi, o_lo, 2 * i, first=i == 0, n=3 if i == 3 else None)
            ffn(1)
            dil_q = lambda b: (lambda t: q2[:, b, t, :])
            dil_k = lambda b: (lambda t: k2[:, b, t, :])
            dil_v = lambda b: (lambda t, hh: v2[:, b, t, HD * hh:HD * hh + HD])
            for i in range(5):
                w, a, b = QKV_BASE + 3 * i, i + 1, (i - 1) % 2
                if i:
                    pe.wait_ge(s.qk_scaled, 3 * i)
                    scores(a, B, dil_q(b), dil_k(b))
                if i < 4:
                    column_block(w, A[0], n=4 if i == 0 else None)
                    if i == 0:
                        sums(4)
                    column_block(w + 1, A[1], halfway=(lambda: rstd(4)) if i == 0 else None)
                    pe.wait_ge(s.lo_ready, w + 3)
                    if i:
                        pe.wait_ge(s.v_scaled, TT * i)
                    wh = w_hi[:, (w + 2) % RING, :].rearrange("p (k c) -> p k c", k=KD)
                    wl = w_lo[:, (w + 2) % RING, :].rearrange("p (k c) -> p k c", k=KD)
                    for t in range(TT):
                        tok = slice(P * t, P * t + P)
                        for k in range(KD):
                            ins = three(A[2][:, 256 * t:256 * t + 256], h_hi[:, k, tok], h_lo[:, k, tok], wh[:, k, :], wl[:, k, :],
                                        k == 0 and t == 0, k == KD - 1)
                    ins.then_inc(s.block_used, 1)
                else:
                    pe.wait_ge(s.v_scaled, TT * i)
                    row_block(ATT_OUT, o_hi, o_lo, 0, first=True,
                              before_last=lambda: pe.wait_ge(s.pv_lo, 5))
                    row_block(ATT_OUT + 1, o_hi, o_lo, 2)
                if i:
                    transposes(a, B, sc2, const("flip"))
                    values(a, B, pT2, dil_v(b), out=A[3] if i < 4 else B[0])
            row_block(ATT_OUT + 2, o_hi, o_lo, 4)
            pe.wait_ge(s.pv_lo, 6)
            row_block(ATT_OUT + 3, o_hi, o_lo, 6, n=5)
            ffn(2)
            norm(6)


def shape_constants():
    c = np.zeros((P, N_CONST), np.float32)
    i, j = np.arange(P)[:, None], np.arange(P)[None, :]
    c[:, slice(*C_AT["ident"])] = i == j
    c[:, slice(*C_AT["flip"])] = i + j == P - 1
    c[:, slice(*C_AT["tri"])] = i <= j
    c[:, slice(*C_AT["future"])] = np.where(j >= i, 0.0, -BIG)
    for l in range(NEXP + 1):
        b = 1 << l
        m = (i // (2 * b) == j // (2 * b)) & ((i // b) % 2 == 0) & ((j // b) % 2 == 1)
        c[:, C_AT["levels"][0] + P * l:C_AT["levels"][0] + P * (l + 1)] = m
    c[:, C_AT["headsel"][0]] = np.arange(P) < 64
    c[:, C_AT["headsel"][0] + 1] = np.arange(P) >= 64
    c[:, C_AT["ones"][0]] = 1.0
    k = np.arange(256)[None, :]
    dist = i + 128 - k
    table = np.where((dist >= 0) & (dist < 128), -dist, -BIG)
    c[:, C_AT["alibi"][0]:C_AT["alibi"][1]] = np.concatenate([table, table[:, 128:]], 1)
    return c


def t5_constants():
    d = 255 - np.arange(384)
    exact = 16
    df = np.maximum(d, 1).astype(np.float32)
    large = exact + (np.log(df / np.float32(exact)) / np.float32(np.log(2048 / exact)) * np.float32(32 - exact)).astype(np.int32)
    bucket = np.where(d < exact, np.maximum(d, 0), np.minimum(large, 31))
    onehot = (np.arange(32)[:, None] == bucket[None, :]).astype(np.float32)
    n = ((d >= 0) & (d <= 128)).astype(int) + ((d >= 0) & (d % 4 == 0)) + ((d >= 0) & (d % 16 == 0))
    log = np.where(n > 0, np.log(np.maximum(n, 1)), -BIG).astype(np.float32)
    return onehot, np.ascontiguousarray(np.broadcast_to(log, (16, 384)))


def lay_out(v):
    def cols(w, at):
        return w[:, at].reshape(KD, P, 256).transpose(1, 0, 2).reshape(P, BLOCK)

    def rows(w, at):
        return w[at].reshape(2, P, D).transpose(1, 0, 2).reshape(P, BLOCK)

    def chunk(a):
        return a.reshape(-1, P).T

    r = np.arange
    w_in, w_out, ada = v["w_in"][0], v["w_out"][0], v["w_ada"][0]
    pair = np.concatenate([np.concatenate([r(64) + 64 * j, r(64) + 64 * (4 + j)]) for j in range(4)])
    starts = [512, 768, 0, 256, 1024, 1280, 1536, 1792]
    w = [cols(w_in, r(a, a + 256)) for a in starts]
    w += [cols(w_in, 2064 + pair[0:256]), cols(w_in, 2064 + pair[256:512]), cols(w_in, r(2576, 2832))]
    w += [rows(w_out, 512 + pair[0:256]), rows(w_out, 512 + pair[256:512]), rows(w_out, r(256)), rows(w_out, r(256, 512))]

    def swiglu(wg, wu, wd):
        out = []
        for j in range(JF + 1):
            if j < JF:
                out += [cols(wg, r(256 * j, 256 * j + 256)), cols(wu, r(256 * j, 256 * j + 256))]
            if j:
                out.append(rows(wd, r(256 * j - 256, 256 * j)))
        return out

    def mixer(w1, w2):
        out = [cols(w1, r(D * j + 256 * i, D * j + 256 * i + 256)) for i in range(4) for j in range(3)]
        return out + [rows(w2, r(256 * i, 256 * i + 256)) for i in range(4)]

    w += swiglu(v["w_gate"][0], v["w_up"][0], v["w_down"][0])
    w += mixer(v["conv_w_in_2"][0], v["conv_w_out_2"][0])
    w += swiglu(v["ffn_w_gate_2"][0], v["ffn_w_up_2"][0], v["ffn_w_down_2"][0])
    w += mixer(v["attn_w_qkv_2"][0], v["attn_w_out_2"][0])
    w += swiglu(v["ffn_w_gate_2"][1], v["ffn_w_up_2"][1], v["ffn_w_down_2"][1])
    assert len(w) == N_WEIGHTS
    stream = []
    for _, kind, n in STREAM_ORDER:
        if kind == "w":
            stream.append(w[n])
            continue
        part = max(i for i in range(4) if MOD_START[i] <= n)
        k, at = n - MOD_START[part], MOD_COLS[part]
        if part < 2:
            stream.append(ada[P * k:P * k + P, at:at + BLOCK])
        else:
            stream.append(np.concatenate([ada[P * q:P * q + P, at:at + BLOCK // 2] for q in (2 * k, 2 * k + 1)], 1))

    vec = np.zeros((P, N_VEC), np.float32)

    def put(name, a):
        vec[:, slice(*V_AT[name])] = a

    put("c", chunk(v["c"][0]))
    for name, a in (("norm1", v["norm1_w"][0]), ("norm2", v["norm2_w"][0]), ("mix0", v["mix_norm_2"][0]),
                    ("mix1", v["mix_norm_2"][1]), ("ffn0", v["ffn_norm_2"][0]), ("ffn1", v["ffn_norm_2"][1]),
                    ("final", v["final_norm_2"]), ("b_ada", v["b_ada"][0])):
        put(name, chunk(a))
    put("conv_w", v["conv_w"][0, :, 0, :].reshape(4, 12, P).transpose(2, 1, 0).reshape(P, 48))
    put("conv_k", v["conv_kernel_2"][0].reshape(3, KD, P).transpose(2, 1, 0).reshape(P, 24))
    for name, a in (("gdn_w", v["gdn_norm_w"][0]), ("qn_w", v["q_norm_w"][0]), ("kn_w", v["k_norm_w"][0])):
        put(name, np.tile(a, 2)[:, None])
    put("dt_bias", v["dt_bias"][0][None, :])
    put("a_log", v["a_log"][0][None, :])
    put("sinks", v["sinks"][0][[2 * a + hh // 2 + 4 * (hh % 2) for a in range(2) for hh in range(4)]][None, :])
    onehot, log = t5_constants()
    return {
        "stream": np.stack(stream),
        "x_in": v["x"][0].T.reshape(KD, P, T).transpose(1, 0, 2),
        "consts_in": shape_constants(),
        "vectors_in": vec,
        "gab_in": w_in[:, 2048:2064].reshape(KD, P, 16).transpose(1, 0, 2).reshape(P, KD * 16),
        "t5_onehot": onehot,
        "t5_log": log,
        "rel_bias": v["rel_bias_2"],
    }


def kernel(**inputs):
    import concourse.bacc as bacc
    from concourse.bass_utils import run_bass_kernel_spmd

    nc = bacc.Bacc("TRN2", target_bir_lowering=False, num_devices=1)
    arrays = {k: np.ascontiguousarray(a) for k, a in lay_out({k: np.asarray(a) for k, a in inputs.items()}).items()}
    args = {k: nc.dram_tensor(k, a.shape, mybir.dt.from_np(a.dtype), kind="ExternalInput").ap() for k, a in arrays.items()}
    out = nc.dram_tensor("out", (P, KD, T), F32, kind="ExternalOutput").ap()
    build(nc, out=out, **args)
    r = run_bass_kernel_spmd(nc, [arrays], core_ids=[0])
    y = r.results[0]["out"]
    return np.ascontiguousarray(y.transpose(1, 0, 2).reshape(D, T).T)[None]
```
